# Optimizing a Trainium2 kernel written in Bass

```python
import math
import jax, jax.numpy as jnp
from jax import lax
import numpy as np

D_MODEL = 1024
BATCH = 1
SEQ = 256
DEPTH = 2

D_FF = 2816
N_NORMS = 6
EPS = 1e-6
HEAD_DIM = 64
CONV_CH = 512
CONV_K = 31
SWA_HQ = 8
SWA_HKV = 2
SWA_G = SWA_HQ // SWA_HKV
WINDOW = 128
BLK = 128
FOX_H = 16
AB_IN = 2 * CONV_CH + SWA_HQ * HEAD_DIM + 2 * SWA_HKV * HEAD_DIM
AB_OUT = CONV_CH + SWA_HQ * HEAD_DIM
FOX_IN = 3 * FOX_H * HEAD_DIM + FOX_H
FOX_OUT = FOX_H * HEAD_DIM
NEG = -1e30


def _rmsnorm(x, g):
    xf = x.astype(jnp.float32)
    y = xf * lax.rsqrt(jnp.mean(xf * xf, axis=-1, keepdims=True) + EPS)
    return (y * g.astype(jnp.float32)).astype(x.dtype)

def _swiglu(x, wg, wu, wd):
    return (jax.nn.silu(x @ wg) * (x @ wu)) @ wd

def _alibi_slopes(n):
    return jnp.asarray([2.0 ** (-8.0 * (i + 1) / n) for i in range(n)], dtype=jnp.float32)

def _conv_module(u, gate, w, b, ln_g, ln_b):
    a = u * jax.nn.sigmoid(gate)
    y = lax.conv_general_dilated(
        a, w.reshape(CONV_K, 1, CONV_CH).astype(a.dtype),
        window_strides=(1,), padding=[(CONV_K - 1, 0)],
        dimension_numbers=("NWC", "WIO", "NWC"),
        feature_group_count=CONV_CH) + b
    yf = y.astype(jnp.float32)
    mu = jnp.mean(yf, axis=-1, keepdims=True)
    var = jnp.mean(jnp.square(yf - mu), axis=-1, keepdims=True)
    yf = (yf - mu) * lax.rsqrt(var + EPS) * ln_g.astype(jnp.float32) + ln_b.astype(jnp.float32)
    return jax.nn.silu(yf).astype(u.dtype)

def _swa_sinks(q, k, v, sinks):
    b, s, _, dh = q.shape
    nb = s // BLK
    qb = q.reshape(b, nb, BLK, SWA_HKV, SWA_G, dh)
    kb = k.reshape(b, nb, BLK, SWA_HKV, dh)
    vb = v.reshape(b, nb, BLK, SWA_HKV, dh)
    pad = ((0, 0), (1, 0), (0, 0), (0, 0), (0, 0))
    kk = jnp.concatenate([jnp.pad(kb, pad)[:, :-1], kb], axis=2)
    vv = jnp.concatenate([jnp.pad(vb, pad)[:, :-1], vb], axis=2)
    sc = jnp.einsum("bnqhgd,bnkhd->bnhgqk", qb, kk).astype(jnp.float32) / math.sqrt(dh)
    t_loc = jnp.arange(BLK)[:, None]
    s_loc = jnp.arange(2 * BLK)[None, :]
    dist = t_loc + BLK - s_loc
    valid = (dist >= 0) & (dist < WINDOW)
    mask = valid[None] & ((jnp.arange(nb)[:, None, None] > 0) | (s_loc >= BLK)[None])
    slopes = _alibi_slopes(SWA_HQ).reshape(SWA_HKV, SWA_G)
    sc = sc - slopes[:, :, None, None] * dist.astype(jnp.float32)
    sc = jnp.where(mask[None, :, None, None], sc, NEG)
    sink = jnp.broadcast_to(sinks.astype(jnp.float32).reshape(SWA_HKV, SWA_G)[None, None, :, :, None, None],
                            sc.shape[:-1] + (1,))
    p = jax.nn.softmax(jnp.concatenate([sc, sink], axis=-1), axis=-1)[..., :-1]
    o = jnp.einsum("bnhgqk,bnkhd->bnqhgd", p.astype(v.dtype), vv)
    return o.reshape(b, s, SWA_HQ * dh)

def _fox_attention(q, k, v, zf, b_f):
    b, s, h, dh = q.shape
    nb = s // BLK
    qh = q.transpose(0, 2, 1, 3)
    kh = k.transpose(0, 2, 1, 3)
    vh = v.transpose(0, 2, 1, 3)
    logf = jax.nn.log_sigmoid(zf.astype(jnp.float32) + b_f.astype(jnp.float32))
    c = jnp.cumsum(logf.transpose(0, 2, 1), axis=-1)
    key_pos = jnp.arange(s)

    def one_block(i):
        start = i * BLK
        qs = lax.dynamic_slice_in_dim(qh, start, BLK, axis=2)
        cs = lax.dynamic_slice_in_dim(c, start, BLK, axis=2)
        sc = jnp.einsum("bhqd,bhkd->bhqk", qs, kh).astype(jnp.float32) / math.sqrt(dh)
        sc = sc + cs[..., :, None] - c[..., None, :]
        tpos = start + jnp.arange(BLK)
        sc = jnp.where(tpos[:, None] >= key_pos[None, :], sc, NEG)
        p = jax.nn.softmax(sc, axis=-1)
        return jnp.einsum("bhqk,bhkd->bhqd", p.astype(vh.dtype), vh)

    o = lax.map(one_block, jnp.arange(nb))
    return o.transpose(1, 0, 3, 2, 4).reshape(b, s, h * dh)

def _mixer_even(h, w_in, conv_w, conv_b, ln_g, ln_b, sinks, w_out):
    b, s, _ = h.shape
    z = h @ w_in
    o0 = CONV_CH
    o1 = o0 + CONV_CH
    o2 = o1 + SWA_HQ * HEAD_DIM
    o3 = o2 + SWA_HKV * HEAD_DIM
    u, gate = z[..., :o0], z[..., o0:o1]
    q = z[..., o1:o2].reshape(b, s, SWA_HQ, HEAD_DIM)
    k = z[..., o2:o3].reshape(b, s, SWA_HKV, HEAD_DIM)
    v = z[..., o3:].reshape(b, s, SWA_HKV, HEAD_DIM)
    a_out = _conv_module(u, gate, conv_w, conv_b, ln_g, ln_b)
    b_out = _swa_sinks(q, k, v, sinks)
    return jnp.concatenate([a_out, b_out], axis=-1) @ w_out

def _mixer_odd(h, w_in, b_f, w_out):
    b, s, _ = h.shape
    z = h @ w_in
    hd = FOX_H * HEAD_DIM
    q = z[..., :hd].reshape(b, s, FOX_H, HEAD_DIM)
    k = z[..., hd:2 * hd].reshape(b, s, FOX_H, HEAD_DIM)
    v = z[..., 2 * hd:3 * hd].reshape(b, s, FOX_H, HEAD_DIM)
    zf = z[..., 3 * hd:]
    return _fox_attention(q, k, v, zf, b_f) @ w_out

def first_inputs(seed: int = 0) -> dict:
    key = jax.random.key(seed)
    ks = jax.random.split(key, 16)
    n_even = (DEPTH + 1) // 2
    n_odd = DEPTH // 2
    f32 = jnp.float32
    nrm = lambda k, shp, fan: jax.random.normal(k, shp, f32) * fan ** -0.5
    return {
        "x": jax.random.normal(ks[0], (BATCH, SEQ, D_MODEL), f32),
        "norm_g": 1.0 + 0.05 * jax.random.normal(ks[1], (DEPTH, N_NORMS, D_MODEL), f32),
        "ffn_w_gate": nrm(ks[2], (DEPTH, 2, D_MODEL, D_FF), D_MODEL),
        "ffn_w_up": nrm(ks[3], (DEPTH, 2, D_MODEL, D_FF), D_MODEL),
        "ffn_w_down": nrm(ks[4], (DEPTH, 2, D_FF, D_MODEL), D_FF),
        "ab_w_in": nrm(ks[5], (n_even, D_MODEL, AB_IN), D_MODEL),
        "conv_w": nrm(ks[6], (n_even, CONV_K, CONV_CH), CONV_K),
        "conv_b": 0.02 * jax.random.normal(ks[7], (n_even, CONV_CH), f32),
        "conv_ln_g": 1.0 + 0.05 * jax.random.normal(ks[8], (n_even, CONV_CH), f32),
        "conv_ln_b": 0.02 * jax.random.normal(ks[9], (n_even, CONV_CH), f32),
        "swa_sinks": 0.5 * jax.random.normal(ks[10], (n_even, SWA_HQ), f32),
        "ab_w_out": nrm(ks[11], (n_even, AB_OUT, D_MODEL), AB_OUT),
        "fox_w_in": nrm(ks[12], (n_odd, D_MODEL, FOX_IN), D_MODEL),
        "fox_b_f": jax.random.uniform(ks[13], (n_odd, FOX_H), f32, 1.0, 6.0),
        "fox_w_out": nrm(ks[14], (n_odd, FOX_OUT, D_MODEL), FOX_OUT),
    }

def first_block(x, norm_g, ffn_w_gate, ffn_w_up, ffn_w_down, ab_w_in, conv_w, conv_b,
              conv_ln_g, conv_ln_b, swa_sinks, ab_w_out, fox_w_in, fox_b_f, fox_w_out):
    for l in range(DEPTH):
        g = norm_g[l]
        h = _swiglu(_rmsnorm(x, g[0]), ffn_w_gate[l, 0], ffn_w_up[l, 0], ffn_w_down[l, 0])
        x = x + 0.5 * _rmsnorm(h, g[1])
        h = _rmsnorm(x, g[2])
        if l % 2 == 0:
            i = l // 2
            h = _mixer_even(h, ab_w_in[i], conv_w[i], conv_b[i], conv_ln_g[i], conv_ln_b[i],
                            swa_sinks[i], ab_w_out[i])
        else:
            i = l // 2
            h = _mixer_odd(h, fox_w_in[i], fox_b_f[i], fox_w_out[i])
        x = x + _rmsnorm(h, g[3])
        h = _swiglu(_rmsnorm(x, g[4]), ffn_w_gate[l, 1], ffn_w_up[l, 1], ffn_w_down[l, 1])
        x = x + 0.5 * _rmsnorm(h, g[5])
    return x


CHUNK = 64
N_A_LAYERS = DEPTH // 2
N_B_LAYERS = DEPTH - N_A_LAYERS
A_HEADS = 8
A_DQK = D_MODEL // 16
A_DV = D_MODEL // 8
A_QK = A_HEADS * A_DQK
A_V = A_HEADS * A_DV
A_IN = 2 * A_QK + 2 * A_V + 2 * A_HEADS
B_HEADS = 16
B_DH = D_MODEL // B_HEADS
B_DIM = B_HEADS * B_DH
LEFT_CHUNKS = 8
BAND = (LEFT_CHUNKS + 1) * CHUNK
MAX_REL = 256
N_REL = 2 * MAX_REL + 1
D_FF_2 = -(-8 * D_MODEL // (3 * 256)) * 256
NEG_INIT = -1e30


def rmsnorm(x, g):
    x32 = x.astype(jnp.float32)
    y = x32 * lax.rsqrt(jnp.mean(x32 * x32, axis=-1, keepdims=True) + EPS) * g.astype(jnp.float32)
    return y.astype(x.dtype)

def swiglu(h, w_gate, w_up, w_down):
    return (jax.nn.silu(h @ w_gate) * (h @ w_up)) @ w_down

def mlstm_mixer(h, w_in, b_gate, g_head, w_out):
    B, S, _ = h.shape
    nc = S // CHUNK
    proj = h @ w_in
    q = proj[..., :A_QK].astype(jnp.float32).reshape(B, S, A_HEADS, A_DQK)
    k = proj[..., A_QK:2 * A_QK].astype(jnp.float32).reshape(B, S, A_HEADS, A_DQK) * (A_DQK ** -0.5)
    v = proj[..., 2 * A_QK:2 * A_QK + A_V].astype(jnp.float32).reshape(B, S, A_HEADS, A_DV)
    o_pre = proj[..., 2 * A_QK + A_V:2 * A_QK + 2 * A_V]
    gates = proj[..., 2 * A_QK + 2 * A_V:].astype(jnp.float32) + b_gate.astype(jnp.float32)
    i_log = gates[..., :A_HEADS]
    f_log = jax.nn.log_sigmoid(gates[..., A_HEADS:])

    def to_chunks(t):
        return t.reshape(B, nc, CHUNK, A_HEADS, -1).transpose(1, 0, 3, 2, 4)

    def gate_chunks(t):
        return t.reshape(B, nc, CHUNK, A_HEADS).transpose(1, 0, 3, 2)

    tri = jnp.tril(jnp.ones((CHUNK, CHUNK), dtype=bool))

    def step(carry, xs):
        C, n, m = carry
        qc, kc, vc, ic, fc = xs
        b = jnp.cumsum(fc, axis=-1)
        logD = b[..., :, None] - b[..., None, :] + ic[..., None, :]
        logD = jnp.where(tri, logD, -jnp.inf)
        inter = b + m[..., None]
        m_j = jnp.maximum(inter, jnp.max(logD, axis=-1))
        D = jnp.exp(logD - m_j[..., None])
        w_inter = jnp.exp(inter - m_j)
        s = jnp.einsum('bhld,bhsd->bhls', qc, kc) * D
        num = jnp.einsum('bhls,bhsv->bhlv', s, vc) + w_inter[..., None] * jnp.einsum('bhvd,bhld->bhlv', C, qc)
        den = jnp.sum(s, axis=-1) + w_inter * jnp.einsum('bhd,bhld->bhl', n, qc)
        h_out = num / jnp.maximum(jnp.abs(den), jnp.exp(-m_j))[..., None]
        bL = b[..., -1]
        a = bL[..., None] - b + ic
        m_new = jnp.maximum(bL + m, jnp.max(a, axis=-1))
        wa = jnp.exp(a - m_new[..., None])
        decay = jnp.exp(bL + m - m_new)
        C_new = decay[..., None, None] * C + jnp.einsum('bhs,bhsv,bhsd->bhvd', wa, vc, kc)
        n_new = decay[..., None] * n + jnp.einsum('bhs,bhsd->bhd', wa, kc)
        return (C_new, n_new, m_new), h_out

    init = (jnp.zeros((B, A_HEADS, A_DV, A_DQK), jnp.float32),
            jnp.zeros((B, A_HEADS, A_DQK), jnp.float32),
            jnp.full((B, A_HEADS), NEG_INIT, jnp.float32))
    _, hs = lax.scan(step, init, (to_chunks(q), to_chunks(k), to_chunks(v),
                                  gate_chunks(i_log), gate_chunks(f_log)))
    hs = hs.transpose(1, 0, 3, 2, 4).reshape(B, S, A_HEADS, A_DV)
    hs = hs * lax.rsqrt(jnp.mean(hs * hs, axis=-1, keepdims=True) + EPS)
    hs = hs.reshape(B, S, A_V) * g_head.astype(jnp.float32)
    hs = jax.nn.sigmoid(o_pre.astype(jnp.float32)) * hs
    return hs.astype(h.dtype) @ w_out

def chunked_relpos_attention(h, w_q, rel_table, w_o, k_sh, v_sh):
    B, S, _ = h.shape
    nc = S // CHUNK
    q = (h @ w_q).reshape(B, S, B_HEADS, B_DH) * (B_DH ** -0.5)
    q_chunks = q.reshape(B, nc, CHUNK, B_HEADS, B_DH).transpose(1, 0, 2, 3, 4)
    pad = ((0, 0), (LEFT_CHUNKS * CHUNK, 0), (0, 0), (0, 0))
    k_pad = jnp.pad(k_sh, pad)
    v_pad = jnp.pad(v_sh, pad)
    qi = jnp.arange(CHUNK)[:, None]
    kj = jnp.arange(BAND)[None, :]
    dist = LEFT_CHUNKS * CHUNK + qi - kj
    rel_idx = jnp.clip(dist, -MAX_REL, MAX_REL) + MAX_REL
    bias = rel_table.astype(jnp.float32)[:, rel_idx]

    def one_chunk(args):
        c, qc = args
        start = c * CHUNK
        kb = lax.dynamic_slice_in_dim(k_pad, start, BAND, axis=1)
        vb = lax.dynamic_slice_in_dim(v_pad, start, BAND, axis=1)
        s = jnp.einsum('bqhd,bkhd->bhqk', qc, kb).astype(jnp.float32) + bias
        valid = (start - LEFT_CHUNKS * CHUNK + jnp.arange(BAND)) >= 0
        s = jnp.where(valid, s, -jnp.inf)
        p = jax.nn.softmax(s, axis=-1)
        return jnp.einsum('bhqk,bkhd->bqhd', p.astype(vb.dtype), vb)

    out = lax.map(one_chunk, (jnp.arange(nc), q_chunks))
    out = out.transpose(1, 0, 2, 3, 4).reshape(B, S, B_DIM)
    return out @ w_o

def second_inputs(seed: int = 0) -> dict:
    key = jax.random.key(seed)
    ks = jax.random.split(key, 20)
    nrm = jax.random.normal
    f32 = jnp.float32
    x = nrm(ks[0], (BATCH, SEQ, D_MODEL), f32)
    a_w_in = nrm(ks[1], (N_A_LAYERS, D_MODEL, A_IN), f32) * D_MODEL ** -0.5
    a_b_gate = jnp.concatenate([0.1 * nrm(ks[2], (N_A_LAYERS, A_HEADS), f32),
                                3.0 + 0.5 * nrm(ks[3], (N_A_LAYERS, A_HEADS), f32)], axis=-1)
    a_g_head = 1.0 + 0.05 * nrm(ks[4], (N_A_LAYERS, A_V), f32)
    a_w_out = nrm(ks[5], (N_A_LAYERS, A_V, D_MODEL), f32) * A_V ** -0.5
    b_w_q = nrm(ks[6], (N_B_LAYERS, D_MODEL, B_DIM), f32) * D_MODEL ** -0.5
    b_rel_bias = 0.1 * nrm(ks[7], (N_B_LAYERS, B_HEADS, N_REL), f32)
    b_w_o = nrm(ks[8], (N_B_LAYERS, B_DIM, D_MODEL), f32) * B_DIM ** -0.5
    kv_norm_g = 1.0 + 0.05 * nrm(ks[9], (D_MODEL,), f32)
    w_kv = nrm(ks[10], (D_MODEL, 2 * B_DIM), f32) * D_MODEL ** -0.5
    norm_mix_g = 1.0 + 0.05 * nrm(ks[11], (DEPTH, D_MODEL), f32)
    norm_ffn_g = 1.0 + 0.05 * nrm(ks[12], (DEPTH, D_MODEL), f32)
    ffn_w_gate = nrm(ks[13], (DEPTH, D_MODEL, D_FF_2), f32) * D_MODEL ** -0.5
    ffn_w_up = nrm(ks[14], (DEPTH, D_MODEL, D_FF_2), f32) * D_MODEL ** -0.5
    ffn_w_down = nrm(ks[15], (DEPTH, D_FF_2, D_MODEL), f32) * D_FF_2 ** -0.5
    final_norm_g = 1.0 + 0.05 * nrm(ks[16], (D_MODEL,), f32)
    return {"x": x, "a_w_in": a_w_in, "a_b_gate": a_b_gate, "a_g_head": a_g_head,
            "a_w_out": a_w_out, "b_w_q": b_w_q, "b_rel_bias": b_rel_bias, "b_w_o": b_w_o,
            "kv_norm_g": kv_norm_g, "w_kv": w_kv, "norm_mix_g": norm_mix_g,
            "norm_ffn_g": norm_ffn_g, "ffn_w_gate": ffn_w_gate, "ffn_w_up": ffn_w_up,
            "ffn_w_down": ffn_w_down, "final_norm_g": final_norm_g}

def second_block(x, a_w_in, a_b_gate, a_g_head, a_w_out, b_w_q, b_rel_bias, b_w_o,
              kv_norm_g, w_kv, norm_mix_g, norm_ffn_g, ffn_w_gate, ffn_w_up,
              ffn_w_down, final_norm_g):
    B, S, _ = x.shape
    h = x
    k_sh = None
    v_sh = None
    for l in range(DEPTH):
        if l == N_A_LAYERS:
            kv = rmsnorm(h, kv_norm_g) @ w_kv
            k_sh = kv[..., :B_DIM].reshape(B, S, B_HEADS, B_DH)
            v_sh = kv[..., B_DIM:].reshape(B, S, B_HEADS, B_DH)
        hn = rmsnorm(h, norm_mix_g[l])
        if l < N_A_LAYERS:
            h = h + mlstm_mixer(hn, a_w_in[l], a_b_gate[l], a_g_head[l], a_w_out[l])
        else:
            j = l - N_A_LAYERS
            h = h + chunked_relpos_attention(hn, b_w_q[j], b_rel_bias[j], b_w_o[j], k_sh, v_sh)
        h = h + swiglu(rmsnorm(h, norm_ffn_g[l]), ffn_w_gate[l], ffn_w_up[l], ffn_w_down[l])
    return rmsnorm(h, final_norm_g)


def setup_inputs(seed=0):
    out = dict(first_inputs(seed))
    for name, value in second_inputs(seed + 1).items():
        if name != "x":
            out[name + "_2"] = value
    return out


def reference(
    x, norm_g, ffn_w_gate, ffn_w_up, ffn_w_down, ab_w_in, conv_w, conv_b, conv_ln_g, conv_ln_b,
    swa_sinks, ab_w_out, fox_w_in, fox_b_f, fox_w_out, a_w_in_2, a_b_gate_2, a_g_head_2,
    a_w_out_2, b_w_q_2, b_rel_bias_2, b_w_o_2, kv_norm_g_2, w_kv_2, norm_mix_g_2, norm_ffn_g_2,
    ffn_w_gate_2, ffn_w_up_2, ffn_w_down_2, final_norm_g_2,
):
    x = first_block(
        x, norm_g, ffn_w_gate, ffn_w_up, ffn_w_down, ab_w_in, conv_w, conv_b, conv_ln_g,
        conv_ln_b, swa_sinks, ab_w_out, fox_w_in, fox_b_f, fox_w_out,
    )
    return second_block(
        x, a_w_in_2, a_b_gate_2, a_g_head_2, a_w_out_2, b_w_q_2, b_rel_bias_2, b_w_o_2,
        kv_norm_g_2, w_kv_2, norm_mix_g_2, norm_ffn_g_2, ffn_w_gate_2, ffn_w_up_2, ffn_w_down_2,
        final_norm_g_2,
    )


_drawn_inputs = setup_inputs


def setup_inputs(seed=0):
    import zlib

    import numpy as np

    out = dict(_drawn_inputs(seed))
    spreads = {}
    factors = {'a_g_head_2': 4.106, 'b_rel_bias_2': 8.0, 'kv_norm_g_2': 5.711}
    for name, (base, spread) in spreads.items():
        noise = np.random.default_rng([zlib.crc32(name.encode()), seed]).standard_normal(out[name].shape)
        drawn = base * np.exp(spread * noise) if base else spread * noise
        out[name] = __import__('jax').numpy.asarray(drawn.astype(out[name].dtype))
    for name, factor in factors.items():
        out[name] = (out[name] * factor).astype(out[name].dtype)
    return out
```

```python
from contextlib import ExitStack

import concourse.bass as bass
from concourse import mybir

F32 = mybir.dt.float32
F32R = mybir.dt.float32r
BF16 = mybir.dt.bfloat16
ALU = mybir.AluOpType
ACT = mybir.ActivationFunctionType
AX_X = mybir.AxisListType.X

P = 128
S = 256
T = S // P
D = 1024
KB = D // P
FF = 2816
FC = 256
NC = FF // FC
PIECE = 2048
RING = 3
CH = 512
CB = CH // P
TAPS = 31
EPS = 1e-6
NEG = -1e30
DH = 64
N_REL = 513
TABLES = "natural_log_exp_and_others"

SWA, FOX, MLSTM, REL = range(4)
HEADS = {SWA: 8, FOX: 16, MLSTM: 8, REL: 16}
HEAD0 = {SWA: 0, FOX: 8, MLSTM: 24, REL: 32}
HEAD0_AUG = {FOX: 0, MLSTM: 16}
O_PAIR0 = {SWA: 0, FOX: 4, REL: 12}
O_BLOCK = {SWA: 4, FOX: 0, REL: 0}
GATES = {FOX: 0, MLSTM: 2}
LF_STEPS = 3
MAX_REL_1 = 256
N_CONST = 39


def plan():
    steps, piece = [], 0

    def add(kind, n_pieces=0, **more):
        nonlocal piece
        steps.append(dict(kind=kind, piece=piece, n=n_pieces, **more))
        piece += n_pieces

    def ffn(index, pre_g, post_g, block):
        add("pre", g=pre_g)
        add("ffn", 2 * NC + NC, index=index, block=block)
        add("post", g=post_g, scale=0.5)

    def mixer(kind, chunks, pre_g, post_g):
        add("pre", g=pre_g)
        for form, what, n in chunks:
            if form == "pre":
                add("pre", g=what)
            else:
                add("proj", n, mixer=kind, form=form, what=what)
        add("mix", mixer=kind)
        add("out", 4, mixer=kind)
        add("post", g=post_g, scale=1.0)

    ffn(0, ("norm_g", 0, 0), ("norm_g", 0, 1), 1)
    mixer(SWA, [("feature", "u", 2), ("feature", "gate", 2), ("feature", "q0", 2), ("both", "kv", 1)],
          ("norm_g", 0, 2), ("norm_g", 0, 3))
    ffn(1, ("norm_g", 0, 4), ("norm_g", 0, 5), 1)
    ffn(2, ("norm_g", 1, 0), ("norm_g", 1, 1), 1)
    mixer(FOX, [("gates", "z", 0), ("feature", "k0", 2), ("sums", "c", 0), ("feature", "k1", 2),
                ("feature", "q0", 2), ("feature", "q1", 2), ("token", "v0", 2), ("token", "v1", 2)],
          ("norm_g", 1, 2), ("norm_g", 1, 3))
    ffn(3, ("norm_g", 1, 4), ("norm_g", 1, 5), 1)
    mixer(MLSTM, [("gates", "z", 0), ("feature", "k0", 2), ("sums", "c", 0), ("feature", "q0", 2),
                  ("token", "v0", 2), ("token", "v1", 2), ("token", "o0", 2), ("token", "o1", 2)],
          ("norm_mix_g_2", 0), None)
    ffn(4, ("norm_ffn_g_2", 0), None, 2)
    mixer(REL, [("feature", "k0", 2), ("feature", "k1", 2), ("token", "v0", 2), ("token", "v1", 2),
                ("pre", ("norm_mix_g_2", 1), 0), ("feature", "q0", 2), ("feature", "q1", 2)],
          ("kv_norm_g_2",), None)
    ffn(5, ("norm_ffn_g_2", 1), None, 2)
    add("final", g=("final_norm_g_2",))
    for n, s in enumerate(x for x in steps if x["kind"] == "proj"):
        s["chunk"] = n
    for kind in ("pre", "post"):
        for n, s in enumerate(x for x in steps if x["kind"] == kind):
            s["at"] = n
    for u, s in enumerate(x for x in steps if x.get("g") is not None):
        s["use"] = u
    for n, s in enumerate(x for x in steps if x["kind"] in ("pre", "final")):
        s["at"] = s["at_normed"] = n
    for n, s in enumerate(x for x in steps if x["kind"] == "post" and x["g"] is not None):
        s["at_normed"] = n
    turns = 0
    for s in steps:
        if s["kind"] == "pre" or (s["kind"] == "mix" and s["mixer"] == MLSTM):
            s["turn"] = turns
            turns += 1
        elif s["kind"] in ("ffn", "proj", "out"):
            s["after_turn"] = turns - 1
    for a, b in zip(steps, steps[1:]):
        if a["kind"] == "pre" and b["kind"] == "proj":
            if b["what"] == "q0":
                a["inside"] = True
            elif b["mixer"] != SWA:
                a["loads"] = b["mixer"]
    return steps, piece


def program(nc, A, out):
    steps, n_pieces = plan()
    gained = [s for s in steps if s.get("g") is not None]
    n_pre = sum(1 for s in steps if s["kind"] == "pre")

    with ExitStack() as ctx:
        def sb(name, shape, dt=F32):
            return ctx.enter_context(nc.sbuf_tensor(name, shape, dt))

        def sem(name):
            return ctx.enter_context(nc.semaphore(name))

        raw = [sb(f"raw{i}", [P, PIECE]) for i in range(RING)]
        w_hi = [sb(f"w_hi{i}", [P, PIECE], F32R) for i in range(RING)]
        w_lo = [sb(f"w_lo{i}", [P, PIECE], F32R) for i in range(RING)]
        x = sb("x_res", [P, T, D])
        xn = sb("xn", [P, T, D])
        junk = sb("junk", [P, D])
        xt_hi = sb("xt_hi", [P, KB, S], F32R)
        xt_lo = sb("xt_lo", [P, KB, S], F32R)
        gain = [sb(f"gain{i}", [P, D]) for i in range(2)]
        ssq = sb("ssq", [P, T])
        lnv = sb("lnv", [P, T])
        rstd = sb("rstd", [P, T])
        pssq = sb("pssq", [P, T])
        plnv = sb("plnv", [P, T])
        prstd = sb("prstd", [P, T])
        epst = sb("epst", [P, 1])
        eps4t = sb("eps4t", [P, 1])
        shared = sb("shared", [P, 5 * 3 * P])
        eg, sg, hid = (shared[:, i * T * FC:(i + 1) * T * FC].rearrange("p (t n) -> p t n", t=T)
                       for i in range(3))
        ht_hi = sb("ht_hi", [P, 2, S], F32R)
        ht_lo = sb("ht_lo", [P, 2, S], F32R)
        ident = sb("ident", [P, P])
        ones = sb("ones", [P, P])
        upper = sb("upper", [P, P])
        flip = sb("flip", [P, P])
        mean_w = sb("mean_w", [P, P])
        ident_b = sb("ident_b", [P, P], BF16)
        causal_b = sb("causal_b", [P, P], BF16)
        chunk_b = sb("chunk_b", [P, P], BF16)
        dist = sb("dist", [P, S])
        alibi_b = sb("alibi_b", [P, 8, S], BF16)
        head_rows = sb("head_rows", [P, 16])
        row_a = sb("row_a", [P, 1])
        row_b = sb("row_b", [P, 1])
        qz = sb("qz", [P, 16, S])
        kt = sb("kt", [P, 8, S])
        vt = sb("vt", [P, T, D])
        mx = sb("mx", [P, 16, S])
        a_in = mx[:, 0:4, :]
        a_gate = mx[:, 4:8, :]
        acc = mx[:, 8:12, :]
        a_sq = mx[:, 12:16, :]
        a_pad = sb("a_pad", [P, CB, TAPS - 1 + S])
        conv_rows = sb("conv_rows", [TAPS + 3, CH])
        conv_cols = sb("conv_cols", [P, CB, TAPS + 3])
        o_gate = mx[:, 0:8, :].rearrange("p a b -> p (a b)").rearrange("p (t n) -> p t n", t=T)
        og_gain = sb("og_gain", [P, D])
        zw = sb("zw", [P, KB, 16])
        zw_hi = sb("zw_hi", [P, KB, 16], F32R)
        zw_lo = sb("zw_lo", [P, KB, 16], F32R)
        z_bias = sb("z_bias", [P, 16])
        z = sb("z", [P, T, 16])
        z_neg = sb("z_neg", [P, T, 16])
        z_exp = sb("z_exp", [P, T, 16])
        z_ln = sb("z_ln", [P, T, 16])
        lf = sb("lf", [P, T, P])
        ig = sb("ig", [P, T, P])
        c_rows = sb("c_rows", [P, S])
        aug_q = sb("aug_q", [P, S])
        aug_k = sb("aug_k", [P, S])
        aug_h = [sb(f"aug_h{i}", [P, S]) for i in range(2)]
        sinks = sb("sinks", [P, 8])
        prob = [shared[:, i * 3 * P:(i + 1) * 3 * P] for i in range(3)]
        prob_t = [shared[:, i * 3 * P:(i + 1) * 3 * P] for i in range(3, 5)]
        top = sb("top", [P, 48, T])
        ntop = sb("ntop", [P, 48, T])
        mass = sb("mass", [P, 48, T])
        mass2 = sb("mass2", [P, 48, T])
        em = sb("em", [P, 48, T])
        rmass = sb("rmass", [P, 48, T])
        hs_ms = sb("hs_ms", [P, T, 8])
        hs_r = sb("hs_r", [P, T, 8])

        ps = ctx.enter_context(nc.psum_tensor("ps", [P, 8, 512], F32))
        y_bank = lambda t: ps[:, 2 * t:2 * t + 2, :]
        gu_bank = lambda t: ps[:, 4 + t, :]
        HT_BANK = 6

        raw_landed = [sem(f"raw_landed{i}") for i in range(RING)]
        hi_made = sem("hi_made")
        lo_made = sem("lo_made")
        piece_used = sem("piece_used")
        x_landed = sem("x_landed")
        small_landed = sem("small_landed")
        gain_landed = [sem(f"gain_landed{i}") for i in range(2)]
        rel_landed = sem("rel_landed")
        zw_landed = sem("zw_landed")
        og_landed = sem("og_landed")
        consts_made = sem("consts_made")
        dve_step = sem("dve_step")
        act_step = sem("act_step")
        rstd_made = sem("rstd_made")
        xn_made = sem("xn_made")
        prstd_made = sem("prstd_made")
        normed_y = sem("normed_y")
        x_added = sem("x_added")
        turned = sem("turned")
        xt_hi_made = sem("xt_hi_made")
        xt_lo_made = sem("xt_lo_made")
        exp_made = sem("exp_made")
        hid_step = sem("hid_step")
        ht_turned = sem("ht_turned")
        ht_hi_made = sem("ht_hi_made")
        ht_lo_made = sem("ht_lo_made")
        gates_made = sem("gates_made")
        proj_read = sem("proj_read")
        lf_made = sem("lf_made")
        aug_made = sem("aug_made")
        zw_split = sem("zw_split")
        lf_step = sem("lf_step")
        conv_turned = sem("conv_turned")
        a_made = sem("a_made")
        conv_ready = sem("conv_ready")
        conv_made = sem("conv_made")
        mean_made = sem("mean_made")
        centered = sem("centered")
        squared = sem("squared")
        var_made = sem("var_made")
        conv_rstd = sem("conv_rstd")
        conv_normed = sem("conv_normed")
        conv_act = sem("conv_act")
        conv_silu = sem("conv_silu")
        conv_hi = sem("conv_hi")
        conv_lo = sem("conv_lo")
        scores_made = sem("scores_made")
        top_made = sem("top_made")
        prob_made = sem("prob_made")
        prob_normed = sem("prob_normed")
        prob_turned = sem("prob_turned")
        prob_t_made = sem("prob_t_made")
        o_made = sem("o_made")
        o_hi_made = sem("o_hi_made")
        o_lo_made = sem("o_lo_made")
        hs_made = sem("hs_made")
        hs_sum = sem("hs_sum")
        hs_gated = sem("hs_gated")
        hs_rstd = sem("hs_rstd")
        stored = sem("stored")

        def rows(w, k0, n, c0, width):
            return w[k0:k0 + n * P, bass.ds(c0, width)].rearrange("(k p) c -> p k c", p=P)

        def ffn_weights(s):
            i = s["index"]
            if s["block"] == 1:
                return [A[n][i // 2, i % 2] for n in ("ffn_w_gate", "ffn_w_up", "ffn_w_down")]
            return [A[n][i - 4] for n in ("ffn_w_gate_2", "ffn_w_up_2", "ffn_w_down_2")]

        IN_W = {SWA: A["ab_w_in"][0], FOX: A["fox_w_in"][0], MLSTM: A["a_w_in_2"][0]}
        OUT_W = {SWA: A["ab_w_out"][0], FOX: A["fox_w_out"][0], MLSTM: A["a_w_out_2"][0],
                 REL: A["b_w_o_2"][0]}
        IN_COL = {(SWA, "u"): 0, (SWA, "gate"): CH, (SWA, "q"): 2 * CH, (SWA, "kv"): 3 * CH,
                  (FOX, "q"): 0, (FOX, "k"): D, (FOX, "v"): 2 * D, (FOX, "z"): 3 * D,
                  (MLSTM, "q"): 0, (MLSTM, "k"): 512, (MLSTM, "v"): 1024, (MLSTM, "o"): 2048,
                  (MLSTM, "z"): 3072, (REL, "k"): 0, (REL, "v"): D, (REL, "q"): 0}

        def proj_source(s):
            m, what = s["mixer"], s["what"]
            if what in ("u", "gate", "kv", "z"):
                return IN_W[m], IN_COL[m, what]
            part, at = what[0], int(what[1])
            w = (A["w_kv_2"] if part in "kv" else A["b_w_q_2"][0]) if m == REL else IN_W[m]
            return w, IN_COL[m, part] + 512 * at


        def next_splits(make):
            state = [0]

            def upto(last):
                while state[0] <= min(last, n_pieces - 1):
                    make(state[0])
                    state[0] += 1

            def skip_to(p):
                state[0] = p
            return upto, skip_to

        def landed(p):
            return 32 * (p // RING + 1)

        def after_posts(s):
            return [x for x in steps[:steps.index(s)] if x["kind"] == "post"]

        def chunks_before(s):
            return sum(1 for x in steps[:steps.index(s)] if x["kind"] == "proj")

        def half_of(s):
            return 4 * (s["chunk"] % 2)

        n_z_ln, n_hs_sq = [], []

        block = ctx.enter_context(nc.Block())

        @block.sync
        def _(sp):
            def piece(p, pairs, more=0):
                slot = p % RING
                if p >= RING or not isinstance(more, int):
                    sp.wait_ge(lo_made, p - RING + 1 + more)
                for dst, src in pairs(raw[slot]):
                    sp.dma_start(dst, src).then_inc(raw_landed[slot], 16)

            def gate_up(wg, wu, c, half):
                def pairs(r):
                    v = r[:, :].rearrange("p (k n) -> p k n", k=4)
                    return [(v[:, :, 0:FC], rows(wg, half * 512, 4, c * FC, FC)),
                            (v[:, :, FC:2 * FC], rows(wu, half * 512, 4, c * FC, FC))]
                return pairs

            def down(wd, c):
                def pairs(r):
                    v = r[:, :].rearrange("p (k n) -> p k n", k=2)
                    return [(v[:, k, :], wd[bass.ds(c * FC + k * P, P), :]) for k in range(2)]
                return pairs

            def columns(w, c0, half):
                def pairs(r):
                    v = r[:, :].rearrange("p (k n) -> p k n", k=4)
                    return [(v[:, 2 * k:2 * k + 2, :], rows(w, half * 512 + 256 * k, 2, c0, 512))
                            for k in range(2)]
                return pairs

            def narrow(w, c0):
                def pairs(r):
                    v = r[:, :].rearrange("p (k n) -> p k n", k=8)
                    return [(v[:, 4 * k:4 * k + 4, :], rows(w, 512 * k, 4, c0, 256)) for k in range(2)]
                return pairs

            sp.dma_start(x[:, :, :], A["x"][0].rearrange("(t p) d -> p t d", p=P)).then_inc(x_landed, 16)
            for s in steps:
                p = s["piece"]
                if s["kind"] == "ffn":
                    wg, wu, wd = ffn_weights(s)
                    piece(p, gate_up(wg, wu, 0, 0))
                    piece(p + 1, gate_up(wg, wu, 0, 1))

                    def chunk(c, q, more=0):
                        piece(q, gate_up(wg, wu, c, 0), more)
                        piece(q + 1, gate_up(wg, wu, c, 1), more)
                        piece(q + 2, down(wd, c - 1), more)

                    chunk(1, p + 2)
                    with sp.Fori(2, NC) as c:
                        chunk(c, p + 5, 3 * (c - 2))
                    piece(p + 3 * NC - 1, down(wd, NC - 1))
                elif s["kind"] == "proj" and s["n"]:
                    w, c0 = proj_source(s)
                    if s["form"] == "both":
                        piece(p, narrow(w, c0))
                    else:
                        for half in range(2):
                            piece(p + half, columns(w, c0, half))
                elif s["kind"] == "out":
                    for n in range(4):
                        piece(p + n, columns(OUT_W[s["mixer"]], 512 * (n // 2), n % 2))
                elif s["kind"] == "final":
                    for t in range(T):
                        sp.wait_ge(xn_made, T * n_pre + t + 1)
                        sp.dma_start(out[0, t * P:(t + 1) * P, :], xn[:, t, :]).then_inc(stored, 16)
            sp.wait_ge(stored, 16 * T)

        @block.gpsimd
        def _(pool):
            def spread(v, n=P):
                return v.partition_broadcast(n)

            pool.dma_start(conv_rows[0:TAPS, :], A["conv_w"][0]).then_inc(small_landed, 16)
            for n, name in enumerate(("conv_b", "conv_ln_g", "conv_ln_b")):
                pool.dma_start(conv_rows[TAPS + n:TAPS + n + 1, :], A[name]).then_inc(small_landed, 16)
            pool.dma_start(sinks[:, :], spread(A["swa_sinks"][0])).then_inc(small_landed, 16)
            pool.dma_start(og_gain[:, :], spread(A["a_g_head_2"][0])).then_inc(og_landed, 16)

            def gate_columns(m):
                pool.dma_start(zw[:, :, :], rows(IN_W[m], 0, KB, IN_COL[m, "z"], 16)).then_inc(zw_landed, 16)
                bias = A["fox_b_f"][0] if m == FOX else A["a_b_gate_2"][0]
                pool.dma_start(z_bias[:, :], spread(bias)).then_inc(zw_landed, 16)

            gate_columns(FOX)

            n_const = 0

            def const(ins):
                nonlocal n_const
                n_const += 1
                ins.then_inc(consts_made, 1)

            def select(m, pattern, base, mult, fill, op=ALU.not_equal):
                pool.wait_ge(consts_made, n_const)
                const(nc.gpsimd.affine_select(out=m, in_=m, compare_op=op, fill=fill, base=base,
                                              pattern=pattern, channel_multiplier=mult))

            const(nc.gpsimd.memset(ident[:, :], 0.0))
            select(ident[:, :], [[-1, P]], 0, 1, 1.0)
            const(nc.gpsimd.memset(epst[:, :], EPS))
            const(nc.gpsimd.memset(eps4t[:, :], 4 * EPS))

            uses = []

            def gain_load(s):
                u = len(uses)
                if u >= 2:
                    kind, at = uses[u - 2]
                    pool.wait_ge(xn_made if kind == "pre" else normed_y, T * (at + 1))
                name, *at = s["g"]
                v = A[name]
                for i in at:
                    v = v[i]
                pool.dma_start(gain[u % 2][:, :], spread(v)).then_inc(gain_landed[u % 2], 16)
                uses.append((s["kind"], s["at_normed"]))

            gain_load(gained[0])
            gain_load(gained[1])

            const(nc.gpsimd.memset(ones[:, :], 1.0))
            const(nc.gpsimd.memset(mean_w[:, :], 1.0 / CH))
            const(nc.gpsimd.memset(upper[:, :], 1.0))
            select(upper[:, :], [[1, P]], 0, -1, 0.0, ALU.is_ge)
            const(nc.gpsimd.memset(flip[:, :], 0.0))
            select(flip[:, :], [[1, P]], 1 - P, 1, 1.0)
            const(nc.gpsimd.memset(ident_b[:, :], 0.0))
            select(ident_b[:, :], [[-1, P]], 0, 1, 1.0)
            const(nc.gpsimd.memset(causal_b[:, :], 0.0))
            select(causal_b[:, :], [[-1, P]], 0, 1, NEG, ALU.is_ge)
            const(nc.gpsimd.memset(chunk_b[:, :], 0.0))
            select(chunk_b[:, 64:P], [[0, 64]], -64, 1, NEG, ALU.is_ge)
            const(nc.gpsimd.memset(head_rows[:, :], 0.0))
            select(head_rows[:, :], [[-1, 16]], 0, 1, 1.0)
            select(head_rows[:, :], [[-1, 16]], -16, 1, 1.0)
            const(nc.gpsimd.memset(row_a[:, :], 1.0))
            select(row_a[:, :], [[0, 1]], 15, -1, 0.0, ALU.is_ge)
            const(nc.gpsimd.memset(row_b[:, :], 1.0))
            select(row_b[:, :], [[0, 1]], 31, -1, 0.0, ALU.is_ge)
            select(row_b[:, :], [[0, 1]], -16, 1, 0.0, ALU.is_ge)
            const(nc.gpsimd.iota(dist[:, :], pattern=[[-1, S]], base=P, channel_multiplier=1,
                                 allow_small_or_imprecise_dtypes=True))
            for h in range(8):
                pool.wait_ge(consts_made, n_const)
                const(nc.gpsimd.tensor_scalar(alibi_b[:, h, :], dist[:, :], -2.0 ** -(h + 1), None, ALU.mult))
            heads_cols = [[0, 8], [-1, S]]
            select(alibi_b[:, :, :], heads_cols, P, 1, NEG, ALU.is_ge)
            select(alibi_b[:, :, :], [[0, 8], [1, S]], -1, -1, NEG, ALU.is_ge)
            const(nc.gpsimd.memset(qz[:, :, :], 0.0))
            const(nc.gpsimd.memset(lf[:, :, :], 0.0))
            const(nc.gpsimd.memset(ig[:, :, :], 0.0))
            const(nc.gpsimd.memset(a_pad[:, :, :], 0.0))
            assert n_const == N_CONST, n_const

            for s in gained[2:]:
                if s.get("loads") == MLSTM:
                    pool.wait_ge(zw_split, 2)
                    pool.wait_ge(lf_made, 1)
                    gate_columns(MLSTM)
                if s.get("loads") == REL:
                    pool.wait_ge(xn_made, T * s["at_normed"])
                    table = A["b_rel_bias_2"]
                    pool.dma_start(mx[:, :, :], bass.AP(table.tensor, table.offset + MAX_REL_1 - (P - 1),
                                                        [[1, P], [N_REL, 16], [1, S]])).then_inc(rel_landed, 16)
                gain_load(s)

        @block.scalar
        def _(act):
            n_step = 0

            def link(ins):
                nonlocal n_step
                n_step += 1
                ins.then_inc(act_step, 1)

            def linked():
                if n_step:
                    act.wait_ge(act_step, n_step)

            def hi(p, more=0, more_landed=0):
                slot = p % RING
                act.wait_ge(raw_landed[slot], landed(p) + more_landed)
                if p >= RING or not isinstance(more, int):
                    act.wait_ge(piece_used, p - RING + 1 + more)
                nc.scalar.copy(w_hi[slot][:, :], raw[slot][:, :]).then_inc(hi_made, 1)

            hi_upto, hi_skip = next_splits(hi)

            def root(src, ln, dst, eps_tile, made):
                linked()
                link(nc.scalar.activation(ln, src, ACT.Ln, bias=eps_tile))
                linked()
                nc.scalar.activation(dst, ln, ACT.Exp, scale=-0.5).then_inc(made, 1)

            def pre(s):
                posts = len(after_posts(s))
                if s.get("loads") in (FOX, MLSTM):
                    act.wait_ge(zw_landed, 32 * (1 + (s["loads"] == MLSTM)))
                    nc.scalar.copy(zw_hi[:, :, :], zw[:, :, :]).then_inc(zw_split, 1)
                for t in range(T):
                    if posts:
                        act.wait_ge(x_added, T * (posts - 1) + t + 1)
                    else:
                        act.wait_ge(x_landed, 16)
                    linked()
                    if s["at"]:
                        act.wait_ge(xn_made, T * (s["at"] - 1) + t + 1)
                    link(nc.scalar.activation(junk[:, :], x[:, t, :], ACT.Square, scale=D ** -0.5,
                                              accum_out=ssq[:, t:t + 1]))
                    root(ssq[:, t:t + 1], lnv[:, t:t + 1], rstd[:, t:t + 1], epst[:, 0:1], rstd_made)

            def turn(s):
                for g in range(4):
                    t, half = g // 2, g % 2
                    act.wait_ge(turned, 4 * s["turn"] + g + 1)
                    nc.scalar.copy(xt_hi[:, 4 * half:4 * half + 4, t * P:(t + 1) * P],
                                   ps[:, 4 + g, :].rearrange("p (k n) -> p k n", k=4)).then_inc(xt_hi_made, 1)

            def ffn(s):
                f, p = s["index"], s["piece"]

                def exp(used):
                    act.wait_ge(piece_used, used)
                    nc.scalar.activation(eg[:, :, :], ps[:, 4:6, 0:FC], ACT.Exp, scale=-1.0)\
                        .then_inc(exp_made, 1)

                def hidden(chunk):
                    act.wait_ge(ht_turned, f * NC + chunk + 1)
                    nc.scalar.copy(ht_hi[:, :, :], ps[:, HT_BANK, :].rearrange("p (k n) -> p k n", k=2))\
                        .then_inc(ht_hi_made, 1)

                exp(p + 2)
                hi(p + 3)
                hi(p + 4)
                hidden(0)
                hi(p + 5)
                with act.Fori(2, NC) as c:
                    more, more_landed = 3 * (c - 2), 32 * (c - 2)
                    exp(p + 4 + more)
                    hi(p + 6, more, more_landed)
                    hi(p + 7, more, more_landed)
                    hidden(c - 1)
                    hi(p + 8, more, more_landed)
                end = p + 3 * NC
                hi_skip(end)
                exp(end - 2)
                hi_upto(end)
                hidden(NC - 1)
                hi_upto(end + 1)

            def post(s):
                if s["g"] is not None:
                    for t in range(T):
                        act.wait_ge(piece_used, s["piece"])
                        linked()
                        if s["at_normed"]:
                            act.wait_ge(normed_y, T * (s["at_normed"] - 1) + t + 1)
                        link(nc.scalar.activation(junk[:, :].rearrange("p (b n) -> p b n", b=2), y_bank(t),
                                                  ACT.Square, scale=D ** -0.5 / s["scale"],
                                                  accum_out=pssq[:, t:t + 1]))
                        eps = epst if s["scale"] == 1.0 else eps4t
                        root(pssq[:, t:t + 1], plnv[:, t:t + 1], prstd[:, t:t + 1], eps[:, 0:1], prstd_made)

            def proj(s):
                m, form, what, b0 = s["mixer"], s["form"], s["what"], half_of(s)
                last = s["piece"] + s["n"] - 1
                if s["n"] == 2:
                    hi_upto(last + RING - 1)
                if s["n"]:
                    act.wait_ge(piece_used, last + 1)
                if form == "feature":
                    blocks = ps[:, b0:b0 + 4, 0:S]
                    if what == "u":
                        done = nc.scalar.copy(a_in, blocks)
                    elif what == "gate":
                        done = nc.scalar.activation(a_gate, blocks, ACT.Exp, scale=-1.0)
                    elif what[0] == "k":
                        at = 4 * int(what[1])
                        done = nc.scalar.copy(kt[:, at:at + 4, :], blocks)
                    elif m == SWA:
                        for odd in range(2):
                            r = slice(64 * odd, 64 * odd + 64)
                            for kv in range(2):
                                first = 2 * odd + kv
                                done = nc.scalar.mul(qz[64 * kv:64 * kv + 64, first:first + 5:4, :],
                                                     ps[r, b0 + 2 * kv:b0 + 2 * kv + 2, 0:S], DH ** -0.5)
                    else:
                        at = 8 * int(what[1])
                        for odd in range(2):
                            r = slice(64 * odd, 64 * odd + 64)
                            done = nc.scalar.mul(qz[r, at + odd:at + 8:2, :], ps[r, b0:b0 + 4, 0:S], DH ** -0.5)
                elif form == "token":
                    at = 512 * int(what[1])
                    if what[0] == "v":
                        done = nc.scalar.copy(vt[:, :, at:at + 512], ps[:, b0:b0 + 2, :])
                    else:
                        done = nc.scalar.activation(o_gate[:, :, at:at + 512], ps[:, b0:b0 + 2, :], ACT.Exp,
                                                    scale=-1.0)
                elif form == "both":
                    nc.scalar.copy(kt[:, 0, :], ps[:, b0, 0:S])
                    done = nc.scalar.copy(vt[:, :, 0:P], ps[:, b0 + 2:b0 + 4, 0:P])
                elif form == "gates":
                    act.wait_ge(gates_made, GATES[m] + 1)
                    done = nc.scalar.copy(z[:, :, :], ps[:, b0:b0 + 2, 0:16])
                elif form == "sums":
                    act.wait_ge(gates_made, GATES[m] + 2)
                    done = nc.scalar.copy(c_rows[:, :], ps[:, b0, 0:S])
                done.then_inc(proj_read, 1)
                if form == "gates":
                    act.wait_ge(lf_step, LF_STEPS * (m == MLSTM) + 2)
                    link(nc.scalar.activation(z_exp[:, :, :], z_neg[:, :, :], ACT.Exp))
                    linked()
                    link(nc.scalar.activation(z_ln[:, :, :], z_exp[:, :, :], ACT.Ln, bias=1.0))
                    n_z_ln.append(n_step)
                hi_upto(last + RING)

            def mix(s):
                m = s["mixer"]
                H = HEADS[m]
                for i in range(H + 3):
                    n = HEAD0[m] + i
                    if i < H:
                        bank = i % (2 if m == MLSTM else 4)
                        act.wait_ge(top_made, n + 1)
                        if m == MLSTM:
                            nc.scalar.activation(em[:, n, :], ntop[:, n, :], ACT.Exp)
                        if m == SWA:
                            nc.scalar.activation(em[:, n, :], ntop[:, n, :], ACT.Exp, bias=sinks[:, i:i + 1])
                        for q in range(T):
                            cols = slice(P * q, P * q + P * (q + 1))
                            sums = {} if m == MLSTM else dict(accum_out=mass[:, n, q:q + 1])
                            done = nc.scalar.activation(prob[i % 3][:, cols], ps[:, bank, cols], ACT.Exp,
                                                        bias=ntop[:, n, q:q + 1], **sums)
                        done.then_inc(prob_made, 1)
                    if 0 <= i - 2 < H:
                        act.wait_ge(prob_turned, n - 2 + 1)
                        nc.scalar.copy(prob_t[i % 2][:, :], ps[:, 4 + i % 2, 0:3 * P]).then_inc(prob_t_made, 1)
                    j = i - 3
                    if m != MLSTM and j > 0 and j % 2:
                        act.wait_ge(o_made, n - 3 + 1)
                        nc.scalar.copy(xt_hi[:, O_BLOCK[m] + j // 2, :], ps[:, 6 + (j // 2) % 2, 0:S])\
                            .then_inc(o_hi_made, 1)
                if m == SWA:
                    act.wait_ge(centered, 1)
                    nc.scalar.activation(a_sq, a_in, ACT.Square).then_inc(squared, 1)
                    act.wait_ge(var_made, 1)
                    link(nc.scalar.activation(a_gate[:, 0, :], ps[:, 5, 0:S], ACT.Ln, bias=epst[:, 0:1]))
                    linked()
                    nc.scalar.activation(a_gate[:, 1, :], a_gate[:, 0, :], ACT.Exp, scale=-0.5)\
                        .then_inc(conv_rstd, 1)
                    act.wait_ge(conv_normed, 1)
                    for b in range(CB):
                        link(nc.scalar.activation(acc[:, b, :], a_in[:, b, :], ACT.Identity,
                                                  bias=conv_cols[:, b, TAPS + 2:TAPS + 3],
                                                  scale=conv_cols[:, b, TAPS + 1:TAPS + 2]))
                    linked()
                    nc.scalar.activation(a_sq, acc, ACT.Exp, scale=-1.0).then_inc(conv_act, 1)
                    act.wait_ge(conv_silu, 3)
                    nc.scalar.copy(xt_hi[:, 0:CB, :], a_in).then_inc(conv_hi, 1)
                if m == MLSTM:
                    for t in range(T):
                        if t == 0:
                            act.wait_ge(hs_made, T * H)
                        else:
                            act.wait_ge(hs_sum, 1)
                        linked()
                        link(nc.scalar.activation(junk[:, :], xn[:, t, :], ACT.Square))
                        n_hs_sq.append(n_step)
                        act.wait_ge(hs_sum, t + 1)
                        link(nc.scalar.activation(hs_ms[:, t, :], hs_ms[:, t, :], ACT.Ln, bias=epst[:, 0:1],
                                                  scale=1.0 / P))
                        linked()
                        nc.scalar.activation(hs_r[:, t, :], hs_ms[:, t, :], ACT.Exp, scale=-0.5)\
                            .then_inc(hs_rstd, 1)
                    turn(s)

            def out_(s):
                hi_upto(s["piece"] + 3 + RING - 1)

            nc.scalar.preload_act_table_set(TABLES)
            act.wait_ge(consts_made, 4)
            hi_upto(2)
            for s in steps:
                k = s["kind"]
                if k == "pre":
                    pre(s)
                    hi_upto(s["piece"] + RING - 1)
                    if s["at"] == 0:
                        act.wait_ge(conv_turned, 1)
                        nc.scalar.copy(conv_cols[:, :, :],
                                       ps[:, 7, 0:CB * (TAPS + 3)].rearrange("p (b n) -> p b n", b=CB))\
                            .then_inc(conv_ready, 1)
                    turn(s)
                elif k == "ffn":
                    ffn(s)
                elif k == "post":
                    post(s)
                elif k == "proj":
                    proj(s)
                elif k == "mix":
                    mix(s)
                elif k == "out":
                    out_(s)
                elif k == "final":
                    pre(s)

        @block.vector
        def _(dve):
            n_step = 0

            def link(ins):
                nonlocal n_step
                n_step += 1
                ins.then_inc(dve_step, 1)

            def linked():
                if n_step:
                    dve.wait_ge(dve_step, n_step)

            def lo(p, more=0):
                slot = p % RING
                dve.wait_ge(hi_made, p + 1 + more)
                nc.vector.tensor_tensor(w_lo[slot][:, :], raw[slot][:, :], w_hi[slot][:, :].bitcast(F32),
                                        ALU.subtract).then_inc(lo_made, 1)

            lo_upto, lo_skip = next_splits(lo)

            def use_gain(s):
                u = s["use"]
                dve.wait_ge(gain_landed[u % 2], 16 * (u // 2 + 1))
                return gain[u % 2]

            def pre(s):
                if s.get("loads") in (FOX, MLSTM):
                    dve.wait_ge(zw_split, 2 * (s["loads"] == MLSTM) + 1)
                    nc.vector.tensor_tensor(zw_lo[:, :, :], zw[:, :, :], zw_hi[:, :, :].bitcast(F32),
                                            ALU.subtract).then_inc(zw_split, 1)
                for t in range(T):
                    dve.wait_ge(rstd_made, T * s["at"] + t + 1)
                    g = use_gain(s)
                    nc.vector.scalar_tensor_tensor(out=xn[:, t, :], in0=x[:, t, :], scalar=rstd[:, t:t + 1],
                                                   in1=g[:, :], op0=ALU.mult, op1=ALU.mult).then_inc(xn_made, 1)

            def turn(s):
                for g in range(4):
                    t, half = g // 2, g % 2
                    dve.wait_ge(xt_hi_made, 4 * s["turn"] + g + 1)
                    place = (slice(None), slice(4 * half, 4 * half + 4), slice(t * P, (t + 1) * P))
                    nc.vector.tensor_tensor(xt_lo[place], ps[:, 4 + g, :].rearrange("p (k n) -> p k n", k=4),
                                            xt_hi[place].bitcast(F32), ALU.subtract).then_inc(xt_lo_made, 1)

            def ffn(s):
                f, p = s["index"], s["piece"]

                def hidden(chunk):
                    at = 4 * (f * NC + chunk)
                    dve.wait_ge(exp_made, f * NC + chunk + 1)
                    nc.vector.tensor_scalar(eg[:, :, :], eg[:, :, :], 1.0, None, ALU.add).then_inc(hid_step, 1)
                    dve.wait_ge(hid_step, at + 1)
                    nc.vector.reciprocal(sg[:, :, :], eg[:, :, :]).then_inc(hid_step, 1)
                    dve.wait_ge(hid_step, at + 2)
                    nc.vector.tensor_tensor(sg[:, :, :], ps[:, 4:6, 0:FC], sg[:, :, :], ALU.mult)\
                        .then_inc(hid_step, 1)
                    dve.wait_ge(hid_step, at + 3)
                    nc.vector.tensor_tensor(hid[:, :, :], ps[:, 4:6, FC:2 * FC], sg[:, :, :], ALU.mult)\
                        .then_inc(hid_step, 1)

                def rest(chunk):
                    dve.wait_ge(ht_hi_made, f * NC + chunk + 1)
                    nc.vector.tensor_tensor(ht_lo[:, :, :], ps[:, HT_BANK, :].rearrange("p (k n) -> p k n", k=2),
                                            ht_hi[:, :, :].bitcast(F32), ALU.subtract).then_inc(ht_lo_made, 1)

                hidden(0)
                lo(p + 3)
                lo(p + 4)
                rest(0)
                lo(p + 5)
                with dve.Fori(2, NC) as c:
                    more = 3 * (c - 2)
                    hidden(c - 1)
                    lo(p + 6, more)
                    lo(p + 7, more)
                    rest(c - 1)
                    lo(p + 8, more)
                end = p + 3 * NC
                lo_skip(end)
                hidden(NC - 1)
                lo_upto(end)
                rest(NC - 1)
                lo_upto(end + 1)

            def post(s):
                for t in range(T):
                    pair = lambda v: v.rearrange("p (b n) -> p b n", b=2)
                    if s["g"] is not None:
                        dve.wait_ge(prstd_made, T * s["at_normed"] + t + 1)
                        g = use_gain(s)
                        nc.vector.scalar_tensor_tensor(out=pair(xn[:, t, :]), in0=y_bank(t),
                                                       scalar=prstd[:, t:t + 1], in1=pair(g[:, :]),
                                                       op0=ALU.mult, op1=ALU.mult).then_inc(normed_y, 1)
                        dve.wait_ge(normed_y, T * s["at_normed"] + t + 1)
                        nc.vector.tensor_tensor(x[:, t, :], x[:, t, :], xn[:, t, :], ALU.add)\
                            .then_inc(x_added, 1)
                    else:
                        dve.wait_ge(piece_used, s["piece"])
                        nc.vector.tensor_tensor(pair(x[:, t, :]), y_bank(t), pair(x[:, t, :]), ALU.add)\
                            .then_inc(x_added, 1)

            def taps(first, last):
                if first == 0:
                    for b in range(CB):
                        nc.vector.tensor_scalar(acc[:, b, :], a_pad[:, b, 0:S], conv_cols[:, b, 0:1], None,
                                                ALU.mult).then_inc(conv_made, 1)
                    first = 1
                with dve.Fori(first, last) as j:
                    for b in range(CB):
                        dve.wait_ge(conv_made, CB * j + b - CB + 1)
                        nc.vector.scalar_tensor_tensor(
                            out=acc[:, b, :], in0=a_pad[:, b, bass.ds(j, S)],
                            scalar=conv_cols[:, b, bass.ds(j, 1)], in1=acc[:, b, :],
                            op0=ALU.mult, op1=ALU.add).then_inc(conv_made, 1)

            def proj(s):
                m, form, what = s["mixer"], s["form"], s["what"]
                last = s["piece"] + s["n"] - 1
                lo_upto(last + RING)
                if what == "gate":
                    dve.wait_ge(proj_read, s["chunk"] + 1)
                    link(nc.vector.tensor_scalar(a_gate, a_gate, 1.0, None, ALU.add))
                    linked()
                    link(nc.vector.reciprocal(a_gate, a_gate))
                    linked()
                    dve.wait_ge(conv_ready, 1)
                    nc.vector.tensor_tensor(a_pad[:, :, TAPS - 1:], a_in, a_gate, ALU.mult).then_inc(a_made, 1)
                    dve.wait_ge(a_made, 1)
                    taps(0, 4)
                if m == SWA and what == "q0":
                    taps(4, 7)
                if form == "gates":
                    base = LF_STEPS * (m == MLSTM)
                    dve.wait_ge(proj_read, s["chunk"] + 1)
                    dve.wait_ge(zw_landed, 32 * (1 + (m == MLSTM)))
                    for t in range(T):
                        ins = nc.vector.tensor_tensor(z[:, t, :], z[:, t, :], z_bias[:, :], ALU.add)
                    ins.then_inc(lf_step, 1)
                    dve.wait_ge(lf_step, base + 1)
                    nc.vector.scalar_tensor_tensor(out=z_neg[:, :, :], in0=z[:, :, :], scalar=-1.0, in1=z[:, :, :],
                                                   op0=ALU.mult, op1=ALU.min).then_inc(lf_step, 1)
                    if m == MLSTM:
                        nc.vector.memset(lf[:, :, 0:32], 0.0).then_inc(lf_step, 1)
                        nc.vector.tensor_copy(ig[:, :, 0:8], z[:, :, 0:8]).then_inc(lf_step, 1)
                    n_f, f0 = (16, 0) if m == FOX else (8, 8)
                    dve.wait_ge(act_step, n_z_ln[m == MLSTM])
                    if m == MLSTM:
                        dve.wait_ge(lf_step, base + 4)
                    nc.vector.scalar_tensor_tensor(out=lf[:, :, 16:16 + n_f], in0=z[:, :, f0:16], scalar=0.0,
                                                   in1=z_ln[:, :, f0:16], op0=ALU.min, op1=ALU.subtract)\
                        .then_inc(lf_step, 1)
                    dve.wait_ge(lf_step, base + 3 + 2 * (m == MLSTM))
                    nc.vector.tensor_scalar(lf[:, :, 0:n_f], lf[:, :, 16:16 + n_f], -1.0, None, ALU.mult)\
                        .then_inc(lf_made, 1)
                if form == "sums":
                    dve.wait_ge(proj_read, s["chunk"] + 1)
                    link(nc.vector.tensor_scalar(aug_q[:, :], c_rows[:, :], row_b[:, 0:1], row_a[:, 0:1],
                                                 ALU.mult, ALU.add))
                    nc.vector.tensor_scalar(aug_k[:, :], c_rows[:, :], row_a[:, 0:1], row_b[:, 0:1],
                                            ALU.mult, ALU.add)
                    linked()
                    for i in range(2):
                        head_bias(m, i)
                if what in ("o0", "o1"):
                    dve.wait_ge(proj_read, s["chunk"] + 1)
                    at = 512 * int(what[1])
                    part = o_gate[:, :, at:at + 512]
                    link(nc.vector.tensor_scalar(part, part, 1.0, None, ALU.add))
                    linked()
                    link(nc.vector.reciprocal(part, part))
                    linked()
                    dve.wait_ge(og_landed, 16)
                    for t in range(T):
                        link(nc.vector.tensor_tensor(part[:, t, :], part[:, t, :], og_gain[:, at:at + 512],
                                                     ALU.mult))

            def head_bias(m, i):
                nc.vector.tensor_scalar(aug_h[i % 2][:, :], aug_q[:, :], head_rows[:, i:i + 1], None,
                                        ALU.mult).then_inc(aug_made, 1)

            def mix(s):
                m = s["mixer"]
                H = HEADS[m]
                for i in range(H + 3):
                    n = HEAD0[m] + i
                    if i < H:
                        bank = i % (2 if m == MLSTM else 4)
                        dve.wait_ge(scores_made, n + 1)
                        nc.vector.reduce_max(top[:, n, 0:1], ps[:, bank, 0:P], AX_X)
                        link(nc.vector.reduce_max(top[:, n, 1:2], ps[:, bank, P:3 * P], AX_X))
                        linked()
                        if m == SWA:
                            ins = nc.vector.tensor_scalar(ntop[:, n, :], top[:, n, :], sinks[:, i:i + 1], -1.0,
                                                          ALU.max, ALU.mult)
                        else:
                            ins = nc.vector.tensor_scalar(ntop[:, n, :], top[:, n, :], -1.0, None, ALU.mult)
                        ins.then_inc(top_made, 1)
                        if m in (FOX, MLSTM) and i + 2 < H:
                            head_bias(m, i + 2)
                    if 0 <= i - 1 < H:
                        normalise(m, i - 1, n - 1)
                    if m == SWA and i < 8:
                        taps(7 + 3 * i, 10 + 3 * i)
                    j = i - 3
                    if m == MLSTM and j >= 0:
                        dve.wait_ge(o_made, n - 3 + 1)
                        for t in range(T):
                            nc.vector.tensor_scalar(xn[:, t, j * P:(j + 1) * P],
                                                    ps[:, 6 + j % 2, t * P:(t + 1) * P],
                                                    rmass[:, n - 3, t:t + 1], None, ALU.mult).then_inc(hs_made, 1)
                    elif m != MLSTM and j > 0 and j % 2:
                        dve.wait_ge(o_hi_made, O_PAIR0[m] + j // 2 + 1)
                        kb = O_BLOCK[m] + j // 2
                        nc.vector.tensor_tensor(xt_lo[:, kb, :], ps[:, 6 + (j // 2) % 2, 0:S],
                                                xt_hi[:, kb, :].bitcast(F32), ALU.subtract).then_inc(o_lo_made, 1)
                if m == SWA:
                    conv_end()
                if m == MLSTM:
                    for t in range(T):
                        dve.wait_ge(act_step, n_hs_sq[t])
                        nc.vector.reduce_sum(hs_ms[:, t, :], junk[:, :].rearrange("p (h n) -> p h n", h=8), AX_X)\
                            .then_inc(hs_sum, 1)
                        dve.wait_ge(hs_rstd, t + 1)
                        by_head = xn[:, t, :].rearrange("p (h n) -> p h n", h=8)
                        link(nc.vector.tensor_tensor(by_head, by_head,
                                                     hs_r[:, t, :].unsqueeze(2).to_broadcast([P, 8, P]), ALU.mult))
                        linked()
                        nc.vector.tensor_tensor(xn[:, t, :], xn[:, t, :], o_gate[:, t, :], ALU.mult)\
                            .then_inc(hs_gated, 1)
                    turn(s)

            def normalise(m, i, n):
                dve.wait_ge(prob_made, n + 1)
                pr = prob[i % 3]
                if m == MLSTM:
                    for q in range(T):
                        cols = slice(P * q, P * q + P * (q + 1))
                        ins = nc.vector.scalar_tensor_tensor(out=pr[:, cols], in0=ps[:, 2 + i % 2, cols],
                                                             scalar=1.0, in1=pr[:, cols], op0=ALU.mult,
                                                             op1=ALU.mult, accum_out=mass[:, n, q:q + 1])
                    ins.then_inc(prob_normed, 1)
                    dve.wait_ge(prob_normed, n + 1)
                    link(nc.vector.scalar_tensor_tensor(out=mass2[:, n, :], in0=mass[:, n, :], scalar=-1.0,
                                                        in1=mass[:, n, :], op0=ALU.mult, op1=ALU.max))
                    linked()
                    link(nc.vector.tensor_tensor(top[:, n, :], mass2[:, n, :], em[:, n, :], ALU.max))
                    linked()
                    link(nc.vector.reciprocal(rmass[:, n, :], top[:, n, :]))
                    return
                total = mass
                if m == SWA:
                    link(nc.vector.tensor_tensor(mass2[:, n, :], mass[:, n, :], em[:, n, :], ALU.add))
                    linked()
                    total = mass2
                link(nc.vector.reciprocal(rmass[:, n, :], total[:, n, :]))
                linked()
                for q in range(T):
                    cols = slice(P * q, P * q + P * (q + 1))
                    ins = nc.vector.tensor_scalar(pr[:, cols], pr[:, cols], rmass[:, n, q:q + 1], None, ALU.mult)
                ins.then_inc(prob_normed, 1)

            def conv_end():
                dve.wait_ge(conv_made, CB * TAPS)
                for b in range(CB):
                    nc.vector.tensor_scalar(acc[:, b, :], acc[:, b, :], conv_cols[:, b, TAPS:TAPS + 1], None,
                                            ALU.add).then_inc(conv_made, 1)
                dve.wait_ge(mean_made, 1)
                dve.wait_ge(conv_made, CB * TAPS + CB)
                nc.vector.tensor_tensor(a_in, acc, ps[:, 4:5, 0:S].to_broadcast([P, CB, S]), ALU.subtract)\
                    .then_inc(centered, 1)
                dve.wait_ge(conv_rstd, 1)
                dve.wait_ge(centered, 1)
                nc.vector.tensor_tensor(a_in, a_in, a_gate[:, 1:2, :].to_broadcast([P, CB, S]), ALU.mult)\
                    .then_inc(conv_normed, 1)
                dve.wait_ge(conv_act, 1)
                nc.vector.tensor_scalar(a_sq, a_sq, 1.0, None, ALU.add).then_inc(conv_silu, 1)
                dve.wait_ge(conv_silu, 1)
                nc.vector.reciprocal(a_gate, a_sq).then_inc(conv_silu, 1)
                dve.wait_ge(conv_silu, 2)
                nc.vector.tensor_tensor(a_in, acc, a_gate, ALU.mult).then_inc(conv_silu, 1)
                dve.wait_ge(conv_hi, 1)
                nc.vector.tensor_tensor(xt_lo[:, 0:CB, :], a_in, xt_hi[:, 0:CB, :].bitcast(F32), ALU.subtract)\
                    .then_inc(conv_lo, 1)

            lo_upto(2)
            dve.wait_ge(consts_made, N_CONST)
            for s in steps:
                k = s["kind"]
                if k == "pre":
                    pre(s)
                    lo_upto(s["piece"] + RING - 1)
                    turn(s)
                elif k == "ffn":
                    ffn(s)
                elif k == "post":
                    post(s)
                elif k == "proj":
                    proj(s)
                elif k == "mix":
                    mix(s)
                elif k == "out":
                    lo_upto(s["piece"] + 3 + RING - 1)
                elif k == "final":
                    pre(s)

        @block.tensor
        def _(pe):
            def three(o, xh, xl, wh, wl, start, stop, stands="x"):
                for n, (a, b) in enumerate(((xh, wh), (xl, wh), (xh, wl))):
                    if stands == "w":
                        a, b = b, a
                    ins = nc.tensor.matmul(o, a, b, start=start and n == 0, stop=stop and n == 2)
                return ins

            def split(p, more=0):
                pe.wait_ge(lo_made, p + 1 + more)

            def x_blocks(kb, t):
                place = (slice(None), kb, slice(t * P, (t + 1) * P))
                return xt_hi[place], xt_lo[place]

            def turn(s):
                sem_, count = (hs_gated, 0) if s["kind"] == "mix" else (xn_made, T * s["at"])
                if s.get("inside"):
                    pe.wait_ge(proj_read, chunks_before(s))
                for g in range(4):
                    t, half = g // 2, g % 2
                    pe.wait_ge(sem_, count + t + 1)
                    for k in range(4):
                        c0 = (4 * half + k) * P
                        ins = nc.tensor.transpose(ps[:, 4 + g, k * P:(k + 1) * P], xn[:, t, c0:c0 + P],
                                                  ident[:, :])
                    ins.then_inc(turned, 1)

            def ffn(s):
                f, p, turn_at = s["index"], s["piece"], s["after_turn"]

                def gate_up(q, more=0):
                    for half in range(2):
                        slot = (q + half) % RING
                        split(q + half, more)
                        for k in range(4):
                            cols = slice(512 * k, 512 * (k + 1))
                            for t in range(T):
                                ins = three(gu_bank(t), *x_blocks(4 * half + k, t), w_hi[slot][:, cols],
                                            w_lo[slot][:, cols], (half, k) == (0, 0), (half, k) == (1, 3))
                        ins.then_inc(piece_used, 1)
                        yield

                def turn_hidden(chunk):
                    pe.wait_ge(hid_step, 4 * (f * NC + chunk + 1))
                    for k in range(2):
                        for t in range(T):
                            ins = nc.tensor.transpose(ps[:, HT_BANK, k * S + t * P:k * S + (t + 1) * P],
                                                      hid[:, t, k * P:(k + 1) * P], ident[:, :])
                    ins.then_inc(ht_turned, 1)

                def down(chunk, q, more=0, start=False, stop=False):
                    slot = q % RING
                    pe.wait_ge(ht_lo_made, f * NC + chunk + 1)
                    split(q, more)
                    for k in range(2):
                        for t in range(T):
                            for n in range(2):
                                cols = slice(k * D + n * 512, k * D + (n + 1) * 512)
                                h = (slice(None), k, slice(t * P, (t + 1) * P))
                                ins = three(ps[:, 2 * t + n, :], ht_hi[h], ht_lo[h], w_hi[slot][:, cols],
                                            w_lo[slot][:, cols], start and k == 0, stop and k == 1)
                    ins.then_inc(piece_used, 1)

                def step(chunk, q, more=0, start=False):
                    pe.wait_ge(hid_step, 4 * (f * NC + chunk))
                    halves = gate_up(q, more)
                    next(halves)
                    turn_hidden(chunk - 1)
                    next(halves)
                    down(chunk - 1, q + 2, more, start)

                pe.wait_ge(xt_lo_made, 4 * (turn_at + 1))
                for _ in gate_up(p):
                    pass
                step(1, p + 2, start=True)
                with pe.Fori(2, NC) as c:
                    step(c, p + 5, 3 * (c - 2))
                turn_hidden(NC - 1)
                down(NC - 1, p + 3 * NC - 1, stop=True)

            def proj(s):
                m, form, what, b0, p = s["mixer"], s["form"], s["what"], half_of(s), s["piece"]
                if s["chunk"] >= 2:
                    pe.wait_ge(proj_read, s["chunk"] - 1)
                pe.wait_ge(xt_lo_made, 4 * (s["after_turn"] + 1))
                if form == "gates":
                    pe.wait_ge(zw_split, 2 * (1 + (m == MLSTM)))
                    for t in range(T):
                        for kb in range(KB):
                            ins = three(ps[:, b0 + t, 0:16], *x_blocks(kb, t), zw_hi[:, kb, :], zw_lo[:, kb, :],
                                        kb == 0, kb == KB - 1)
                    ins.then_inc(gates_made, 1)
                elif form == "sums":
                    pe.wait_ge(lf_made, 1 + (m == MLSTM))
                    last = m != MLSTM
                    for t in range(T):
                        o = ps[:, b0, t * P:(t + 1) * P]
                        nc.tensor.matmul(o, lf[:, t, :], upper[:, :], start=True, stop=last and t == 0)
                        if t == 1:
                            nc.tensor.matmul(o, lf[:, 0, :], ones[:, :], start=False, stop=last)
                        if m == MLSTM:
                            nc.tensor.matmul(o, ig[:, t, :], ident[:, :], start=False, stop=True)
                    nc.tensor.matmul(ps[:, b0 + 1, 0:P], lf[:, 0, :], ones[:, :], start=True, stop=True)\
                        .then_inc(gates_made, 1)
                elif form == "both":
                    split(p)
                    slot = p % RING
                    wh, wl = (w[slot][:, :].rearrange("p (k n) -> p k n", k=KB) for w in (w_hi, w_lo))
                    for kb in range(KB):
                        ends = (kb == 0, kb == KB - 1)
                        three(ps[:, b0, 0:S], xt_hi[:, kb, :], xt_lo[:, kb, :], wh[:, kb, 0:P], wl[:, kb, 0:P],
                              *ends, stands="w")
                        for t in range(T):
                            ins = three(ps[:, b0 + 2 + t, 0:P], *x_blocks(kb, t), wh[:, kb, P:2 * P],
                                        wl[:, kb, P:2 * P], *ends)
                    ins.then_inc(piece_used, 1)
                else:
                    for half in range(2):
                        slot = (p + half) % RING
                        split(p + half)
                        for k in range(4):
                            kb = 4 * half + k
                            ends = (kb == 0, kb == KB - 1)
                            cols = slice(512 * k, 512 * (k + 1))
                            wh, wl = w_hi[slot][:, cols], w_lo[slot][:, cols]
                            if form == "token":
                                for t in range(T):
                                    ins = three(ps[:, b0 + t, :], *x_blocks(kb, t), wh, wl, *ends)
                            else:
                                for b in range(4):
                                    bs = slice(b * P, (b + 1) * P)
                                    ins = three(ps[:, b0 + b, 0:S], xt_hi[:, kb, :], xt_lo[:, kb, :],
                                                wh[:, bs], wl[:, bs], *ends, stands="w")
                        ins.then_inc(piece_used, 1)

            def scores(m, i, n):
                H = HEADS[m]
                bank = i % (2 if m == MLSTM else 4)
                qk_bank = 2 + i % 2 if m == MLSTM else bank
                slot = i if m != SWA else 2 * (i % 4) + i // 4
                kb = {SWA: 0}.get(m, i // 2)
                if m == MLSTM and i >= 2:
                    pe.wait_ge(prob_normed, n - 1)
                elif i >= 4:
                    pe.wait_ge(prob_made, n - 3)
                if m in (FOX, MLSTM):
                    pe.wait_ge(aug_made, HEAD0_AUG[m] + i + 1)
                mm = nc.tensor.matmul
                for q in range(T):
                    qs = slice(q * P, (q + 1) * P)
                    o = ps[:, bank, P * q:P * q + P * (q + 1)]
                    diagonal = ps[:, bank, 2 * P * q:2 * P * q + P]
                    if m == MLSTM:
                        mm(ps[:, qk_bank, P * q:P * q + P * (q + 1)], qz[:, slot, qs], kt[:, kb, 0:P * (q + 1)],
                           start=True, stop=True)
                        mm(o, aug_h[i % 2][:, qs], aug_k[:, 0:P * (q + 1)], start=True, stop=False)
                        ins = mm(diagonal, ident_b[:, :], causal_b[:, :], start=False, stop=True)
                        continue
                    mm(o, qz[:, slot, qs], kt[:, kb, 0:P * (q + 1)], start=True, stop=False)
                    if m == SWA:
                        ins = mm(o, ident_b[:, :], alibi_b[:, i, P * (1 - q):S], start=False, stop=True)
                    elif m == FOX:
                        mm(o, aug_h[i % 2][:, qs], aug_k[:, 0:P * (q + 1)], start=False, stop=False)
                        ins = mm(diagonal, ident_b[:, :], causal_b[:, :], start=False, stop=True)
                    else:
                        mm(diagonal, mx[:, i, 0:P], flip[:, :], start=False, stop=False)
                        if q == 1:
                            mm(ps[:, bank, P:2 * P], mx[:, i, P:S], flip[:, :], start=False, stop=False)
                        ins = mm(diagonal, ident_b[:, :], chunk_b[:, :], start=False, stop=True)
                ins.then_inc(scores_made, 1)

            def mix(s):
                m = s["mixer"]
                H = HEADS[m]
                pe.wait_ge(proj_read, chunks_before(s))
                if m == REL:
                    pe.wait_ge(rel_landed, 16)
                for i in range(H + 3):
                    n = HEAD0[m] + i
                    if i < H:
                        scores(m, i, n)
                    j = i - 3
                    if j >= 0:
                        pe.wait_ge(prob_t_made, n - 3 + 1)
                        seg = lambda g: prob_t[j % 2][:, g * P:(g + 1) * P]
                        if m == MLSTM:
                            if j >= 2:
                                pe.wait_ge(hs_made, T * (j - 1))
                            v = lambda kt_: vt[:, kt_, j * P:(j + 1) * P]
                            bank = ps[:, 6 + j % 2, :]
                            nc.tensor.matmul(bank[:, 0:P], seg(0), v(0), start=True, stop=True)
                            nc.tensor.matmul(bank[:, P:S], seg(1), v(0), start=True, stop=False)
                            ins = nc.tensor.matmul(bank[:, P:S], seg(2), v(1), start=False, stop=True)
                        else:
                            if j >= 4 and j % 2 == 0:
                                pe.wait_ge(o_lo_made, O_PAIR0[m] + j // 2 - 1)
                            c0 = (j // 4 if m == SWA else j) * DH
                            r = slice(64 * (j % 2), 64 * (j % 2) + 64)
                            v = lambda kt_: vt[:, kt_, c0:c0 + DH]
                            bank = ps[r, 6 + (j // 2) % 2, :]
                            nc.tensor.matmul(bank[:, 0:P], v(0), seg(0), start=True, stop=True)
                            nc.tensor.matmul(bank[:, P:S], v(0), seg(1), start=True, stop=False)
                            ins = nc.tensor.matmul(bank[:, P:S], v(1), seg(2), start=False, stop=True)
                        ins.then_inc(o_made, 1)
                    if 0 <= i - 2 < H:
                        k = i - 2
                        pe.wait_ge(prob_normed, n - 2 + 1)
                        if k >= 2:
                            pe.wait_ge(prob_t_made, n - 2 - 1)
                        for g in range(3):
                            ins = nc.tensor.transpose(ps[:, 4 + k % 2, g * P:(g + 1) * P],
                                                      prob[k % 3][:, g * P:(g + 1) * P], ident[:, :])
                        ins.then_inc(prob_turned, 1)
                if m == SWA:
                    for made, bank, src, first in ((mean_made, 4, acc, conv_made), (var_made, 5, a_sq, squared)):
                        pe.wait_ge(first, CB * TAPS + CB if first is conv_made else 1)
                        for b in range(CB):
                            ins = nc.tensor.matmul(ps[:, bank, 0:S], mean_w[:, :], src[:, b, :], start=b == 0,
                                                   stop=b == CB - 1)
                        ins.then_inc(made, 1)
                if m == MLSTM:
                    turn(s)

            def out_(s):
                m, p = s["mixer"], s["piece"]
                if m == MLSTM:
                    pe.wait_ge(xt_lo_made, 4 * (s["after_turn"] + 1))
                else:
                    pe.wait_ge(o_lo_made, O_PAIR0[m] + HEADS[m] // 2)
                if m == SWA:
                    pe.wait_ge(conv_lo, 1)
                for n in range(2):
                    for half in range(2):
                        q = p + 2 * n + half
                        split(q)
                        for k in range(4):
                            kb = 4 * half + k
                            cols = slice(512 * k, 512 * (k + 1))
                            for t in range(T):
                                ins = three(ps[:, 2 * t + n, :], *x_blocks(kb, t), w_hi[q % RING][:, cols],
                                            w_lo[q % RING][:, cols], kb == 0, kb == KB - 1)
                        ins.then_inc(piece_used, 1)

            pe.wait_ge(small_landed, 16 * 5)
            pe.wait_ge(consts_made, 2)
            for b in range(CB):
                ins = nc.tensor.transpose(ps[:, 7, b * (TAPS + 3):(b + 1) * (TAPS + 3)],
                                          conv_rows[:, b * P:(b + 1) * P], ident[0:TAPS + 3, 0:TAPS + 3])
            ins.then_inc(conv_turned, 1)
            pe.wait_ge(conv_ready, 1)
            for s in steps:
                k = s["kind"]
                if k == "pre":
                    turn(s)
                elif k == "ffn":
                    ffn(s)
                elif k == "proj":
                    proj(s)
                elif k == "mix":
                    pe.wait_ge(consts_made, N_CONST)
                    mix(s)
                elif k == "out":
                    out_(s)


_INS = ["x", "norm_g", "ffn_w_gate", "ffn_w_up", "ffn_w_down", "ab_w_in", "conv_w", "conv_b",
        "conv_ln_g", "conv_ln_b", "swa_sinks", "ab_w_out", "fox_w_in", "fox_b_f", "fox_w_out",
        "a_w_in_2", "a_b_gate_2", "a_g_head_2", "a_w_out_2", "b_w_q_2", "b_rel_bias_2", "b_w_o_2",
        "kv_norm_g_2", "w_kv_2", "norm_mix_g_2", "norm_ffn_g_2", "ffn_w_gate_2", "ffn_w_up_2",
        "ffn_w_down_2", "final_norm_g_2"]


def kernel(**inputs):
    import numpy as _np
    import concourse.bacc as _bacc
    from concourse.bass_utils import run_bass_kernel_spmd as _run

    nc = _bacc.Bacc("TRN2", target_bir_lowering=False, num_devices=1)
    arrays, args = {}, {}
    for name in _INS:
        a = _np.ascontiguousarray(inputs[name])
        arrays[f"in_{name}_dram"] = a
        args[name] = nc.dram_tensor(f"in_{name}_dram", a.shape, mybir.dt.from_np(a.dtype),
                                    kind="ExternalInput").ap()
    out = nc.dram_tensor("out_0_dram", (1, S, D), F32, kind="ExternalOutput").ap()
    program(nc, args, out)
    r = _run(nc, [arrays], core_ids=[0])
    return r.results[0]["out_0_dram"]
```

```python
from contextlib import ExitStack

import concourse.bass as bass
from concourse import mybir

F32 = mybir.dt.float32
F32R = mybir.dt.float32r
BF16 = mybir.dt.bfloat16
ALU = mybir.AluOpType
ACT = mybir.ActivationFunctionType
AX_X = mybir.AxisListType.X

P = 128
S = 256
T = S // P
D = 1024
KB = D // P
FF = 2816
FC = 256
NC = FF // FC
PIECE = 2048
RING = 3
CH = 512
CB = CH // P
TAPS = 31
EPS = 1e-6
NEG = -1e30
DH = 64
N_REL = 513
TABLES = "natural_log_exp_and_others"
SILU_TABLES = "silu_and_others"
SIGMOID_TABLES = "sigmoid_and_others"

SWA, FOX, MLSTM, REL = range(4)
HEADS = {SWA: 8, FOX: 16, MLSTM: 8, REL: 16}
HEAD0 = {SWA: 0, FOX: 8, MLSTM: 24, REL: 32}
HEAD0_AUG = {FOX: 0, MLSTM: 16}
O_PAIR0 = {SWA: 0, FOX: 4, REL: 12}
O_BLOCK = {SWA: 4, FOX: 0, REL: 0}
GATES = {FOX: 0, MLSTM: 2}
LF_STEPS = 3
MAX_REL_1 = 256
N_CONST = 39
TAP_HEAD0 = 8


def plan():
    steps, piece = [], 0

    def add(kind, n_pieces=0, **more):
        nonlocal piece
        steps.append(dict(kind=kind, piece=piece, n=n_pieces, **more))
        piece += n_pieces

    def ffn(index, pre_g, post_g, block):
        add("pre", g=pre_g)
        add("ffn", 2 * NC + NC, index=index, block=block)
        add("post", g=post_g, scale=0.5)

    def mixer(kind, chunks, pre_g, post_g):
        add("pre", g=pre_g)
        for form, what, n in chunks:
            if form == "again":
                add("again", g=what)
            else:
                add("proj", n, mixer=kind, form=form, what=what)
        add("mix", mixer=kind)
        add("out", 4, mixer=kind)
        add("post", g=post_g, scale=1.0)

    ffn(0, ("norm_g", 0, 0), ("norm_g", 0, 1), 1)
    mixer(SWA, [("feature", "a0", 2), ("feature", "a1", 2), ("feature", "q0", 2), ("both", "kv", 1)],
          ("norm_g", 0, 2), ("norm_g", 0, 3))
    ffn(1, ("norm_g", 0, 4), ("norm_g", 0, 5), 1)
    ffn(2, ("norm_g", 1, 0), ("norm_g", 1, 1), 1)
    mixer(FOX, [("token", "v0", 2), ("gates", "z", 0), ("token", "v1", 2), ("sums", "c", 0),
                ("feature", "k0", 2), ("feature", "k1", 2), ("feature", "q0", 2), ("feature", "q1", 2)],
          ("norm_g", 1, 2), ("norm_g", 1, 3))
    ffn(3, ("norm_g", 1, 4), ("norm_g", 1, 5), 1)
    mixer(MLSTM, [("token", "v0", 2), ("gates", "z", 0), ("token", "v1", 2), ("sums", "c", 0),
                  ("feature", "k0", 2), ("token", "o0", 2), ("token", "o1", 2), ("feature", "q0", 2)],
          ("norm_mix_g_2", 0), None)
    ffn(4, ("norm_ffn_g_2", 0), None, 2)
    mixer(REL, [("token", "v0", 2), ("token", "v1", 2), ("feature", "k0", 2), ("feature", "k1", 2),
                ("again", ("norm_mix_g_2", 1), 0), ("feature", "q0", 2), ("feature", "q1", 2)],
          ("kv_norm_g_2",), None)
    ffn(5, ("norm_ffn_g_2", 1), None, 2)
    add("final", g=("final_norm_g_2",))
    for n, s in enumerate(x for x in steps if x["kind"] == "proj"):
        s["chunk"] = n
    for u, s in enumerate(x for x in steps if x.get("g") is not None):
        s["use"] = u
    for n, s in enumerate(x for x in steps if x["kind"] in ("pre", "again", "final")):
        s["at"] = n
    for n, s in enumerate(x for x in steps if x["kind"] in ("pre", "final")):
        s["stat"] = n
    for n, s in enumerate(x for x in steps if x["kind"] == "post"):
        s["at"] = n
    for n, s in enumerate(x for x in steps if x["kind"] == "post" and x["g"] is not None):
        s["at_normed"] = n
    for n, s in enumerate(x for x in steps if x["kind"] in ("ffn", "out")):
        s["y"] = n
    turns = 0
    for n, s in enumerate(steps):
        if s["kind"] in ("pre", "again") or (s["kind"] == "mix" and s["mixer"] == MLSTM):
            s["turn"] = turns
            turns += 1
        elif s["kind"] in ("ffn", "proj", "out"):
            s["after_turn"] = turns - 1
        if s["kind"] in ("pre", "final"):
            s["post"] = steps[n - 1] if n else None
            s["defer"] = steps[n + 1]["kind"] == "ffn" if s["kind"] == "pre" else False
        if s["kind"] == "mix":
            s["out"] = steps[n + 1]
        if s["kind"] == "proj" and steps[n - 1]["kind"] == "pre":
            s["first"] = True
            if s["mixer"] != SWA:
                steps[n - 1]["loads"] = s["mixer"]
        if s["kind"] == "post":
            s["y"] = steps[n - 1]["y"]
        if s["kind"] == "ffn":
            s["stat"] = steps[n - 1]["stat"]
        if s["kind"] == "again":
            s["stat"] = steps[n - 5]["stat"]
    return steps, piece


def program(nc, A, out):
    steps, n_pieces = plan()
    gained = [s for s in steps if s.get("g") is not None]
    n_pre = sum(1 for s in steps if s["kind"] in ("pre", "again"))
    pool_pieces = [p for s in steps if s.get("mixer") == SWA for p in range(s["piece"], s["piece"] + s["n"])]

    with ExitStack() as ctx:
        def sb(name, shape, dt=F32):
            return ctx.enter_context(nc.sbuf_tensor(name, shape, dt))

        def sem(name):
            return ctx.enter_context(nc.semaphore(name))

        raw = [sb(f"raw{i}", [P, PIECE]) for i in range(RING)]
        w_hi = [sb(f"w_hi{i}", [P, PIECE], F32R) for i in range(RING)]
        w_lo = [sb(f"w_lo{i}", [P, PIECE], F32R) for i in range(RING)]
        x = sb("x_res", [P, T, D])
        xn = sb("xn", [P, T, D])
        junk = sb("junk", [P, D])
        xt_hi = sb("xt_hi", [P, KB, S], F32R)
        xt_lo = sb("xt_lo", [P, KB, S], F32R)
        gain = [sb(f"gain{i}", [P, D]) for i in range(2)]
        ssq = sb("ssq", [P, T])
        lnv = sb("lnv", [P, T])
        rstd = sb("rstd", [P, T])
        pssq = sb("pssq", [P, T])
        plnv = sb("plnv", [P, T])
        prstd = sb("prstd", [P, T])
        epst = sb("epst", [P, 1])
        eps4t = sb("eps4t", [P, 1])
        shared = sb("shared", [P, 5 * 3 * P])
        sg, hid = (shared[:, i * T * FC:(i + 1) * T * FC].rearrange("p (t n) -> p t n", t=T)
                   for i in range(2))
        ht_hi = sb("ht_hi", [P, 2, S], F32R)
        ht_lo = sb("ht_lo", [P, 2, S], F32R)
        ident = sb("ident", [P, P])
        ones = sb("ones", [P, P])
        upper = sb("upper", [P, P])
        flip = sb("flip", [P, P])
        mean_w = sb("mean_w", [P, P])
        ident_b = sb("ident_b", [P, P], BF16)
        causal_b = sb("causal_b", [P, P], BF16)
        chunk_b = sb("chunk_b", [P, P], BF16)
        dist = sb("dist", [P, S])
        alibi_b = sb("alibi_b", [P, 8, S], BF16)
        head_rows = sb("head_rows", [P, 16])
        row_a = sb("row_a", [P, 1])
        row_b = sb("row_b", [P, 1])
        qz = sb("qz", [P, 16, S])
        kt = sb("kt", [P, 8, S])
        vt = sb("vt", [P, T, D])
        mx = sb("mx", [P, 16, S])
        a_in = mx[:, 0:4, :]
        a_gate = mx[:, 4:8, :]
        acc = mx[:, 8:12, :]
        a_sq = mx[:, 12:16, :]
        a_pad = sb("a_pad", [P, CB, TAPS - 1 + S])
        conv_rows = sb("conv_rows", [TAPS + 3, CH])
        conv_cols = sb("conv_cols", [P, CB, TAPS + 3])
        o_gate = mx[:, 0:8, :].rearrange("p a b -> p (a b)").rearrange("p (t n) -> p t n", t=T)
        og_gain = kt[:, 4:8, :].rearrange("p a b -> p (a b)")
        zw = sb("zw", [P, KB, 16])
        zw_hi = sb("zw_hi", [P, KB, 16], F32R)
        zw_lo = sb("zw_lo", [P, KB, 16], F32R)
        z_bias = sb("z_bias", [P, 16])
        z = sb("z", [P, T, 16])
        z_neg = sb("z_neg", [P, T, 16])
        z_exp = sb("z_exp", [P, T, 16])
        z_ln = sb("z_ln", [P, T, 16])
        lf = sb("lf", [P, T, P])
        ig = sb("ig", [P, T, P])
        c_rows = sb("c_rows", [P, S])
        aug_q = sb("aug_q", [P, S])
        aug_k = sb("aug_k", [P, S])
        aug_h = [sb(f"aug_h{i}", [P, S]) for i in range(2)]
        sinks = sb("sinks", [P, 8])
        prob = [shared[:, i * 3 * P:(i + 1) * 3 * P] for i in range(3)]
        prob_t = [shared[:, i * 3 * P:(i + 1) * 3 * P] for i in range(3, 5)]
        top = sb("top", [P, 48, T])
        ntop = sb("ntop", [P, 48, T])
        mass = sb("mass", [P, 48, T])
        mass2 = sb("mass2", [P, 48, T])
        em = sb("em", [P, 48, T])
        rmass = sb("rmass", [P, 48, T])
        hs_ms = sb("hs_ms", [P, T, 8])
        hs_r = sb("hs_r", [P, T, 8])

        ps = ctx.enter_context(nc.psum_tensor("ps", [P, 8, 512], F32))
        y_bank = lambda t: ps[:, 2 * t:2 * t + 2, :]
        gu_bank = lambda t: ps[:, 4 + t, :]
        HT_BANK = 6
        GU_FIRST = (5, 7)

        def half_cols(v, t, half):
            return v[:, t, half * 512:(half + 1) * 512]

        raw_landed = [sem(f"raw_landed{i}") for i in range(RING)]
        hi_made = sem("hi_made")
        lo_made = sem("lo_made")
        piece_used = sem("piece_used")
        x_landed = sem("x_landed")
        small_landed = sem("small_landed")
        gain_landed = [sem(f"gain_landed{i}") for i in range(2)]
        rel_landed = sem("rel_landed")
        zw_landed = sem("zw_landed")
        og_landed = sem("og_landed")
        consts_made = sem("consts_made")
        dve_step = sem("dve_step")
        act_step = sem("act_step")
        rstd_made = sem("rstd_made")
        xn_made = sem("xn_made")
        prstd_made = sem("prstd_made")
        normed_y = sem("normed_y")
        x_added = sem("x_added")
        turned = sem("turned")
        xt_hi_made = sem("xt_hi_made")
        xt_lo_made = sem("xt_lo_made")
        gu_tile0 = sem("gu_tile0")
        silu_made = sem("silu_made")
        hid_made = sem("hid_made")
        y_tile0 = sem("y_tile0")
        lo_pool = sem("lo_pool")
        ht_turned = sem("ht_turned")
        ht_hi_made = sem("ht_hi_made")
        ht_lo_made = sem("ht_lo_made")
        gates_made = sem("gates_made")
        proj_read = sem("proj_read")
        lf_made = sem("lf_made")
        aug_made = sem("aug_made")
        zw_split = sem("zw_split")
        lf_step = sem("lf_step")
        conv_turned = sem("conv_turned")
        a_made = sem("a_made")
        conv_ready = sem("conv_ready")
        conv_made = sem("conv_made")
        mean_made = sem("mean_made")
        centered = sem("centered")
        squared = sem("squared")
        var_made = sem("var_made")
        conv_rstd = sem("conv_rstd")
        conv_normed = sem("conv_normed")
        conv_hi = sem("conv_hi")
        conv_lo = sem("conv_lo")
        scores_made = sem("scores_made")
        top_made = sem("top_made")
        prob_made = sem("prob_made")
        prob_normed = sem("prob_normed")
        prob_turned = sem("prob_turned")
        prob_t_made = sem("prob_t_made")
        o_made = sem("o_made")
        o_hi_made = sem("o_hi_made")
        o_lo_made = sem("o_lo_made")
        hs_made = sem("hs_made")
        hs_sum = sem("hs_sum")
        hs_gated = sem("hs_gated")
        hs_rstd = sem("hs_rstd")
        stored = sem("stored")

        def rows(w, k0, n, c0, width):
            return w[k0:k0 + n * P, bass.ds(c0, width)].rearrange("(k p) c -> p k c", p=P)

        def ffn_weights(s):
            i = s["index"]
            if s["block"] == 1:
                return [A[n][i // 2, i % 2] for n in ("ffn_w_gate", "ffn_w_up", "ffn_w_down")]
            return [A[n][i - 4] for n in ("ffn_w_gate_2", "ffn_w_up_2", "ffn_w_down_2")]

        IN_W = {SWA: A["ab_w_in"][0], FOX: A["fox_w_in"][0], MLSTM: A["a_w_in_2"][0]}
        OUT_W = {SWA: A["ab_w_out"][0], FOX: A["fox_w_out"][0], MLSTM: A["a_w_out_2"][0],
                 REL: A["b_w_o_2"][0]}
        IN_COL = {(SWA, "a"): 0, (SWA, "q"): 2 * CH, (SWA, "kv"): 3 * CH,
                  (FOX, "q"): 0, (FOX, "k"): D, (FOX, "v"): 2 * D, (FOX, "z"): 3 * D,
                  (MLSTM, "q"): 0, (MLSTM, "k"): 512, (MLSTM, "v"): 1024, (MLSTM, "o"): 2048,
                  (MLSTM, "z"): 3072, (REL, "k"): 0, (REL, "v"): D, (REL, "q"): 0}

        def proj_source(s):
            m, what = s["mixer"], s["what"]
            if what in ("kv", "z"):
                return IN_W[m], IN_COL[m, what]
            part, at = what[0], int(what[1])
            w = (A["w_kv_2"] if part in "kv" else A["b_w_q_2"][0]) if m == REL else IN_W[m]
            return w, IN_COL[m, part] + (256 if part == "a" else 512) * at


        def lo_count(p):
            if p in pool_pieces:
                return lo_pool, pool_pieces.index(p) + 1
            return lo_made, p + 1 - sum(1 for q in pool_pieces if q < p)

        def next_splits(make):
            state = [0]

            def upto(last):
                while state[0] <= min(last, n_pieces - 1):
                    make(state[0])
                    state[0] += 1

            def skip_to(p):
                state[0] = p
            return upto, skip_to

        def landed(p):
            return 32 * (p // RING + 1)

        def chunks_before(s):
            return sum(1 for x in steps[:steps.index(s)] if x["kind"] == "proj")

        def out_half(s, n):
            return (n // 2) ^ (s["mixer"] == SWA)

        def half_of(s):
            return 4 * (s["chunk"] % 2)

        n_z_ln, n_hs_sq = [], []

        block = ctx.enter_context(nc.Block())

        @block.sync
        def _(sp):
            def piece(p, pairs, more=0):
                slot = p % RING
                if p >= RING or not isinstance(more, int):
                    split_sem, count = lo_count(p - RING)
                    sp.wait_ge(split_sem, count + more)
                for dst, src in pairs(raw[slot]):
                    sp.dma_start(dst, src).then_inc(raw_landed[slot], 16)

            def gate_up(wg, wu, c, half):
                def pairs(r):
                    v = r[:, :].rearrange("p (k n) -> p k n", k=4)
                    return [(v[:, :, 0:FC], rows(wg, half * 512, 4, c * FC, FC)),
                            (v[:, :, FC:2 * FC], rows(wu, half * 512, 4, c * FC, FC))]
                return pairs

            def down(wd, c):
                def pairs(r):
                    v = r[:, :].rearrange("p (k n) -> p k n", k=2)
                    return [(v[:, k, :], wd[bass.ds(c * FC + k * P, P), :]) for k in range(2)]
                return pairs

            def columns(w, c0, half):
                def pairs(r):
                    v = r[:, :].rearrange("p (k n) -> p k n", k=4)
                    return [(v[:, 2 * k:2 * k + 2, :], rows(w, half * 512 + 256 * k, 2, c0, 512))
                            for k in range(2)]
                return pairs

            def narrow(w, c0):
                def pairs(r):
                    v = r[:, :].rearrange("p (k n) -> p k n", k=8)
                    return [(v[:, 4 * k:4 * k + 4, :], rows(w, 512 * k, 4, c0, 256)) for k in range(2)]
                return pairs

            for s in steps:
                p = s["piece"]
                if s["kind"] == "ffn":
                    wg, wu, wd = ffn_weights(s)
                    piece(p, gate_up(wg, wu, 0, 0))
                    piece(p + 1, gate_up(wg, wu, 0, 1))

                    def chunk(c, q, more=0):
                        piece(q, gate_up(wg, wu, c, 0), more)
                        piece(q + 1, gate_up(wg, wu, c, 1), more)
                        piece(q + 2, down(wd, c - 1), more)

                    chunk(1, p + 2)
                    with sp.Fori(2, NC) as c:
                        chunk(c, p + 5, 3 * (c - 2))
                    piece(p + 3 * NC - 1, down(wd, NC - 1))
                elif s["kind"] == "proj" and s["n"]:
                    w, c0 = proj_source(s)
                    if s["form"] == "both":
                        piece(p, narrow(w, c0))
                    elif s["what"][0] == "a":
                        for half in range(2):
                            piece(p + half, gate_up(w[:, 0:CH], w[:, CH:2 * CH], int(s["what"][1]), half))
                    else:
                        for half in range(2):
                            piece(p + half, columns(w, c0, half))
                elif s["kind"] == "out":
                    for n in range(4):
                        piece(p + n, columns(OUT_W[s["mixer"]], 512 * (n % 2), out_half(s, n)))
                elif s["kind"] == "final":
                    for t in range(T):
                        sp.wait_ge(xn_made, 4 * n_pre + 2 * t + 2)
                        sp.dma_start(out[0, t * P:(t + 1) * P, :], xn[:, t, :]).then_inc(stored, 16)
            sp.wait_ge(stored, 16 * T)

        @block.gpsimd
        def _(pool):
            def spread(v, n=P):
                return v.partition_broadcast(n)

            def gate_columns(m):
                pool.dma_start(zw[:, :, :], rows(IN_W[m], 0, KB, IN_COL[m, "z"], 16)).then_inc(zw_landed, 16)
                bias = A["fox_b_f"][0] if m == FOX else A["a_b_gate_2"][0]
                pool.dma_start(z_bias[:, :], spread(bias)).then_inc(zw_landed, 16)

            n_const = 0

            def const(ins):
                nonlocal n_const
                n_const += 1
                ins.then_inc(consts_made, 1)

            def select(m, pattern, base, mult, fill, op=ALU.not_equal):
                pool.wait_ge(consts_made, n_const)
                const(nc.gpsimd.affine_select(out=m, in_=m, compare_op=op, fill=fill, base=base,
                                              pattern=pattern, channel_multiplier=mult))

            const(nc.gpsimd.memset(ident[:, :], 0.0))
            select(ident[:, :], [[-1, P]], 0, 1, 1.0)
            const(nc.gpsimd.memset(epst[:, :], EPS))
            const(nc.gpsimd.memset(eps4t[:, :], 4 * EPS))

            uses = []

            def gain_load(s):
                u = len(uses)
                if u >= 2:
                    kind, at = uses[u - 2]
                    pool.wait_ge(normed_y if kind == "post" else xn_made, 4 * (at + 1))
                name, *at = s["g"]
                v = A[name]
                for i in at:
                    v = v[i]
                pool.dma_start(gain[u % 2][:, :], spread(v)).then_inc(gain_landed[u % 2], 16)
                uses.append((s["kind"], s["at_normed"] if s["kind"] == "post" else s["at"]))

            gain_load(gained[0])
            gain_load(gained[1])
            pool.dma_start(conv_rows[0:TAPS, :], A["conv_w"][0]).then_inc(small_landed, 16)
            for n, name in enumerate(("conv_b", "conv_ln_g", "conv_ln_b")):
                pool.dma_start(conv_rows[TAPS + n:TAPS + n + 1, :], A[name]).then_inc(small_landed, 16)
            pool.dma_start(sinks[:, :], spread(A["swa_sinks"][0])).then_inc(small_landed, 16)

            gate_columns(FOX)

            const(nc.gpsimd.memset(ones[:, :], 1.0))
            const(nc.gpsimd.memset(mean_w[:, :], 1.0 / CH))
            const(nc.gpsimd.memset(upper[:, :], 1.0))
            select(upper[:, :], [[1, P]], 0, -1, 0.0, ALU.is_ge)
            const(nc.gpsimd.memset(flip[:, :], 0.0))
            select(flip[:, :], [[1, P]], 1 - P, 1, 1.0)
            const(nc.gpsimd.memset(ident_b[:, :], 0.0))
            select(ident_b[:, :], [[-1, P]], 0, 1, 1.0)
            const(nc.gpsimd.memset(causal_b[:, :], 0.0))
            select(causal_b[:, :], [[-1, P]], 0, 1, NEG, ALU.is_ge)
            const(nc.gpsimd.memset(chunk_b[:, :], 0.0))
            select(chunk_b[:, 64:P], [[0, 64]], -64, 1, NEG, ALU.is_ge)
            const(nc.gpsimd.memset(head_rows[:, :], 0.0))
            select(head_rows[:, :], [[-1, 16]], 0, 1, 1.0)
            select(head_rows[:, :], [[-1, 16]], -16, 1, 1.0)
            const(nc.gpsimd.memset(row_a[:, :], 1.0))
            select(row_a[:, :], [[0, 1]], 15, -1, 0.0, ALU.is_ge)
            const(nc.gpsimd.memset(row_b[:, :], 1.0))
            select(row_b[:, :], [[0, 1]], 31, -1, 0.0, ALU.is_ge)
            select(row_b[:, :], [[0, 1]], -16, 1, 0.0, ALU.is_ge)
            const(nc.gpsimd.iota(dist[:, :], pattern=[[-1, S]], base=P, channel_multiplier=1,
                                 allow_small_or_imprecise_dtypes=True))
            for h in range(8):
                pool.wait_ge(consts_made, n_const)
                const(nc.gpsimd.tensor_scalar(alibi_b[:, h, :], dist[:, :], -2.0 ** -(h + 1), None, ALU.mult))
            heads_cols = [[0, 8], [-1, S]]
            select(alibi_b[:, :, :], heads_cols, P, 1, NEG, ALU.is_ge)
            select(alibi_b[:, :, :], [[0, 8], [1, S]], -1, -1, NEG, ALU.is_ge)
            const(nc.gpsimd.memset(qz[:, :, :], 0.0))
            const(nc.gpsimd.memset(lf[:, :, :], 0.0))
            const(nc.gpsimd.memset(ig[:, :, :], 0.0))
            const(nc.gpsimd.memset(a_pad[:, :, :], 0.0))
            assert n_const == N_CONST, n_const

            def lo(p):
                slot = p % RING
                pool.wait_ge(hi_made, p + 1)
                nc.gpsimd.tensor_tensor(w_lo[slot][:, :], raw[slot][:, :], w_hi[slot][:, :].bitcast(F32),
                                        ALU.subtract).then_inc(lo_pool, 1)

            for u, s in enumerate(gained[2:], start=2):
                if s.get("loads") == MLSTM:
                    pool.wait_ge(zw_split, 2)
                    pool.wait_ge(lf_made, 1)
                    gate_columns(MLSTM)
                    pool.wait_ge(x_added, 4 * (s["post"]["at"]))
                    pool.dma_start(og_gain, spread(A["a_g_head_2"][0])).then_inc(og_landed, 16)
                if s.get("loads") == REL:
                    pool.wait_ge(hs_gated, T)
                    table = A["b_rel_bias_2"]
                    pool.dma_start(mx[:, :, :], bass.AP(table.tensor, table.offset + MAX_REL_1 - (P - 1),
                                                        [[1, P], [N_REL, 16], [1, S]])).then_inc(rel_landed, 16)
                if u == 3:
                    lo(pool_pieces[0])
                    lo(pool_pieces[1])
                if u == 4:
                    for p in pool_pieces[2:]:
                        lo(p)
                gain_load(s)

        @block.scalar
        def _(act):
            n_step = 0

            def link(ins):
                nonlocal n_step
                n_step += 1
                ins.then_inc(act_step, 1)

            def linked():
                if n_step:
                    act.wait_ge(act_step, n_step)

            def hi(p, more=0, more_landed=0):
                slot = p % RING
                act.wait_ge(raw_landed[slot], landed(p) + more_landed)
                if p >= RING or not isinstance(more, int):
                    act.wait_ge(piece_used, p - RING + 1 + more)
                nc.scalar.copy(w_hi[slot][:, :], raw[slot][:, :]).then_inc(hi_made, 1)

            hi_upto, hi_skip = next_splits(hi)

            def root(src, ln, dst, eps_tile, made):
                linked()
                link(nc.scalar.activation(ln, src, ACT.Ln, bias=eps_tile))
                linked()
                nc.scalar.activation(dst, ln, ACT.Exp, scale=-0.5).then_inc(made, 1)

            def post_square(s, t):
                if s["g"] is None:
                    return
                if t == 0:
                    act.wait_ge(y_tile0, s["y"] + 1)
                else:
                    act.wait_ge(piece_used, s["piece"])
                linked()
                if s["at_normed"]:
                    act.wait_ge(normed_y, 4 * (s["at_normed"] - 1) + 2 * t + 2)
                link(nc.scalar.activation(junk[:, :].rearrange("p (b n) -> p b n", b=2), y_bank(t),
                                          ACT.Square, scale=D ** -0.5 / s["scale"],
                                          accum_out=pssq[:, t:t + 1]))
                eps = epst if s["scale"] == 1.0 else eps4t
                root(pssq[:, t:t + 1], plnv[:, t:t + 1], prstd[:, t:t + 1], eps[:, 0:1], prstd_made)

            def pre_square(s, t):
                if s["post"]:
                    act.wait_ge(x_added, 4 * s["post"]["at"] + 2 * t + 2)
                else:
                    act.wait_ge(x_landed, 16)
                linked()
                link(nc.scalar.activation(junk[:, :], x[:, t, :], ACT.Square, scale=D ** -0.5,
                                          accum_out=ssq[:, t:t + 1]))
                root(ssq[:, t:t + 1], lnv[:, t:t + 1], rstd[:, t:t + 1], epst[:, 0:1], rstd_made)

            def turn(s, t):
                bank0 = 0 if s["kind"] == "again" else 4
                for g in (2 * t, 2 * t + 1):
                    half = g % 2
                    act.wait_ge(turned, 4 * s["turn"] + g + 1)
                    nc.scalar.copy(xt_hi[:, 4 * half:4 * half + 4, t * P:(t + 1) * P],
                                   ps[:, bank0 + g, :].rearrange("p (k n) -> p k n", k=4)).then_inc(xt_hi_made, 1)

            def norms(s):
                if s.get("loads") in (FOX, MLSTM):
                    act.wait_ge(zw_landed, 32 * (1 + (s["loads"] == MLSTM)))
                    nc.scalar.copy(zw_hi[:, :, :], zw[:, :, :]).then_inc(zw_split, 1)
                for t in range(T):
                    if s["post"]:
                        post_square(s["post"], t)
                if not s["defer"]:
                    for t in range(T):
                        pre_square(s, t)
                if s["kind"] == "final":
                    return
                for t in range(T):
                    turn(s, t)
                    if s["defer"]:
                        pre_square(s, t)
                if s["defer"]:
                    nc.scalar.preload_act_table_set(SILU_TABLES)
                hi_upto(s["piece"] + RING - 1)

            def ffn(s):
                f, p = s["index"], s["piece"]

                def silu(chunk, banks, waits):
                    for t in range(T):
                        act.wait_ge(*waits[t])
                        nc.scalar.activation(sg[:, t, :], ps[:, banks[t], 0:FC], ACT.Silu,
                                             scale=rstd[:, t:t + 1]).then_inc(silu_made, 1)

                def hidden(chunk):
                    act.wait_ge(ht_turned, f * NC + chunk + 1)
                    nc.scalar.copy(ht_hi[:, :, :], ps[:, HT_BANK, :].rearrange("p (k n) -> p k n", k=2))\
                        .then_inc(ht_hi_made, 1)

                act.wait_ge(rstd_made, T * (s["stat"] + 1))
                silu(0, GU_FIRST, [(gu_tile0, f + 1), (piece_used, p + 2)])
                hi(p + 3)
                hi(p + 4)
                hidden(0)
                hi(p + 5)
                with act.Fori(2, NC) as c:
                    more, more_landed = 3 * (c - 2), 32 * (c - 2)
                    silu(c - 1, (4, 5), [(piece_used, p + 4 + more)] * 2)
                    hi(p + 6, more, more_landed)
                    hi(p + 7, more, more_landed)
                    hidden(c - 1)
                    hi(p + 8, more, more_landed)
                end = p + 3 * NC
                hi_skip(end)
                silu(NC - 1, (4, 5), [(piece_used, end - 2)] * 2)
                nc.scalar.preload_act_table_set(TABLES)
                hi_upto(end)
                hidden(NC - 1)
                hi_upto(end + 1)

            def proj(s):
                m, form, what, b0 = s["mixer"], s["form"], s["what"], half_of(s)
                last = s["piece"] + s["n"] - 1
                if what == "a0":
                    act.wait_ge(conv_turned, 1)
                    nc.scalar.copy(conv_cols[:, :, :],
                                   ps[:, 7, 0:CB * (TAPS + 3)].rearrange("p (b n) -> p b n", b=CB))\
                        .then_inc(conv_ready, 1)
                if what in ("a0", "o0"):
                    nc.scalar.preload_act_table_set(SIGMOID_TABLES)
                if s["n"] == 2:
                    hi_upto(last + RING - 1)
                if s["n"]:
                    act.wait_ge(piece_used, last + 1)
                if form == "feature":
                    blocks = ps[:, b0:b0 + 4, 0:S]
                    if what[0] == "a":
                        at = 2 * int(what[1])
                        nc.scalar.copy(a_in[:, at:at + 2, :], ps[:, b0:b0 + 2, 0:S])
                        done = nc.scalar.activation(a_gate[:, at:at + 2, :], ps[:, b0 + 2:b0 + 4, 0:S],
                                                    ACT.Sigmoid)
                    elif what[0] == "k":
                        at = 4 * int(what[1])
                        done = nc.scalar.copy(kt[:, at:at + 4, :], blocks)
                    elif m == SWA:
                        for odd in range(2):
                            r = slice(64 * odd, 64 * odd + 64)
                            for kv in range(2):
                                first = 2 * odd + kv
                                done = nc.scalar.mul(qz[64 * kv:64 * kv + 64, first:first + 5:4, :],
                                                     ps[r, b0 + 2 * kv:b0 + 2 * kv + 2, 0:S], DH ** -0.5)
                    else:
                        at = 8 * int(what[1])
                        for odd in range(2):
                            r = slice(64 * odd, 64 * odd + 64)
                            done = nc.scalar.mul(qz[r, at + odd:at + 8:2, :], ps[r, b0:b0 + 4, 0:S], DH ** -0.5)
                elif form == "token":
                    at = 512 * int(what[1])
                    if what[0] == "v":
                        done = nc.scalar.copy(vt[:, :, at:at + 512], ps[:, b0:b0 + 2, :])
                    else:
                        done = nc.scalar.activation(o_gate[:, :, at:at + 512], ps[:, b0:b0 + 2, :], ACT.Sigmoid)
                elif form == "both":
                    nc.scalar.copy(kt[:, 0, :], ps[:, b0, 0:S])
                    done = nc.scalar.copy(vt[:, :, 0:P], ps[:, b0 + 2:b0 + 4, 0:P])
                elif form == "gates":
                    act.wait_ge(gates_made, GATES[m] + 1)
                    done = nc.scalar.copy(z[:, :, :], ps[:, b0:b0 + 2, 0:16])
                elif form == "sums":
                    act.wait_ge(gates_made, GATES[m] + 2)
                    done = nc.scalar.copy(c_rows[:, :], ps[:, b0, 0:S])
                done.then_inc(proj_read, 1)
                if what in ("a1", "o1"):
                    nc.scalar.preload_act_table_set(TABLES)
                if form == "gates":
                    act.wait_ge(lf_step, LF_STEPS * (m == MLSTM) + 2)
                    link(nc.scalar.activation(z_exp[:, :, :], z_neg[:, :, :], ACT.Exp))
                    linked()
                    link(nc.scalar.activation(z_ln[:, :, :], z_exp[:, :, :], ACT.Ln, bias=1.0))
                    n_z_ln.append(n_step)
                hi_upto(last + RING)

            def mix(s):
                m = s["mixer"]
                H = HEADS[m]
                for i in range(H + 3):
                    n = HEAD0[m] + i
                    if i < H:
                        bank = i % (2 if m == MLSTM else 4)
                        act.wait_ge(top_made, n + 1)
                        if m == MLSTM:
                            nc.scalar.activation(em[:, n, :], ntop[:, n, :], ACT.Exp)
                        if m == SWA:
                            nc.scalar.activation(em[:, n, :], ntop[:, n, :], ACT.Exp, bias=sinks[:, i:i + 1])
                        for q in range(T):
                            cols = slice(P * q, P * q + P * (q + 1))
                            sums = {} if m == MLSTM else dict(accum_out=mass[:, n, q:q + 1])
                            done = nc.scalar.activation(prob[i % 3][:, cols], ps[:, bank, cols], ACT.Exp,
                                                        bias=ntop[:, n, q:q + 1], **sums)
                        done.then_inc(prob_made, 1)
                    if 0 <= i - 2 < H:
                        act.wait_ge(prob_turned, n - 2 + 1)
                        nc.scalar.copy(prob_t[i % 2][:, :], ps[:, 4 + i % 2, 0:3 * P]).then_inc(prob_t_made, 1)
                    j = i - 3
                    if m != MLSTM and j > 0 and j % 2:
                        act.wait_ge(o_made, n - 3 + 1)
                        nc.scalar.copy(xt_hi[:, O_BLOCK[m] + j // 2, :], ps[:, 6 + (j // 2) % 2, 0:S])\
                            .then_inc(o_hi_made, 1)
                if m == SWA:
                    act.wait_ge(centered, 1)
                    nc.scalar.activation(a_sq, a_in, ACT.Square).then_inc(squared, 1)
                    act.wait_ge(var_made, 1)
                    link(nc.scalar.activation(a_gate[:, 0, :], ps[:, 5, 0:S], ACT.Ln, bias=epst[:, 0:1]))
                    linked()
                    nc.scalar.activation(a_gate[:, 1, :], a_gate[:, 0, :], ACT.Exp, scale=-0.5)\
                        .then_inc(conv_rstd, 1)
                    nc.scalar.preload_act_table_set(SILU_TABLES)
                    act.wait_ge(conv_normed, 1)
                    for b in range(CB):
                        link(nc.scalar.activation(a_sq[:, b, :], a_in[:, b, :], ACT.Silu,
                                                  bias=conv_cols[:, b, TAPS + 2:TAPS + 3],
                                                  scale=conv_cols[:, b, TAPS + 1:TAPS + 2]))
                    linked()
                    nc.scalar.copy(xt_hi[:, 0:CB, :], a_sq).then_inc(conv_hi, 1)
                    nc.scalar.preload_act_table_set(TABLES)
                if m == MLSTM:
                    for t in range(T):
                        if t == 0:
                            act.wait_ge(hs_made, T * H)
                        else:
                            act.wait_ge(hs_sum, 1)
                        linked()
                        link(nc.scalar.activation(junk[:, :], xn[:, t, :], ACT.Square))
                        n_hs_sq.append(n_step)
                        act.wait_ge(hs_sum, t + 1)
                        link(nc.scalar.activation(hs_ms[:, t, :], hs_ms[:, t, :], ACT.Ln, bias=epst[:, 0:1],
                                                  scale=1.0 / P))
                        linked()
                        nc.scalar.activation(hs_r[:, t, :], hs_ms[:, t, :], ACT.Exp, scale=-0.5)\
                            .then_inc(hs_rstd, 1)
                    turn(s, 0)
                    turn(s, 1)

            def out_(s):
                hi_upto(s["piece"] + 3 + RING - 1)

            act.dma_start(x[:, :, :], A["x"][0].rearrange("(t p) d -> p t d", p=P)).then_inc(x_landed, 16)
            nc.scalar.preload_act_table_set(TABLES)
            act.wait_ge(consts_made, 4)
            hi_upto(1)
            for s in steps:
                k = s["kind"]
                if k in ("pre", "final"):
                    norms(s)
                elif k == "again":
                    for t in range(T):
                        turn(s, t)
                elif k == "ffn":
                    ffn(s)
                elif k == "proj":
                    proj(s)
                elif k == "mix":
                    mix(s)
                elif k == "out":
                    out_(s)

        @block.vector
        def _(dve):
            n_step = 0

            def link(ins):
                nonlocal n_step
                n_step += 1
                ins.then_inc(dve_step, 1)

            def linked():
                if n_step:
                    dve.wait_ge(dve_step, n_step)

            def lo(p, more=0):
                if p in pool_pieces:
                    return
                slot = p % RING
                dve.wait_ge(hi_made, p + 1 + more)
                nc.vector.tensor_tensor(w_lo[slot][:, :], raw[slot][:, :], w_hi[slot][:, :].bitcast(F32),
                                        ALU.subtract).then_inc(lo_made, 1)

            lo_upto, lo_skip = next_splits(lo)

            def use_gain(s):
                u = s["use"]
                dve.wait_ge(gain_landed[u % 2], 16 * (u // 2 + 1))
                return gain[u % 2]

            def post_tile(s, t):
                for half in range(2):
                    y, at = ps[:, 2 * t + half, :], 4 * s["at"] + 2 * t + half
                    xh = half_cols(x, t, half)
                    if s["g"] is None:
                        if t == 0:
                            dve.wait_ge(y_tile0, s["y"] + 1)
                        else:
                            dve.wait_ge(piece_used, s["piece"])
                        nc.vector.tensor_tensor(xh, y, xh, ALU.add).then_inc(x_added, 1)
                        continue
                    dve.wait_ge(prstd_made, T * s["at_normed"] + t + 1)
                    g = use_gain(s)
                    nc.vector.scalar_tensor_tensor(out=half_cols(xn, t, half), in0=y, scalar=prstd[:, t:t + 1],
                                                   in1=g[:, half * 512:(half + 1) * 512],
                                                   op0=ALU.mult, op1=ALU.mult).then_inc(normed_y, 1)
                if s["g"] is not None:
                    for half in range(2):
                        dve.wait_ge(normed_y, 4 * s["at_normed"] + 2 * t + half + 1)
                        nc.vector.tensor_tensor(half_cols(x, t, half), half_cols(x, t, half),
                                                half_cols(xn, t, half), ALU.add).then_inc(x_added, 1)

            def pre_tile(s, t):
                g = use_gain(s)
                if s["kind"] != "again":
                    if s["post"]:
                        dve.wait_ge(x_added, 4 * s["post"]["at"] + 2 * t + 2)
                    else:
                        dve.wait_ge(x_landed, 16)
                if s["kind"] != "pre" or not s["defer"]:
                    dve.wait_ge(rstd_made, T * (s["stat"] + 1) - (T - 1 - t if s["kind"] != "again" else 0))
                for half in range(2):
                    gh = g[:, half * 512:(half + 1) * 512]
                    if s.get("defer"):
                        ins = nc.vector.tensor_tensor(half_cols(xn, t, half), half_cols(x, t, half), gh, ALU.mult)
                    else:
                        ins = nc.vector.scalar_tensor_tensor(
                            out=half_cols(xn, t, half), in0=half_cols(x, t, half), scalar=rstd[:, t:t + 1],
                            in1=gh, op0=ALU.mult, op1=ALU.mult)
                    ins.then_inc(xn_made, 1)

            def turn(s, t):
                bank0 = 0 if s["kind"] == "again" else 4
                for g in (2 * t, 2 * t + 1):
                    half = g % 2
                    dve.wait_ge(xt_hi_made, 4 * s["turn"] + g + 1)
                    place = (slice(None), slice(4 * half, 4 * half + 4), slice(t * P, (t + 1) * P))
                    nc.vector.tensor_tensor(xt_lo[place], ps[:, bank0 + g, :].rearrange("p (k n) -> p k n", k=4),
                                            xt_hi[place].bitcast(F32), ALU.subtract).then_inc(xt_lo_made, 1)

            def norms(s):
                if s.get("loads") in (FOX, MLSTM):
                    dve.wait_ge(zw_split, 2 * (s["loads"] == MLSTM) + 1)
                    nc.vector.tensor_tensor(zw_lo[:, :, :], zw[:, :, :], zw_hi[:, :, :].bitcast(F32),
                                            ALU.subtract).then_inc(zw_split, 1)
                if s["kind"] == "pre" and s["defer"]:
                    for t in range(T):
                        if s["post"]:
                            post_tile(s["post"], t)
                        pre_tile(s, t)
                        turn(s, t)
                    lo_upto(s["piece"] + RING - 1)
                    return
                for t in range(T):
                    post_tile(s["post"], t)
                for t in range(T):
                    pre_tile(s, t)
                if s["kind"] == "final":
                    return
                for t in range(T):
                    turn(s, t)
                again = steps[steps.index(s) + 5]
                if again["kind"] == "again":
                    dve.wait_ge(turned, 4 * (s["turn"] + 1))
                    for t in range(T):
                        pre_tile(again, t)
                lo_upto(s["piece"] + RING - 1)

            def ffn(s):
                f, p = s["index"], s["piece"]

                def hidden(banks, at):
                    for t in range(T):
                        dve.wait_ge(silu_made, at + t + 1)
                        nc.vector.scalar_tensor_tensor(out=hid[:, t, :], in0=ps[:, banks[t], FC:2 * FC],
                                                       scalar=rstd[:, t:t + 1], in1=sg[:, t, :],
                                                       op0=ALU.mult, op1=ALU.mult).then_inc(hid_made, 1)

                def rest(chunk):
                    dve.wait_ge(ht_hi_made, f * NC + chunk + 1)
                    nc.vector.tensor_tensor(ht_lo[:, :, :], ps[:, HT_BANK, :].rearrange("p (k n) -> p k n", k=2),
                                            ht_hi[:, :, :].bitcast(F32), ALU.subtract).then_inc(ht_lo_made, 1)

                hidden(GU_FIRST, T * f * NC)
                lo(p + 3)
                lo(p + 4)
                rest(0)
                lo(p + 5)
                with dve.Fori(2, NC) as c:
                    more = 3 * (c - 2)
                    hidden((4, 5), T * (f * NC - 1) + T * c)
                    lo(p + 6 , more)
                    lo(p + 7 , more)
                    rest(c - 1)
                    lo(p + 8 , more)
                end = p + 3 * NC
                lo_skip(end)
                hidden((4, 5), T * (f * NC + NC - 1))
                lo_upto(end)
                rest(NC - 1)
                lo_upto(end + 1)

            def taps(group, first, last):
                n0, b0 = 2 * TAPS * group, 2 * group
                if first == 0:
                    for b in range(2):
                        nc.vector.tensor_scalar(acc[:, b0 + b, :], a_pad[:, b0 + b, 0:S],
                                                conv_cols[:, b0 + b, 0:1], conv_cols[:, b0 + b, TAPS:TAPS + 1],
                                                ALU.mult, ALU.add).then_inc(conv_made, 1)
                    first = 1
                with dve.Fori(first, last) as j:
                    for b in range(2):
                        dve.wait_ge(conv_made, n0 + 2 * j + b - 1)
                        nc.vector.scalar_tensor_tensor(
                            out=acc[:, b0 + b, :], in0=a_pad[:, b0 + b, bass.ds(j, S)],
                            scalar=conv_cols[:, b0 + b, bass.ds(j, 1)], in1=acc[:, b0 + b, :],
                            op0=ALU.mult, op1=ALU.add).then_inc(conv_made, 1)

            def proj(s):
                m, form, what = s["mixer"], s["form"], s["what"]
                last = s["piece"] + s["n"] - 1
                lo_upto(last + RING)
                if what[0] == "a":
                    group = int(what[1])
                    dve.wait_ge(proj_read, s["chunk"] + 1)
                    two = slice(2 * group, 2 * group + 2)
                    nc.vector.tensor_tensor(a_pad[:, two, TAPS - 1:], a_in[:, two, :], a_gate[:, two, :],
                                            ALU.mult).then_inc(a_made, 1)
                    dve.wait_ge(a_made, group + 1)
                    dve.wait_ge(conv_ready, 1)
                    if group == 0:
                        taps(0, 0, 14)
                    else:
                        taps(0, 14, TAPS)
                if what == "kv":
                    taps(1, 0, TAP_HEAD0)
                if form == "gates":
                    base = LF_STEPS * (m == MLSTM)
                    dve.wait_ge(proj_read, s["chunk"] + 1)
                    dve.wait_ge(zw_landed, 32 * (1 + (m == MLSTM)))
                    for t in range(T):
                        ins = nc.vector.tensor_tensor(z[:, t, :], z[:, t, :], z_bias[:, :], ALU.add)
                    ins.then_inc(lf_step, 1)
                    dve.wait_ge(lf_step, base + 1)
                    nc.vector.scalar_tensor_tensor(out=z_neg[:, :, :], in0=z[:, :, :], scalar=-1.0, in1=z[:, :, :],
                                                   op0=ALU.mult, op1=ALU.min).then_inc(lf_step, 1)
                    if m == MLSTM:
                        nc.vector.memset(lf[:, :, 0:32], 0.0).then_inc(lf_step, 1)
                        nc.vector.tensor_copy(ig[:, :, 0:8], z[:, :, 0:8]).then_inc(lf_step, 1)
                    n_f, f0 = (16, 0) if m == FOX else (8, 8)
                    dve.wait_ge(act_step, n_z_ln[m == MLSTM])
                    if m == MLSTM:
                        dve.wait_ge(lf_step, base + 4)
                    nc.vector.scalar_tensor_tensor(out=lf[:, :, 16:16 + n_f], in0=z[:, :, f0:16], scalar=0.0,
                                                   in1=z_ln[:, :, f0:16], op0=ALU.min, op1=ALU.subtract)\
                        .then_inc(lf_step, 1)
                    dve.wait_ge(lf_step, base + 3 + 2 * (m == MLSTM))
                    nc.vector.tensor_scalar(lf[:, :, 0:n_f], lf[:, :, 16:16 + n_f], -1.0, None, ALU.mult)\
                        .then_inc(lf_made, 1)
                if form == "sums":
                    dve.wait_ge(proj_read, s["chunk"] + 1)
                    link(nc.vector.tensor_scalar(aug_q[:, :], c_rows[:, :], row_b[:, 0:1], row_a[:, 0:1],
                                                 ALU.mult, ALU.add))
                    nc.vector.tensor_scalar(aug_k[:, :], c_rows[:, :], row_a[:, 0:1], row_b[:, 0:1],
                                            ALU.mult, ALU.add)
                    linked()
                    for i in range(2):
                        head_bias(m, i)
                if what in ("o0", "o1"):
                    dve.wait_ge(proj_read, s["chunk"] + 1)
                    at = 512 * int(what[1])
                    part = o_gate[:, :, at:at + 512]
                    dve.wait_ge(og_landed, 16)
                    for t in range(T):
                        link(nc.vector.tensor_tensor(part[:, t, :], part[:, t, :], og_gain[:, at:at + 512],
                                                     ALU.mult))

            def head_bias(m, i):
                nc.vector.tensor_scalar(aug_h[i % 2][:, :], aug_q[:, :], head_rows[:, i:i + 1], None,
                                        ALU.mult).then_inc(aug_made, 1)

            def mix(s):
                m = s["mixer"]
                H = HEADS[m]
                for i in range(H + 3):
                    n = HEAD0[m] + i
                    if i < H:
                        bank = i % (2 if m == MLSTM else 4)
                        dve.wait_ge(scores_made, n + 1)
                        nc.vector.reduce_max(top[:, n, 0:1], ps[:, bank, 0:P], AX_X)
                        link(nc.vector.reduce_max(top[:, n, 1:2], ps[:, bank, P:3 * P], AX_X))
                        linked()
                        if m == SWA:
                            ins = nc.vector.tensor_scalar(ntop[:, n, :], top[:, n, :], sinks[:, i:i + 1], -1.0,
                                                          ALU.max, ALU.mult)
                        else:
                            ins = nc.vector.tensor_scalar(ntop[:, n, :], top[:, n, :], -1.0, None, ALU.mult)
                        ins.then_inc(top_made, 1)
                        if m in (FOX, MLSTM) and i + 2 < H:
                            head_bias(m, i + 2)
                    if 0 <= i - 1 < H:
                        normalise(m, i - 1, n - 1)
                    if m == SWA and i < 8:
                        taps(1, TAP_HEAD0 + 2 * i, TAP_HEAD0 + 2 * i + 2)
                    j = i - 3
                    if m == MLSTM and j >= 0:
                        dve.wait_ge(o_made, n - 3 + 1)
                        for t in range(T):
                            nc.vector.tensor_scalar(xn[:, t, j * P:(j + 1) * P],
                                                    ps[:, 6 + j % 2, t * P:(t + 1) * P],
                                                    rmass[:, n - 3, t:t + 1], None, ALU.mult).then_inc(hs_made, 1)
                    elif m != MLSTM and j > 0 and j % 2:
                        dve.wait_ge(o_hi_made, O_PAIR0[m] + j // 2 + 1)
                        kb = O_BLOCK[m] + j // 2
                        nc.vector.tensor_tensor(xt_lo[:, kb, :], ps[:, 6 + (j // 2) % 2, 0:S],
                                                xt_hi[:, kb, :].bitcast(F32), ALU.subtract).then_inc(o_lo_made, 1)
                if m == SWA:
                    conv_end()
                if m == MLSTM:
                    for t in range(T):
                        dve.wait_ge(act_step, n_hs_sq[t])
                        nc.vector.reduce_sum(hs_ms[:, t, :], junk[:, :].rearrange("p (h n) -> p h n", h=8), AX_X)\
                            .then_inc(hs_sum, 1)
                        dve.wait_ge(hs_rstd, t + 1)
                        by_head = xn[:, t, :].rearrange("p (h n) -> p h n", h=8)
                        link(nc.vector.tensor_tensor(by_head, by_head,
                                                     hs_r[:, t, :].unsqueeze(2).to_broadcast([P, 8, P]), ALU.mult))
                        linked()
                        nc.vector.tensor_tensor(xn[:, t, :], xn[:, t, :], o_gate[:, t, :], ALU.mult)\
                            .then_inc(hs_gated, 1)
                    turn(s, 0)
                    turn(s, 1)

            def normalise(m, i, n):
                dve.wait_ge(prob_made, n + 1)
                pr = prob[i % 3]
                if m == MLSTM:
                    for q in range(T):
                        cols = slice(P * q, P * q + P * (q + 1))
                        ins = nc.vector.scalar_tensor_tensor(out=pr[:, cols], in0=ps[:, 2 + i % 2, cols],
                                                             scalar=1.0, in1=pr[:, cols], op0=ALU.mult,
                                                             op1=ALU.mult, accum_out=mass[:, n, q:q + 1])
                    ins.then_inc(prob_normed, 1)
                    dve.wait_ge(prob_normed, n + 1)
                    link(nc.vector.scalar_tensor_tensor(out=mass2[:, n, :], in0=mass[:, n, :], scalar=-1.0,
                                                        in1=mass[:, n, :], op0=ALU.mult, op1=ALU.max))
                    linked()
                    link(nc.vector.tensor_tensor(top[:, n, :], mass2[:, n, :], em[:, n, :], ALU.max))
                    linked()
                    link(nc.vector.reciprocal(rmass[:, n, :], top[:, n, :]))
                    return
                total = mass
                if m == SWA:
                    link(nc.vector.tensor_tensor(mass2[:, n, :], mass[:, n, :], em[:, n, :], ALU.add))
                    linked()
                    total = mass2
                link(nc.vector.reciprocal(rmass[:, n, :], total[:, n, :]))
                linked()
                for q in range(T):
                    cols = slice(P * q, P * q + P * (q + 1))
                    ins = nc.vector.tensor_scalar(pr[:, cols], pr[:, cols], rmass[:, n, q:q + 1], None, ALU.mult)
                ins.then_inc(prob_normed, 1)

            def conv_end():
                taps(1, TAP_HEAD0 + 16, TAPS)
                dve.wait_ge(mean_made, 1)
                nc.vector.tensor_tensor(a_in, acc, ps[:, 4:5, 0:S].to_broadcast([P, CB, S]), ALU.subtract)\
                    .then_inc(centered, 1)
                dve.wait_ge(conv_rstd, 1)
                dve.wait_ge(centered, 1)
                nc.vector.tensor_tensor(a_in, a_in, a_gate[:, 1:2, :].to_broadcast([P, CB, S]), ALU.mult)\
                    .then_inc(conv_normed, 1)
                dve.wait_ge(conv_hi, 1)
                nc.vector.tensor_tensor(xt_lo[:, 0:CB, :], a_sq, xt_hi[:, 0:CB, :].bitcast(F32), ALU.subtract)\
                    .then_inc(conv_lo, 1)

            lo_upto(1)
            for s in steps:
                k = s["kind"]
                if k in ("pre", "final"):
                    if k == "pre" and s["stat"] == 1:
                        dve.wait_ge(consts_made, N_CONST)
                    norms(s)
                elif k == "again":
                    turn(s, 0)
                    turn(s, 1)
                elif k == "ffn":
                    ffn(s)
                elif k == "proj":
                    proj(s)
                elif k == "mix":
                    mix(s)
                elif k == "out":
                    lo_upto(s["piece"] + 3 + RING - 1)

        @block.tensor
        def _(pe):
            def three(o, xh, xl, wh, wl, start, stop, stands="x"):
                for n, (a, b) in enumerate(((xh, wh), (xl, wh), (xh, wl))):
                    if stands == "w":
                        a, b = b, a
                    ins = nc.tensor.matmul(o, a, b, start=start and n == 0, stop=stop and n == 2)
                return ins

            def split(p, more=0):
                made, count = lo_count(p)
                pe.wait_ge(made, count + more)

            def x_blocks(kb, t):
                place = (slice(None), kb, slice(t * P, (t + 1) * P))
                return xt_hi[place], xt_lo[place]

            def turn(s, t):
                bank0 = 0 if s["kind"] == "again" else 4
                for g in (2 * t, 2 * t + 1):
                    half = g % 2
                    if s["kind"] == "mix":
                        pe.wait_ge(hs_gated, t + 1)
                    else:
                        pe.wait_ge(xn_made, 4 * s["at"] + g + 1)
                    for k in range(4):
                        c0 = (4 * half + k) * P
                        ins = nc.tensor.transpose(ps[:, bank0 + g, k * P:(k + 1) * P], xn[:, t, c0:c0 + P],
                                                  ident[:, :])
                    ins.then_inc(turned, 1)

            def half_product(o, p, half, t, ends=(0, KB - 1)):
                w = [v[p % RING] for v in (w_hi, w_lo)]
                for k in range(4):
                    kb = 4 * half + k
                    cols = slice(512 * k, 512 * (k + 1))
                    ins = three(o, *x_blocks(kb, t), w[0][:, cols], w[1][:, cols], kb == ends[0], kb == ends[1])
                return ins

            def first_product(s, banks, tile0):
                p, pre = s["piece"], steps[steps.index(s) - 1]
                turn_at = 4 * s["after_turn"]
                pe.wait_ge(xt_lo_made, turn_at + 2)
                split(p)
                half_product(ps[:, banks[0], :], p, 0, 0)
                turn(pre, 1)
                split(p + 1)
                ins = half_product(ps[:, banks[0], :], p + 1, 1, 0)
                if tile0:
                    ins.then_inc(gu_tile0, 1)
                pe.wait_ge(xt_lo_made, turn_at + 4)
                for half in range(2):
                    half_product(ps[:, banks[1], :], p + half, half, 1).then_inc(piece_used, 1)

            def ffn(s):
                f, p = s["index"], s["piece"]

                def gate_up(q, more=0):
                    for half in range(2):
                        slot = (q + half) % RING
                        split(q + half, more)
                        for k in range(4):
                            cols = slice(512 * k, 512 * (k + 1))
                            for t in range(T):
                                ins = three(gu_bank(t), *x_blocks(4 * half + k, t), w_hi[slot][:, cols],
                                            w_lo[slot][:, cols], (half, k) == (0, 0), (half, k) == (1, 3))
                        ins.then_inc(piece_used, 1)
                        yield

                def turn_hidden(chunk):
                    pe.wait_ge(hid_made, T * (f * NC + chunk) + T)
                    for k in range(2):
                        for t in range(T):
                            ins = nc.tensor.transpose(ps[:, HT_BANK, k * S + t * P:k * S + (t + 1) * P],
                                                      hid[:, t, k * P:(k + 1) * P], ident[:, :])
                    ins.then_inc(ht_turned, 1)

                def down(chunk, q, more=0, start=False, stop=False):
                    slot = q % RING
                    pe.wait_ge(ht_lo_made, f * NC + chunk + 1)
                    split(q, more)
                    order = [(k, t) for k in range(2) for t in range(T)]
                    if stop:
                        order.sort(key=lambda kt_: kt_[1])
                    for k, t in order:
                        for n in range(2):
                            cols = slice(k * D + n * 512, k * D + (n + 1) * 512)
                            h = (slice(None), k, slice(t * P, (t + 1) * P))
                            ins = three(ps[:, 2 * t + n, :], ht_hi[h], ht_lo[h], w_hi[slot][:, cols],
                                        w_lo[slot][:, cols], start and k == 0, stop and k == 1)
                        if stop and (k, t) == (1, 0):
                            ins.then_inc(y_tile0, 1)
                    ins.then_inc(piece_used, 1)

                def step(chunk, q, more=0, start=False):
                    pe.wait_ge(hid_made, T * (f * NC + chunk) - start)
                    halves = gate_up(q, more)
                    next(halves)
                    turn_hidden(chunk - 1)
                    next(halves)
                    down(chunk - 1, q + 2, more, start)

                first_product(s, GU_FIRST, True)
                step(1, p + 2, start=True)
                with pe.Fori(2, NC) as c:
                    step(c, p + 5, 3 * (c - 2))
                turn_hidden(NC - 1)
                down(NC - 1, p + 3 * NC - 1, stop=True)

            def proj(s):
                m, form, what, b0, p = s["mixer"], s["form"], s["what"], half_of(s), s["piece"]
                if s["chunk"] >= 2:
                    pe.wait_ge(proj_read, s["chunk"] - 1)
                if what == "v0":
                    first_product(s, (b0, b0 + 1), False)
                    return
                pe.wait_ge(xt_lo_made, 4 * (s["after_turn"] + 1))
                if what == "a0":
                    pe.wait_ge(small_landed, 16 * 5)
                    for b in range(CB):
                        ins = nc.tensor.transpose(ps[:, 7, b * (TAPS + 3):(b + 1) * (TAPS + 3)],
                                                  conv_rows[:, b * P:(b + 1) * P], ident[0:TAPS + 3, 0:TAPS + 3])
                    ins.then_inc(conv_turned, 1)
                if what == "a1":
                    pe.wait_ge(conv_ready, 1)
                if form == "gates":
                    pe.wait_ge(zw_split, 2 * (1 + (m == MLSTM)))
                    for t in range(T):
                        for kb in range(KB):
                            ins = three(ps[:, b0 + t, 0:16], *x_blocks(kb, t), zw_hi[:, kb, :], zw_lo[:, kb, :],
                                        kb == 0, kb == KB - 1)
                    ins.then_inc(gates_made, 1)
                elif form == "sums":
                    pe.wait_ge(lf_made, 1 + (m == MLSTM))
                    last = m != MLSTM
                    for t in range(T):
                        o = ps[:, b0, t * P:(t + 1) * P]
                        nc.tensor.matmul(o, lf[:, t, :], upper[:, :], start=True, stop=last and t == 0)
                        if t == 1:
                            nc.tensor.matmul(o, lf[:, 0, :], ones[:, :], start=False, stop=last)
                        if m == MLSTM:
                            nc.tensor.matmul(o, ig[:, t, :], ident[:, :], start=False, stop=True)
                    nc.tensor.matmul(ps[:, b0 + 1, 0:P], lf[:, 0, :], ones[:, :], start=True, stop=True)\
                        .then_inc(gates_made, 1)
                elif form == "both":
                    split(p)
                    slot = p % RING
                    wh, wl = (w[slot][:, :].rearrange("p (k n) -> p k n", k=KB) for w in (w_hi, w_lo))
                    for kb in range(KB):
                        ends = (kb == 0, kb == KB - 1)
                        three(ps[:, b0, 0:S], xt_hi[:, kb, :], xt_lo[:, kb, :], wh[:, kb, 0:P], wl[:, kb, 0:P],
                              *ends, stands="w")
                        for t in range(T):
                            ins = three(ps[:, b0 + 2 + t, 0:P], *x_blocks(kb, t), wh[:, kb, P:2 * P],
                                        wl[:, kb, P:2 * P], *ends)
                    ins.then_inc(piece_used, 1)
                else:
                    for half in range(2):
                        slot = (p + half) % RING
                        split(p + half)
                        for k in range(4):
                            kb = 4 * half + k
                            ends = (kb == 0, kb == KB - 1)
                            cols = slice(512 * k, 512 * (k + 1))
                            wh, wl = w_hi[slot][:, cols], w_lo[slot][:, cols]
                            if form == "token":
                                for t in range(T):
                                    ins = three(ps[:, b0 + t, :], *x_blocks(kb, t), wh, wl, *ends)
                            else:
                                for b in range(4):
                                    bs = slice(b * P, (b + 1) * P)
                                    ins = three(ps[:, b0 + b, 0:S], xt_hi[:, kb, :], xt_lo[:, kb, :],
                                                wh[:, bs], wl[:, bs], *ends, stands="w")
                        ins.then_inc(piece_used, 1)

            def scores(m, i, n):
                H = HEADS[m]
                bank = i % (2 if m == MLSTM else 4)
                qk_bank = 2 + i % 2 if m == MLSTM else bank
                slot = i if m != SWA else 2 * (i % 4) + i // 4
                kb = {SWA: 0}.get(m, i // 2)
                if m == MLSTM and i >= 2:
                    pe.wait_ge(prob_normed, n - 1)
                elif i >= 4:
                    pe.wait_ge(prob_made, n - 3)
                if m in (FOX, MLSTM):
                    pe.wait_ge(aug_made, HEAD0_AUG[m] + i + 1)
                mm = nc.tensor.matmul
                for q in range(T):
                    qs = slice(q * P, (q + 1) * P)
                    o = ps[:, bank, P * q:P * q + P * (q + 1)]
                    diagonal = ps[:, bank, 2 * P * q:2 * P * q + P]
                    if m == MLSTM:
                        mm(ps[:, qk_bank, P * q:P * q + P * (q + 1)], qz[:, slot, qs], kt[:, kb, 0:P * (q + 1)],
                           start=True, stop=True)
                        mm(o, aug_h[i % 2][:, qs], aug_k[:, 0:P * (q + 1)], start=True, stop=False)
                        ins = mm(diagonal, ident_b[:, :], causal_b[:, :], start=False, stop=True)
                        continue
                    mm(o, qz[:, slot, qs], kt[:, kb, 0:P * (q + 1)], start=True, stop=False)
                    if m == SWA:
                        ins = mm(o, ident_b[:, :], alibi_b[:, i, P * (1 - q):S], start=False, stop=True)
                    elif m == FOX:
                        mm(o, aug_h[i % 2][:, qs], aug_k[:, 0:P * (q + 1)], start=False, stop=False)
                        ins = mm(diagonal, ident_b[:, :], causal_b[:, :], start=False, stop=True)
                    else:
                        mm(diagonal, mx[:, i, 0:P], flip[:, :], start=False, stop=False)
                        if q == 1:
                            mm(ps[:, bank, P:2 * P], mx[:, i, P:S], flip[:, :], start=False, stop=False)
                        ins = mm(diagonal, ident_b[:, :], chunk_b[:, :], start=False, stop=True)
                ins.then_inc(scores_made, 1)

            def mix(s):
                m = s["mixer"]
                H = HEADS[m]
                pe.wait_ge(proj_read, chunks_before(s))
                if m == REL:
                    pe.wait_ge(rel_landed, 16)
                for i in range(H + 3):
                    n = HEAD0[m] + i
                    if i < H:
                        scores(m, i, n)
                    j = i - 3
                    if j >= 0:
                        pe.wait_ge(prob_t_made, n - 3 + 1)
                        seg = lambda g: prob_t[j % 2][:, g * P:(g + 1) * P]
                        if m == MLSTM:
                            if j >= 2:
                                pe.wait_ge(hs_made, T * (j - 1))
                            v = lambda kt_: vt[:, kt_, j * P:(j + 1) * P]
                            bank = ps[:, 6 + j % 2, :]
                            nc.tensor.matmul(bank[:, 0:P], seg(0), v(0), start=True, stop=True)
                            nc.tensor.matmul(bank[:, P:S], seg(1), v(0), start=True, stop=False)
                            ins = nc.tensor.matmul(bank[:, P:S], seg(2), v(1), start=False, stop=True)
                        else:
                            if j >= 4 and j % 2 == 0:
                                pe.wait_ge(o_lo_made, O_PAIR0[m] + j // 2 - 1)
                            c0 = (j // 4 if m == SWA else j) * DH
                            r = slice(64 * (j % 2), 64 * (j % 2) + 64)
                            v = lambda kt_: vt[:, kt_, c0:c0 + DH]
                            bank = ps[r, 6 + (j // 2) % 2, :]
                            nc.tensor.matmul(bank[:, 0:P], v(0), seg(0), start=True, stop=True)
                            nc.tensor.matmul(bank[:, P:S], v(0), seg(1), start=True, stop=False)
                            ins = nc.tensor.matmul(bank[:, P:S], v(1), seg(2), start=False, stop=True)
                        ins.then_inc(o_made, 1)
                    if 0 <= i - 2 < H:
                        k = i - 2
                        pe.wait_ge(prob_normed, n - 2 + 1)
                        if k >= 2:
                            pe.wait_ge(prob_t_made, n - 2 - 1)
                        for g in range(3):
                            ins = nc.tensor.transpose(ps[:, 4 + k % 2, g * P:(g + 1) * P],
                                                      prob[k % 3][:, g * P:(g + 1) * P], ident[:, :])
                        ins.then_inc(prob_turned, 1)
                    if m in (FOX, REL) and i in (H, H + 1):
                        pe.wait_ge(prob_made, HEAD0[m] + i - 1)
                        pe.wait_ge(o_lo_made, O_PAIR0[m] + 4)
                        out_piece(s["out"], i - H)
                if m == SWA:
                    pe.wait_ge(o_lo_made, O_PAIR0[m] + HEADS[m] // 2)
                    out_piece(s["out"], 0)
                    out_piece(s["out"], 1)
                    for made, bank, src, first in ((mean_made, 4, acc, conv_made), (var_made, 5, a_sq, squared)):
                        pe.wait_ge(first, CB * TAPS if first is conv_made else 1)
                        for b in range(CB):
                            ins = nc.tensor.matmul(ps[:, bank, 0:S], mean_w[:, :], src[:, b, :], start=b == 0,
                                                   stop=b == CB - 1)
                        ins.then_inc(made, 1)
                if m == MLSTM:
                    turn(s, 0)
                    turn(s, 1)

            def out_piece(s, n):
                q, half = s["piece"] + n, out_half(s, n)
                ends = (4 * out_half(s, 0), 4 * out_half(s, 2) + 3)
                split(q)
                banks = [ps[:, 2 * t + n % 2, :] for t in range(T)]
                if n == 3:
                    half_product(banks[0], q, half, 0, ends).then_inc(y_tile0, 1)
                    ins = half_product(banks[1], q, half, 1, ends)
                else:
                    for k in range(4):
                        kb = 4 * half + k
                        cols = slice(512 * k, 512 * (k + 1))
                        for t in range(T):
                            ins = three(banks[t], *x_blocks(kb, t), w_hi[q % RING][:, cols],
                                        w_lo[q % RING][:, cols], kb == ends[0], kb == ends[1])
                ins.then_inc(piece_used, 1)

            def out_(s):
                m = s["mixer"]
                if m == MLSTM:
                    pe.wait_ge(xt_lo_made, 4 * (s["after_turn"] + 1))
                    out_piece(s, 0)
                    out_piece(s, 1)
                elif m == SWA:
                    pe.wait_ge(conv_lo, 1)
                else:
                    pe.wait_ge(o_lo_made, O_PAIR0[m] + HEADS[m] // 2)
                out_piece(s, 2)
                out_piece(s, 3)

            pe.wait_ge(consts_made, 2)
            for s in steps:
                k = s["kind"]
                if k == "pre":
                    turn(s, 0)
                    if steps[steps.index(s) + 1].get("mixer") == SWA:
                        turn(s, 1)
                elif k == "again":
                    pe.wait_ge(proj_read, chunks_before(s) - 1)
                    turn(s, 0)
                    turn(s, 1)
                elif k == "ffn":
                    ffn(s)
                elif k == "proj":
                    proj(s)
                elif k == "mix":
                    pe.wait_ge(consts_made, N_CONST)
                    mix(s)
                elif k == "out":
                    out_(s)


_INS = ["x", "norm_g", "ffn_w_gate", "ffn_w_up", "ffn_w_down", "ab_w_in", "conv_w", "conv_b",
        "conv_ln_g", "conv_ln_b", "swa_sinks", "ab_w_out", "fox_w_in", "fox_b_f", "fox_w_out",
        "a_w_in_2", "a_b_gate_2", "a_g_head_2", "a_w_out_2", "b_w_q_2", "b_rel_bias_2", "b_w_o_2",
        "kv_norm_g_2", "w_kv_2", "norm_mix_g_2", "norm_ffn_g_2", "ffn_w_gate_2", "ffn_w_up_2",
        "ffn_w_down_2", "final_norm_g_2"]


def kernel(**inputs):
    import numpy as _np
    import concourse.bacc as _bacc
    from concourse.bass_utils import run_bass_kernel_spmd as _run

    nc = _bacc.Bacc("TRN2", target_bir_lowering=False, num_devices=1)
    arrays, args = {}, {}
    for name in _INS:
        a = _np.ascontiguousarray(inputs[name])
        arrays[f"in_{name}_dram"] = a
        args[name] = nc.dram_tensor(f"in_{name}_dram", a.shape, mybir.dt.from_np(a.dtype),
                                    kind="ExternalInput").ap()
    out = nc.dram_tensor("out_0_dram", (1, S, D), F32, kind="ExternalOutput").ap()
    program(nc, args, out)
    r = _run(nc, [arrays], core_ids=[0])
    return r.results[0]["out_0_dram"]
```

```python
from contextlib import ExitStack

import concourse.bass as bass
from concourse import mybir

F32 = mybir.dt.float32
F32R = mybir.dt.float32r
BF16 = mybir.dt.bfloat16
ALU = mybir.AluOpType
ACT = mybir.ActivationFunctionType
AX_X = mybir.AxisListType.X

P = 128
S = 256
T = S // P
D = 1024
KB = D // P
FF = 2816
FC = 256
NC = FF // FC
PIECE = 2048
RING = 3
CH = 512
CB = CH // P
TAPS = 31
EPS = 1e-6
NEG = -1e30
DH = 64
N_REL = 513
TABLES = "natural_log_exp_and_others"
SILU_TABLES = "silu_and_others"
SIGMOID_TABLES = "sigmoid_and_others"

SWA, FOX, MLSTM, REL = range(4)
HEADS = {SWA: 8, FOX: 16, MLSTM: 8, REL: 16}
HEAD0 = {SWA: 0, FOX: 8, MLSTM: 24, REL: 32}
HEAD0_AUG = {FOX: 0, MLSTM: 16}
O_PAIR0 = {SWA: 0, FOX: 4, REL: 12}
O_BLOCK = {SWA: 4, FOX: 0, REL: 0}
GATES = {FOX: 0, MLSTM: 2}
LF_STEPS = 4
MAX_REL_1 = 256
N_CONST = 47
N_ONES = 5
TAPS_AT = (5, 0, 1, 2, 2, 2, 2, 2, 2, 2, 2, 2)


def plan():
    steps, piece = [], 0

    def add(kind, n_pieces=0, **more):
        nonlocal piece
        steps.append(dict(kind=kind, piece=piece, n=n_pieces, **more))
        piece += n_pieces

    def ffn(index, pre_g, post_g, block):
        add("pre", g=pre_g)
        add("ffn", 2 * NC + NC, index=index, block=block)
        add("post", g=post_g, scale=0.5)

    def mixer(kind, chunks, pre_g, post_g):
        add("pre", g=pre_g)
        for form, what, n in chunks:
            if form == "again":
                add("again", g=what)
            else:
                add("proj", n, mixer=kind, form=form, what=what)
        add("mix", mixer=kind)
        add("out", 4, mixer=kind)
        add("post", g=post_g, scale=1.0)

    ffn(0, ("norm_g", 0, 0), ("norm_g", 0, 1), 1)
    mixer(SWA, [("feature", "a0", 2), ("feature", "a1", 2), ("feature", "q0", 2), ("both", "kv", 1)],
          ("norm_g", 0, 2), ("norm_g", 0, 3))
    ffn(1, ("norm_g", 0, 4), ("norm_g", 0, 5), 1)
    ffn(2, ("norm_g", 1, 0), ("norm_g", 1, 1), 1)
    mixer(FOX, [("token", "v0", 2), ("gates", "z", 0), ("token", "v1", 2), ("sums", "c", 0),
                ("feature", "k0", 2), ("feature", "k1", 2), ("feature", "q0", 2), ("feature", "q1", 2)],
          ("norm_g", 1, 2), ("norm_g", 1, 3))
    ffn(3, ("norm_g", 1, 4), ("norm_g", 1, 5), 1)
    mixer(MLSTM, [("token", "v0", 2), ("gates", "z", 0), ("token", "v1", 2), ("sums", "c", 0),
                  ("feature", "k0", 2), ("feature", "q0", 2), ("token", "o0", 2), ("token", "o1", 2)],
          ("norm_mix_g_2", 0), None)
    ffn(4, ("norm_ffn_g_2", 0), None, 2)
    mixer(REL, [("token", "v0", 2), ("token", "v1", 2), ("feature", "k0", 2), ("feature", "k1", 2),
                ("again", ("norm_mix_g_2", 1), 0), ("feature", "q0", 2), ("feature", "q1", 2)],
          ("kv_norm_g_2",), None)
    ffn(5, ("norm_ffn_g_2", 1), None, 2)
    add("final", g=("final_norm_g_2",))
    for n, s in enumerate(x for x in steps if x["kind"] == "proj"):
        s["chunk"] = n
    for u, s in enumerate(x for x in steps if x.get("g") is not None):
        s["use"] = u
    for n, s in enumerate(x for x in steps if x["kind"] in ("pre", "again", "final")):
        s["at"] = n
    for n, s in enumerate(x for x in steps if x["kind"] in ("pre", "final")):
        s["stat"] = n
    for n, s in enumerate(x for x in steps if x["kind"] == "post"):
        s["at"] = n
    for n, s in enumerate(x for x in steps if x["kind"] == "post" and x["g"] is not None):
        s["at_normed"] = n
    for n, s in enumerate(x for x in steps if x["kind"] in ("ffn", "out")):
        s["y"] = n
    turns = 0
    for n, s in enumerate(steps):
        if s["kind"] in ("pre", "again") or (s["kind"] == "mix" and s["mixer"] == MLSTM):
            s["turn"] = turns
            turns += 1
        elif s["kind"] in ("ffn", "proj", "out"):
            s["after_turn"] = turns - 1
        if s["kind"] in ("pre", "final"):
            s["post"] = steps[n - 1] if n else None
            s["defer"] = steps[n + 1]["kind"] == "ffn" if s["kind"] == "pre" else False
        if s["kind"] == "mix":
            s["out"] = steps[n + 1]
        if s["kind"] == "proj" and steps[n - 1]["kind"] == "pre":
            s["first"] = True
            if s["mixer"] != SWA:
                steps[n - 1]["loads"] = s["mixer"]
        if s["kind"] == "post":
            s["y"] = steps[n - 1]["y"]
        if s["kind"] == "ffn":
            s["stat"] = steps[n - 1]["stat"]
        if s["kind"] == "again":
            s["stat"] = steps[n - 5]["stat"]
    return steps, piece


def program(nc, A, out):
    steps, n_pieces = plan()
    gained = [s for s in steps if s.get("g") is not None]
    n_pre = sum(1 for s in steps if s["kind"] in ("pre", "again"))
    pool_pieces = sorted({p for s in steps if s.get("mixer") == SWA for p in range(s["piece"], s["piece"] + s["n"])}
                         | {s["piece"] + 1 for s in steps if s["kind"] == "pre" and s["post"]})

    with ExitStack() as ctx:
        def sb(name, shape, dt=F32):
            return ctx.enter_context(nc.sbuf_tensor(name, shape, dt))

        def sem(name):
            return ctx.enter_context(nc.semaphore(name))

        raw = [sb(f"raw{i}", [P, PIECE]) for i in range(RING)]
        w_hi = [sb(f"w_hi{i}", [P, PIECE], F32R) for i in range(RING)]
        w_lo = [sb(f"w_lo{i}", [P, PIECE], F32R) for i in range(RING)]
        x = sb("x_res", [P, T, D])
        xn = sb("xn", [P, T, D])
        junk = sb("junk", [P, D])
        xt = sb("xt", [P, KB, 2 * S], F32R)
        xt_hi, xt_lo = xt[:, :, 0:S], xt[:, :, S:2 * S]
        gain = [sb(f"gain{i}", [P, D]) for i in range(2)]
        ssq = sb("ssq", [P, T])
        lnv = sb("lnv", [P, T])
        rstd = sb("rstd", [P, T])
        pssq = sb("pssq", [P, T])
        plnv = sb("plnv", [P, T])
        prstd = sb("prstd", [P, T])
        epst = sb("epst", [P, 1])
        eps4t = sb("eps4t", [P, 1])
        shared = sb("shared", [P, 5 * 3 * P])
        sg, hid = (shared[:, i * T * FC:(i + 1) * T * FC].rearrange("p (t n) -> p t n", t=T)
                   for i in range(2))
        gu_part = xn[:, 0, :].rearrange("p (b n) -> p b n", b=4)
        r_diag = shared[:, 2 * T * FC:2 * T * FC + S].rearrange("p (t n) -> p t n", t=T)
        ht_hi = [sb(f"ht_hi{i}", [P, 2, S], F32R) for i in range(2)]
        ht_lo = [sb(f"ht_lo{i}", [P, 2, S], F32R) for i in range(2)]
        r_row = sb("r_row", [P, S])
        ident = sb("ident", [P, P])
        ones = sb("ones", [P, P])
        upper = sb("upper", [P, P])
        flip = sb("flip", [P, P])
        mean_w = sb("mean_w", [P, P])
        ident_b = sb("ident_b", [P, P], BF16)
        causal_b = sb("causal_b", [P, P], BF16)
        chunk_b = sb("chunk_b", [P, P], BF16)
        dist = sb("dist", [P, S])
        alibi_b = sb("alibi_b", [P, 8, S], BF16)
        head_rows = sb("head_rows", [P, 16])
        row_a = sb("row_a", [P, 1])
        row_b = sb("row_b", [P, 1])
        qz = sb("qz", [P, 16, S])
        kt = sb("kt", [P, 8, S])
        vt = sb("vt", [P, T, D])
        mx = sb("mx", [P, 16, S])
        a_in = mx[:, 0:4, :]
        a_gate = mx[:, 4:8, :]
        acc = mx[:, 8:12, :]
        a_sq = mx[:, 12:16, :]
        a_pad = sb("a_pad", [P, CB, TAPS - 1 + S])
        conv_rows = sb("conv_rows", [TAPS + 3, CH])
        conv_cols = sb("conv_cols", [P, CB, TAPS + 3])
        o_gate = mx[:, 0:8, :].rearrange("p a b -> p (a b)").rearrange("p (t n) -> p t n", t=T)
        og_gain = kt[:, 4:8, :].rearrange("p a b -> p (a b)")
        zw = sb("zw", [P, KB, 16])
        zw_hi = sb("zw_hi", [P, KB, 16], F32R)
        zw_lo = sb("zw_lo", [P, KB, 16], F32R)
        z_bias = sb("z_bias", [P, 16])
        z = sb("z", [P, T, 16])
        z_neg = sb("z_neg", [P, T, 16])
        z_exp = sb("z_exp", [P, T, 16])
        z_ln = sb("z_ln", [P, T, 16])
        lf = sb("lf", [P, T, P])
        ig = sb("ig", [P, T, P])
        c_rows = sb("c_rows", [P, S])
        c_part = sb("c_part", [P, S], BF16)
        c_parts = sb("c_parts", [P, S], BF16)
        aug_q = sb("aug_q", [P, S], BF16)
        aug_k = sb("aug_k", [P, S], BF16)
        aug_h = [sb(f"aug_h{i}", [P, S], BF16) for i in range(2)]
        sinks = sb("sinks", [P, 8])
        prob = [shared[:, i * 3 * P:(i + 1) * 3 * P] for i in range(3)]
        prob_t = [shared[:, i * 3 * P:(i + 1) * 3 * P] for i in range(3, 5)]
        top = sb("top", [P, 48, T])
        ntop = sb("ntop", [P, 48, T])
        mass = sb("mass", [P, 48, T])
        mass2 = sb("mass2", [P, 48, T])
        em = sb("em", [P, 48, T])
        rmass = sb("rmass", [P, 48, T])
        hs_ms = sb("hs_ms", [P, T, 8])
        hs_r = sb("hs_r", [P, T, 8])

        ps = ctx.enter_context(nc.psum_tensor("ps", [P, 8, 512], F32))
        y_bank = lambda t: ps[:, 2 * t:2 * t + 2, :]
        GU_BANKS = {0: (4, 6), 1: (5, 7)}
        GU_LAST, GU_LOOP = (4, 5), 4
        HT_BANK, R_BANK = 3, 2

        def half_cols(v, t, half):
            return v[:, t, half * 512:(half + 1) * 512]

        raw_landed = [sem(f"raw_landed{i}") for i in range(RING)]
        hi_made = sem("hi_made")
        lo_made = sem("lo_made")
        piece_used = sem("piece_used")
        x_landed = [sem(f"x_landed{t}") for t in range(T)]
        small_landed = sem("small_landed")
        gain_landed = [sem(f"gain_landed{i}") for i in range(2)]
        rel_landed = sem("rel_landed")
        zw_landed = sem("zw_landed")
        og_landed = sem("og_landed")
        consts_made = sem("consts_made")
        dve_step = sem("dve_step")
        act_step = sem("act_step")
        rstd_made = sem("rstd_made")
        xn_made = sem("xn_made")
        prstd_made = sem("prstd_made")
        normed_y = sem("normed_y")
        x_added = sem("x_added")
        turned = sem("turned")
        xt_hi_made = sem("xt_hi_made")
        xt_lo_made = sem("xt_lo_made")
        gu_tile0 = sem("gu_tile0")
        gu_copied = sem("gu_copied")
        gu_summed = sem("gu_summed")
        gate_scaled = sem("gate_scaled")
        up_scaled = sem("up_scaled")
        silu_made = sem("silu_made")
        hid_made = sem("hid_made")
        r_diag_made = sem("r_diag_made")
        r_row_turned = sem("r_row_turned")
        r_row_made = sem("r_row_made")
        y_tile0 = sem("y_tile0")
        lo_pool = sem("lo_pool")
        ht_turned = sem("ht_turned")
        ht_hi_made = sem("ht_hi_made")
        ht_lo_made = sem("ht_lo_made")
        gates_made = sem("gates_made")
        proj_read = sem("proj_read")
        lf_made = sem("lf_made")
        aug_made = sem("aug_made")
        zw_split = sem("zw_split")
        lf_step = sem("lf_step")
        conv_turned = sem("conv_turned")
        a_made = sem("a_made")
        conv_ready = sem("conv_ready")
        conv_made = sem("conv_made")
        mean_made = sem("mean_made")
        centered = sem("centered")
        squared = sem("squared")
        var_made = sem("var_made")
        conv_rstd = sem("conv_rstd")
        conv_normed = sem("conv_normed")
        conv_hi = sem("conv_hi")
        conv_lo = sem("conv_lo")
        scores_made = sem("scores_made")
        top_made = sem("top_made")
        prob_made = sem("prob_made")
        prob_normed = sem("prob_normed")
        rmass_made = sem("rmass_made")
        prob_turned = sem("prob_turned")
        prob_t_made = sem("prob_t_made")
        o_made = sem("o_made")
        o_hi_made = sem("o_hi_made")
        o_lo_made = sem("o_lo_made")
        hs_made = sem("hs_made")
        hs_sq = sem("hs_sq")
        hs_gated = sem("hs_gated")
        hs_rstd = sem("hs_rstd")
        stored = sem("stored")

        def rows(w, k0, n, c0, width):
            return w[k0:k0 + n * P, bass.ds(c0, width)].rearrange("(k p) c -> p k c", p=P)

        def ffn_weights(s):
            i = s["index"]
            if s["block"] == 1:
                return [A[n][i // 2, i % 2] for n in ("ffn_w_gate", "ffn_w_up", "ffn_w_down")]
            return [A[n][i - 4] for n in ("ffn_w_gate_2", "ffn_w_up_2", "ffn_w_down_2")]

        IN_W = {SWA: A["ab_w_in"][0], FOX: A["fox_w_in"][0], MLSTM: A["a_w_in_2"][0]}
        OUT_W = {SWA: A["ab_w_out"][0], FOX: A["fox_w_out"][0], MLSTM: A["a_w_out_2"][0],
                 REL: A["b_w_o_2"][0]}
        IN_COL = {(SWA, "a"): 0, (SWA, "q"): 2 * CH, (SWA, "kv"): 3 * CH,
                  (FOX, "q"): 0, (FOX, "k"): D, (FOX, "v"): 2 * D, (FOX, "z"): 3 * D,
                  (MLSTM, "q"): 0, (MLSTM, "k"): 512, (MLSTM, "v"): 1024, (MLSTM, "o"): 2048,
                  (MLSTM, "z"): 3072, (REL, "k"): 0, (REL, "v"): D, (REL, "q"): 0}

        def proj_source(s):
            m, what = s["mixer"], s["what"]
            if what in ("kv", "z"):
                return IN_W[m], IN_COL[m, what]
            part, at = what[0], int(what[1])
            w = (A["w_kv_2"] if part in "kv" else A["b_w_q_2"][0]) if m == REL else IN_W[m]
            return w, IN_COL[m, part] + (256 if part == "a" else 512) * at


        def lo_count(p):
            if p in pool_pieces:
                return lo_pool, pool_pieces.index(p) + 1
            return lo_made, p + 1 - sum(1 for q in pool_pieces if q < p)

        def next_splits(make):
            state = [0]

            def upto(last):
                while state[0] <= min(last, n_pieces - 1):
                    make(state[0])
                    state[0] += 1

            def skip_to(p):
                state[0] = p
            return upto, skip_to

        def landed(p):
            return 32 * (p // RING + 1)

        def chunks_before(s):
            return sum(1 for x in steps[:steps.index(s)] if x["kind"] == "proj")

        def out_half(s, n):
            return (n // 2) ^ (s["mixer"] == SWA)

        def half_of(s):
            return 4 * (s["chunk"] % 2)

        n_z_ln = []

        def group_place(s, g):
            if s["kind"] == "mix":
                return g % 2, g // 2, g + 2 * (g >= 2)
            return g // 2, g % 2, g + 4 * (s["kind"] != "again")

        block = ctx.enter_context(nc.Block())

        @block.sync
        def _(sp):
            def piece(p, pairs, more=0):
                slot = p % RING
                if p >= RING or not isinstance(more, int):
                    split_sem, count = lo_count(p - RING)
                    sp.wait_ge(split_sem, count + more)
                for dst, src in pairs(raw[slot]):
                    sp.dma_start(dst, src).then_inc(raw_landed[slot], 16)

            def gate_up(wg, wu, c, half):
                def pairs(r):
                    v = r[:, :].rearrange("p (k n) -> p k n", k=4)
                    return [(v[:, :, 0:FC], rows(wg, half * 512, 4, c * FC, FC)),
                            (v[:, :, FC:2 * FC], rows(wu, half * 512, 4, c * FC, FC))]
                return pairs

            def down(wd, c):
                def pairs(r):
                    v = r[:, :].rearrange("p (k n) -> p k n", k=2)
                    return [(v[:, k, :], wd[bass.ds(c * FC + k * P, P), :]) for k in range(2)]
                return pairs

            def columns(w, c0, half):
                def pairs(r):
                    v = r[:, :].rearrange("p (k n) -> p k n", k=4)
                    return [(v[:, 2 * k:2 * k + 2, :], rows(w, half * 512 + 256 * k, 2, c0, 512))
                            for k in range(2)]
                return pairs

            def narrow(w, c0):
                def pairs(r):
                    v = r[:, :].rearrange("p (k n) -> p k n", k=8)
                    return [(v[:, 4 * k:4 * k + 4, :], rows(w, 512 * k, 4, c0, 256)) for k in range(2)]
                return pairs

            for s in steps:
                p = s["piece"]
                if s["kind"] == "ffn":
                    wg, wu, wd = ffn_weights(s)
                    piece(p, gate_up(wg, wu, 0, 0))
                    if s["index"] == 0:
                        sp.dma_start(x[:, 1, :], A["x"][0, P:S, :]).then_inc(x_landed[1], 16)
                    piece(p + 1, gate_up(wg, wu, 0, 1))

                    def chunk(c, q, more=0):
                        piece(q, gate_up(wg, wu, c, 0), more)
                        piece(q + 1, gate_up(wg, wu, c, 1), more)
                        piece(q + 2, down(wd, c - 1), more)

                    chunk(1, p + 2)
                    with sp.Fori(2, NC) as c:
                        chunk(c, p + 5, 3 * (c - 2))
                    piece(p + 3 * NC - 1, down(wd, NC - 1))
                elif s["kind"] == "proj" and s["n"]:
                    w, c0 = proj_source(s)
                    if s["form"] == "both":
                        piece(p, narrow(w, c0))
                    elif s["what"][0] == "a":
                        for half in range(2):
                            piece(p + half, gate_up(w[:, 0:CH], w[:, CH:2 * CH], int(s["what"][1]), half))
                    else:
                        for half in range(2):
                            piece(p + half, columns(w, c0, half))
                elif s["kind"] == "out":
                    for n in range(4):
                        piece(p + n, columns(OUT_W[s["mixer"]], 512 * (n % 2), out_half(s, n)))
                elif s["kind"] == "final":
                    for t in range(T):
                        sp.wait_ge(xn_made, 4 * n_pre + 2 * t + 2)
                        sp.dma_start(out[0, t * P:(t + 1) * P, :], xn[:, t, :]).then_inc(stored, 16)
            sp.wait_ge(stored, 16 * T)

        @block.gpsimd
        def _(pool):
            def spread(v, n=P):
                return v.partition_broadcast(n)

            def gate_columns(m):
                pool.dma_start(zw[:, :, :], rows(IN_W[m], 0, KB, IN_COL[m, "z"], 16)).then_inc(zw_landed, 16)
                bias = A["fox_b_f"][0] if m == FOX else A["a_b_gate_2"][0]
                pool.dma_start(z_bias[:, :], spread(bias)).then_inc(zw_landed, 16)

            n_const = 0

            def const(ins):
                nonlocal n_const
                n_const += 1
                ins.then_inc(consts_made, 1)

            def select(m, pattern, base, mult, fill, op=ALU.not_equal):
                pool.wait_ge(consts_made, n_const)
                const(nc.gpsimd.affine_select(out=m, in_=m, compare_op=op, fill=fill, base=base,
                                              pattern=pattern, channel_multiplier=mult))

            const(nc.gpsimd.memset(ident[:, :], 0.0))
            select(ident[:, :], [[-1, P]], 0, 1, 1.0)
            const(nc.gpsimd.memset(epst[:, :], EPS))
            const(nc.gpsimd.memset(eps4t[:, :], 4 * EPS))

            def gain_load(u):
                s = gained[u]
                if u >= 2:
                    last = gained[u - 2]
                    if last["kind"] == "post":
                        pool.wait_ge(normed_y, 4 * (last["at_normed"] + 1))
                    else:
                        pool.wait_ge(xn_made, 4 * (last["at"] + 1))
                name, *at = s["g"]
                v = A[name]
                for i in at:
                    v = v[i]
                pool.dma_start(gain[u % 2][:, :], spread(v)).then_inc(gain_landed[u % 2], 16)

            gain_load(0)

            const(nc.gpsimd.memset(ones[:, :], 1.0))
            const(nc.gpsimd.memset(mean_w[:, :], 1.0 / CH))
            const(nc.gpsimd.memset(upper[:, :], 1.0))
            select(upper[:, :], [[1, P]], 0, -1, 0.0, ALU.is_ge)
            const(nc.gpsimd.memset(flip[:, :], 0.0))
            select(flip[:, :], [[1, P]], 1 - P, 1, 1.0)
            const(nc.gpsimd.memset(ident_b[:, :], 0.0))
            select(ident_b[:, :], [[-1, P]], 0, 1, 1.0)
            const(nc.gpsimd.memset(causal_b[:, :], 0.0))
            select(causal_b[:, :], [[-1, P]], 0, 1, NEG, ALU.is_ge)
            const(nc.gpsimd.memset(chunk_b[:, :], 0.0))
            select(chunk_b[:, 64:P], [[0, 64]], -64, 1, NEG, ALU.is_ge)
            const(nc.gpsimd.memset(head_rows[:, :], 0.0))
            for group in range(3):
                select(head_rows[:, :], [[-1, 16]], -32 * group, 1, 1.0)
                select(head_rows[:, :], [[-1, 16]], -32 * group - 16, 1, 1.0)
            const(nc.gpsimd.memset(row_a[:, :], 0.0))
            const(nc.gpsimd.memset(row_b[:, :], 0.0))
            pool.wait_ge(consts_made, n_const)
            const(nc.gpsimd.memset(row_b[0:96, :], 1.0))
            pool.wait_ge(consts_made, n_const)
            for group in range(3):
                const(nc.gpsimd.memset(row_a[32 * group:32 * group + 16, :], 1.0))
                pool.wait_ge(consts_made, n_const)
                const(nc.gpsimd.memset(row_b[32 * group:32 * group + 16, :], 0.0))
                pool.wait_ge(consts_made, n_const)
            const(nc.gpsimd.iota(dist[:, :], pattern=[[-1, S]], base=P, channel_multiplier=1,
                                 allow_small_or_imprecise_dtypes=True))
            for h in range(8):
                pool.wait_ge(consts_made, n_const)
                const(nc.gpsimd.tensor_scalar(alibi_b[:, h, :], dist[:, :], -2.0 ** -(h + 1), None, ALU.mult))
            heads_cols = [[0, 8], [-1, S]]
            select(alibi_b[:, :, :], heads_cols, P, 1, NEG, ALU.is_ge)
            select(alibi_b[:, :, :], [[0, 8], [1, S]], -1, -1, NEG, ALU.is_ge)
            const(nc.gpsimd.memset(qz[:, :, :], 0.0))
            const(nc.gpsimd.memset(lf[:, :, :], 0.0))
            const(nc.gpsimd.memset(ig[:, :, :], 0.0))
            const(nc.gpsimd.memset(a_pad[:, :, :], 0.0))
            assert n_const == N_CONST, n_const

            def lo(p):
                slot = p % RING
                pool.wait_ge(hi_made, p + 1)
                nc.gpsimd.tensor_tensor(w_lo[slot][:, :], raw[slot][:, :], w_hi[slot][:, :].bitcast(F32),
                                        ALU.subtract).then_inc(lo_pool, 1)

            pool.wait_ge(raw_landed[1], 32)
            gain_load(1)
            pool.dma_start(conv_rows[0:TAPS, :], A["conv_w"][0]).then_inc(small_landed, 16)
            for n, name in enumerate(("conv_b", "conv_ln_g", "conv_ln_b")):
                pool.dma_start(conv_rows[TAPS + n:TAPS + n + 1, :], A[name]).then_inc(small_landed, 16)
            pool.dma_start(sinks[:, :], spread(A["swa_sinks"][0])).then_inc(small_landed, 16)
            gate_columns(FOX)
            for u, s in enumerate(gained):
                pre = steps[steps.index(s) + 1] if s["kind"] == "post" else s
                if s["kind"] == "post" or (s["kind"] == "pre" and s["post"] and s["post"]["g"] is None):
                    for p in pool_pieces:
                        if pre["piece"] <= p < pre["piece"] + 2:
                            lo(p)
                if u + 2 < len(gained):
                    ahead = gained[u + 2]
                    if ahead.get("loads") == MLSTM:
                        pool.wait_ge(zw_split, 2)
                        pool.wait_ge(lf_made, 1)
                        gate_columns(MLSTM)
                        pool.wait_ge(x_added, 4 * ahead["post"]["at"])
                        pool.dma_start(og_gain, spread(A["a_g_head_2"][0])).then_inc(og_landed, 16)
                    if ahead.get("loads") == REL:
                        pool.wait_ge(hs_made, T * HEADS[MLSTM])
                        table = A["b_rel_bias_2"]
                        pool.dma_start(mx[:, :, :], bass.AP(table.tensor, table.offset + MAX_REL_1 - (P - 1),
                                                            [[1, P], [N_REL, 16], [1, S]])).then_inc(rel_landed, 16)
                    gain_load(u + 2)
                if s["kind"] == "pre" and steps[steps.index(s) + 1].get("mixer") == SWA:
                    for p in pool_pieces:
                        if s["piece"] + 2 <= p < s["piece"] + 11:
                            lo(p)

        @block.scalar
        def _(act):
            n_step = 0

            def link(ins):
                nonlocal n_step
                n_step += 1
                ins.then_inc(act_step, 1)

            def linked():
                if n_step:
                    act.wait_ge(act_step, n_step)

            def hi(p, more=0, more_landed=0):
                slot = p % RING
                act.wait_ge(raw_landed[slot], landed(p) + more_landed)
                if p >= RING or not isinstance(more, int):
                    act.wait_ge(piece_used, p - RING + 1 + more)
                nc.scalar.copy(w_hi[slot][:, :], raw[slot][:, :]).then_inc(hi_made, 1)

            hi_upto, hi_skip = next_splits(hi)

            def root(src, ln, dst, eps_tile, made):
                linked()
                link(nc.scalar.activation(ln, src, ACT.Ln, bias=eps_tile))
                linked()
                nc.scalar.activation(dst, ln, ACT.Exp, scale=-0.5).then_inc(made, 1)

            def post_square(s, t):
                if s["g"] is None:
                    return
                if t == 0:
                    act.wait_ge(y_tile0, s["y"] + 1)
                else:
                    act.wait_ge(piece_used, s["piece"])
                linked()
                if s["at_normed"]:
                    act.wait_ge(normed_y, 4 * (s["at_normed"] - 1) + 2 * t + 2)
                link(nc.scalar.activation(junk[:, :].rearrange("p (b n) -> p b n", b=2), y_bank(t),
                                          ACT.Square, scale=D ** -0.5 / s["scale"],
                                          accum_out=pssq[:, t:t + 1]))
                eps = epst if s["scale"] == 1.0 else eps4t
                root(pssq[:, t:t + 1], plnv[:, t:t + 1], prstd[:, t:t + 1], eps[:, 0:1], prstd_made)

            def pre_square(s, t):
                if s["post"]:
                    act.wait_ge(x_added, 4 * s["post"]["at"] + 2 * t + 2)
                else:
                    act.wait_ge(x_landed[t], 16)
                linked()
                link(nc.scalar.activation(junk[:, :], x[:, t, :], ACT.Square, scale=D ** -0.5,
                                          accum_out=ssq[:, t:t + 1]))
                root(ssq[:, t:t + 1], lnv[:, t:t + 1], rstd[:, t:t + 1], epst[:, 0:1], rstd_made)

            def turn(s, *groups):
                for g in groups:
                    t, half, bank = group_place(s, g)
                    act.wait_ge(turned, 4 * s["turn"] + g + 1)
                    nc.scalar.copy(xt_hi[:, 4 * half:4 * half + 4, t * P:(t + 1) * P],
                                   ps[:, bank, :].rearrange("p (k n) -> p k n", k=4)).then_inc(xt_hi_made, 1)

            def norms(s):
                if s.get("loads") in (FOX, MLSTM):
                    act.wait_ge(zw_landed, 32 * (1 + (s["loads"] == MLSTM)))
                    nc.scalar.copy(zw_hi[:, :, :], zw[:, :, :]).then_inc(zw_split, 1)
                p, post = s["piece"], s["post"]
                if s["kind"] == "final":
                    for t in range(T):
                        post_square(post, t)
                    for t in range(T):
                        pre_square(s, t)
                elif s["defer"]:
                    if post:
                        post_square(post, 0)
                        hi_upto(p + 1)
                        turn(s, 0)
                        post_square(post, 1)
                        turn(s, 1)
                    else:
                        turn(s, 0, 1)
                        hi_upto(p + 1)
                    pre_square(s, 0)
                    turn(s, 2, 3)
                    hi_upto(p + RING - 1)
                    pre_square(s, 1)
                    nc.scalar.preload_act_table_set(SILU_TABLES)
                elif steps[steps.index(s) + 1]["mixer"] == SWA:
                    post_square(post, 0)
                    hi_upto(p + 1)
                    for t in range(T):
                        if t == 0:
                            post_square(post, 1)
                        pre_square(s, t)
                    turn(s, 0, 1, 2, 3)
                    hi_upto(p + RING - 1)
                else:
                    post_square(post, 0)
                    hi_upto(p + 1)
                    pre_square(s, 0)
                    post_square(post, 1)
                    turn(s, 0, 1)
                    pre_square(s, 1)
                    turn(s, 2, 3)
                    hi_upto(p + RING - 1)

            def ffn(s):
                f, p = s["index"], s["piece"]

                def hidden_hi(src, dst):
                    nc.scalar.copy(dst[:, :, :], src).then_inc(ht_hi_made, 1)

                def chunk_(c, odd, more=0, more_landed=0, pieces=True, copy=False):
                    if copy:
                        act.wait_ge(piece_used, p + 4 + more)
                        nc.scalar.copy(gu_part, ps[:, GU_LOOP:GU_LOOP + 4, S:2 * S]).then_inc(gu_copied, 1)
                    act.wait_ge(gate_scaled, (NC - 1) * f + c)
                    nc.scalar.activation(sg[:, :, :], sg[:, :, :], ACT.Silu).then_inc(silu_made, 1)
                    if pieces:
                        hi(p + 6, more, more_landed)
                    act.wait_ge(hid_made, (NC + 1) * f + 2 + c)
                    hidden_hi(hid[:, :, :], ht_hi[odd])
                    if pieces:
                        hi(p + 7, more, more_landed)
                        hi(p + 8, more, more_landed)

                for t, used in enumerate(((gu_tile0, f + 1), (piece_used, p + 2))):
                    act.wait_ge(*used)
                    act.wait_ge(rstd_made, T * s["stat"] + t + 1)
                    nc.scalar.activation(sg[:, t, :], ps[:, GU_BANKS[0][t], 0:FC], ACT.Silu,
                                         scale=rstd[:, t:t + 1]).then_inc(silu_made, 1)
                hi(p + 3)
                hi(p + 4)
                act.wait_ge(r_row_turned, f + 1)
                nc.scalar.copy(r_row[:, :], ps[:, R_BANK, 0:S]).then_inc(r_row_made, 1)
                act.wait_ge(ht_turned, f + 1)
                hidden_hi(ps[:, HT_BANK, :].rearrange("p (k n) -> p k n", k=2), ht_hi[0])
                hi(p + 5)
                chunk_(1, 1)
                with act.Fori(2, NC - 1, 2) as c:
                    chunk_(c, 0, 3 * (c - 1), 32 * (c - 1), copy=True)
                    chunk_(c + 1, 1, 3 * c, 32 * c, copy=True)
                chunk_(NC - 1, 0, pieces=False)
                nc.scalar.preload_act_table_set(TABLES)
                end = p + 3 * NC
                hi_skip(end)
                hi_upto(end)

            def proj(s):
                m, form, what, b0 = s["mixer"], s["form"], s["what"], half_of(s)
                last = s["piece"] + s["n"] - 1
                if what == "a0":
                    act.wait_ge(conv_turned, 1)
                    nc.scalar.copy(conv_cols[:, :, :],
                                   ps[:, 7, 0:CB * (TAPS + 3)].rearrange("p (b n) -> p b n", b=CB))\
                        .then_inc(conv_ready, 1)
                if what in ("a0", "o0"):
                    nc.scalar.preload_act_table_set(SIGMOID_TABLES)
                if s["n"] == 2:
                    hi_upto(last + RING - 1)
                if s["n"]:
                    act.wait_ge(piece_used, last + 1)
                if form == "feature":
                    blocks = ps[:, b0:b0 + 4, 0:S]
                    if what[0] == "a":
                        at = 2 * int(what[1])
                        nc.scalar.copy(a_in[:, at:at + 2, :], ps[:, b0:b0 + 2, 0:S])
                        done = nc.scalar.activation(a_gate[:, at:at + 2, :], ps[:, b0 + 2:b0 + 4, 0:S],
                                                    ACT.Sigmoid)
                    elif what[0] == "k":
                        at = 4 * int(what[1])
                        done = nc.scalar.copy(kt[:, at:at + 4, :], blocks)
                    elif m == SWA:
                        for odd in range(2):
                            r = slice(64 * odd, 64 * odd + 64)
                            for kv in range(2):
                                first = 2 * odd + kv
                                done = nc.scalar.mul(qz[64 * kv:64 * kv + 64, first:first + 5:4, :],
                                                     ps[r, b0 + 2 * kv:b0 + 2 * kv + 2, 0:S], DH ** -0.5)
                    else:
                        at = 8 * int(what[1])
                        for odd in range(2):
                            r = slice(64 * odd, 64 * odd + 64)
                            done = nc.scalar.mul(qz[r, at + odd:at + 8:2, :], ps[r, b0:b0 + 4, 0:S], DH ** -0.5)
                elif form == "token":
                    at = 512 * int(what[1])
                    if what[0] == "v":
                        done = nc.scalar.copy(vt[:, :, at:at + 512], ps[:, b0:b0 + 2, :])
                    else:
                        done = nc.scalar.activation(o_gate[:, :, at:at + 512], ps[:, b0:b0 + 2, :], ACT.Sigmoid)
                elif form == "both":
                    nc.scalar.copy(kt[:, 0, :], ps[:, b0, 0:S])
                    done = nc.scalar.copy(vt[:, :, 0:P], ps[:, b0 + 2:b0 + 4, 0:P])
                elif form == "gates":
                    act.wait_ge(gates_made, GATES[m] + 1)
                    done = nc.scalar.copy(z[:, :, :], ps[:, b0:b0 + 2, 0:16])
                elif form == "sums":
                    act.wait_ge(gates_made, GATES[m] + 2)
                    done = nc.scalar.copy(c_rows[:, :], ps[:, b0, 0:S])
                done.then_inc(proj_read, 1)
                if what in ("a1", "o1"):
                    nc.scalar.preload_act_table_set(TABLES)
                if form == "gates":
                    act.wait_ge(lf_step, LF_STEPS * (m == MLSTM) + 2)
                    link(nc.scalar.activation(z_exp[:, :, :], z_neg[:, :, :], ACT.Exp))
                    linked()
                    link(nc.scalar.activation(z_ln[:, :, :], z_exp[:, :, :], ACT.Ln, bias=1.0))
                    n_z_ln.append(n_step)
                if steps[steps.index(s) + 1]["kind"] == "proj":
                    hi_upto(last + RING)

            def mix(s):
                m = s["mixer"]
                H = HEADS[m]
                for i in range(H + 3):
                    n = HEAD0[m] + i
                    if i < H:
                        bank = i % (2 if m == MLSTM else 4)
                        act.wait_ge(top_made, n + 1)
                        if m == MLSTM:
                            nc.scalar.activation(em[:, n, :], ntop[:, n, :], ACT.Exp)
                        if m == SWA:
                            nc.scalar.activation(em[:, n, :], ntop[:, n, :], ACT.Exp, bias=sinks[:, i:i + 1])
                        for q in range(T):
                            cols = slice(P * q, P * q + P * (q + 1))
                            sums = {} if m == MLSTM else dict(accum_out=mass[:, n, q:q + 1])
                            done = nc.scalar.activation(prob[i % 3][:, cols], ps[:, bank, cols], ACT.Exp,
                                                        bias=ntop[:, n, q:q + 1], **sums)
                        done.then_inc(prob_made, 1)
                    if m == SWA and 0 <= i - 1 < H:
                        act.wait_ge(rmass_made, n)
                        for q in range(T):
                            cols = slice(P * q, P * q + P * (q + 1))
                            pr = prob[(i - 1) % 3][:, cols]
                            done = nc.scalar.activation(pr, pr, ACT.Copy, scale=rmass[:, n - 1, q:q + 1])
                        done.then_inc(prob_normed, 1)
                    if 0 <= i - 2 < H:
                        act.wait_ge(prob_turned, n - 2 + 1)
                        nc.scalar.copy(prob_t[i % 2][:, :], ps[:, 4 + i % 2, 0:3 * P]).then_inc(prob_t_made, 1)
                    if i == {SWA: H + 2, MLSTM: H + 1}.get(m, H):
                        hi_upto(s["piece"] + RING - 1)
                    if i == (H + 2 if m == MLSTM else H + 1) and m != SWA:
                        hi_upto(s["piece"] + RING)
                    j = i - 3
                    if m == MLSTM and j >= 0:
                        head_squares(j, n - 3)
                    if m == MLSTM and i == H:
                        turn(s, 0, 1)
                    if m != MLSTM and j > 0 and j % 2:
                        act.wait_ge(o_made, n - 3 + 1)
                        nc.scalar.copy(xt_hi[:, O_BLOCK[m] + j // 2, :], ps[:, 6 + (j // 2) % 2, 0:S])\
                            .then_inc(o_hi_made, 1)
                if m == SWA:
                    hi_upto(s["piece"] + RING)
                    twos = [slice(2 * g, 2 * g + 2) for g in range(2)]
                    for g, two in enumerate(twos):
                        act.wait_ge(centered, g + 1)
                        nc.scalar.activation(a_sq[:, two, :], a_in[:, two, :], ACT.Square).then_inc(squared, 1)
                    act.wait_ge(var_made, 1)
                    link(nc.scalar.activation(a_gate[:, 0, :], ps[:, 5, 0:S], ACT.Ln, bias=epst[:, 0:1]))
                    linked()
                    nc.scalar.activation(a_gate[:, 1, :], a_gate[:, 0, :], ACT.Exp, scale=-0.5)\
                        .then_inc(conv_rstd, 1)
                    nc.scalar.preload_act_table_set(SILU_TABLES)
                    for g, two in enumerate(twos):
                        act.wait_ge(conv_normed, g + 1)
                        for b in (2 * g, 2 * g + 1):
                            link(nc.scalar.activation(a_sq[:, b, :], a_in[:, b, :], ACT.Silu,
                                                      bias=conv_cols[:, b, TAPS + 2:TAPS + 3],
                                                      scale=conv_cols[:, b, TAPS + 1:TAPS + 2]))
                        linked()
                        nc.scalar.copy(xt_hi[:, two, :], a_sq[:, two, :]).then_inc(conv_hi, 1)
                    nc.scalar.preload_act_table_set(TABLES)
                if m == MLSTM:
                    turn(s, 2, 3)

            def head_squares(j, n):
                act.wait_ge(hs_made, T * (j + 1))
                if j == 0:
                    linked()
                if j >= 4:
                    act.wait_ge(hs_sq, j - 3)
                for t in range(T):
                    part = 2 * (j % 4) + t
                    ins = nc.scalar.activation(junk[:, part * P:(part + 1) * P], ps[:, 6 + j % 2, t * P:(t + 1) * P],
                                               ACT.Square, scale=rmass[:, n, t:t + 1],
                                               accum_out=hs_ms[:, t, j:j + 1])
                ins.then_inc(hs_sq, 1)
                if j % 4 == 3:
                    act.wait_ge(hs_sq, j + 1)
                    four = slice(j - 3, j + 1)
                    link(nc.scalar.activation(hs_ms[:, :, four], hs_ms[:, :, four], ACT.Ln, bias=epst[:, 0:1],
                                              scale=1.0 / P))
                    linked()
                    nc.scalar.activation(hs_r[:, :, four], hs_ms[:, :, four], ACT.Exp, scale=-0.5)\
                        .then_inc(hs_rstd, 1)

            def out_(s):
                hi_upto(s["piece"] + 4)

            act.dma_start(x[:, 0, :], A["x"][0, 0:P, :]).then_inc(x_landed[0], 16)
            nc.scalar.preload_act_table_set(TABLES)
            act.wait_ge(consts_made, 4)
            hi_upto(0)
            for s in steps:
                k = s["kind"]
                if k in ("pre", "final"):
                    norms(s)
                elif k == "again":
                    turn(s, 0, 1, 2, 3)
                    hi_upto(s["piece"] + RING - 1)
                elif k == "ffn":
                    ffn(s)
                elif k == "proj":
                    proj(s)
                elif k == "mix":
                    mix(s)
                elif k == "out":
                    out_(s)

        @block.vector
        def _(dve):
            n_step = 0

            def link(ins):
                nonlocal n_step
                n_step += 1
                ins.then_inc(dve_step, 1)

            def linked():
                if n_step:
                    dve.wait_ge(dve_step, n_step)

            def lo(p, more=0):
                if p in pool_pieces:
                    return
                slot = p % RING
                dve.wait_ge(hi_made, p + 1 + more)
                nc.vector.tensor_tensor(w_lo[slot][:, :], raw[slot][:, :], w_hi[slot][:, :].bitcast(F32),
                                        ALU.subtract).then_inc(lo_made, 1)

            lo_upto, lo_skip = next_splits(lo)

            def use_gain(s):
                u = s["use"]
                dve.wait_ge(gain_landed[u % 2], 16 * (u // 2 + 1))
                return gain[u % 2]

            def post_half(s, t, half):
                y, xh = ps[:, 2 * t + half, :], half_cols(x, t, half)
                if s["g"] is None:
                    if t == 0:
                        dve.wait_ge(y_tile0, s["y"] + 1)
                    else:
                        dve.wait_ge(piece_used, s["piece"])
                    nc.vector.tensor_tensor(xh, y, xh, ALU.add).then_inc(x_added, 1)
                    return
                dve.wait_ge(prstd_made, T * s["at_normed"] + t + 1)
                g = use_gain(s)
                nc.vector.scalar_tensor_tensor(out=half_cols(xn, t, half), in0=y, scalar=prstd[:, t:t + 1],
                                               in1=g[:, half * 512:(half + 1) * 512],
                                               op0=ALU.mult, op1=ALU.mult).then_inc(normed_y, 1)
                dve.wait_ge(normed_y, 4 * s["at_normed"] + 2 * t + half + 1)
                nc.vector.tensor_tensor(xh, xh, half_cols(xn, t, half), ALU.add).then_inc(x_added, 1)

            def pre_half(s, t, half):
                g = use_gain(s)[:, half * 512:(half + 1) * 512]
                if s["kind"] != "again":
                    if s["post"]:
                        dve.wait_ge(x_added, 4 * s["post"]["at"] + 2 * t + half + 1)
                    else:
                        dve.wait_ge(x_landed[t], 16)
                if s.get("defer"):
                    ins = nc.vector.tensor_tensor(half_cols(xn, t, half), half_cols(x, t, half), g, ALU.mult)
                else:
                    dve.wait_ge(rstd_made, T * (s["stat"] + 1) - (T - 1 - t if s["kind"] != "again" else 0))
                    ins = nc.vector.scalar_tensor_tensor(
                        out=half_cols(xn, t, half), in0=half_cols(x, t, half), scalar=rstd[:, t:t + 1],
                        in1=g, op0=ALU.mult, op1=ALU.mult)
                ins.then_inc(xn_made, 1)

            def post_tile(s, t):
                for half in range(2):
                    post_half(s, t, half)

            def pre_tile(s, t):
                for half in range(2):
                    pre_half(s, t, half)

            def turn(s, *groups):
                for g in groups:
                    t, half, bank = group_place(s, g)
                    dve.wait_ge(xt_hi_made, 4 * s["turn"] + g + 1)
                    place = (slice(None), slice(4 * half, 4 * half + 4), slice(t * P, (t + 1) * P))
                    nc.vector.tensor_tensor(xt_lo[place], ps[:, bank, :].rearrange("p (k n) -> p k n", k=4),
                                            xt_hi[place].bitcast(F32), ALU.subtract).then_inc(xt_lo_made, 1)

            def norms(s):
                if s.get("loads") in (FOX, MLSTM):
                    dve.wait_ge(zw_split, 2 * (s["loads"] == MLSTM) + 1)
                    nc.vector.tensor_tensor(zw_lo[:, :, :], zw[:, :, :], zw_hi[:, :, :].bitcast(F32),
                                            ALU.subtract).then_inc(zw_split, 1)
                p, post = s["piece"], s["post"]
                if s["kind"] == "final":
                    for t in range(T):
                        post_tile(post, t)
                    for t in range(T):
                        pre_tile(s, t)
                    return

                def both(t, half):
                    if post:
                        post_half(post, t, half)
                    pre_half(s, t, half)

                if s["defer"]:
                    both(0, 0)
                    both(0, 1)
                    turn(s, 0)
                    lo_upto(p)
                    both(1, 0)
                    turn(s, 1)
                    both(1, 1)
                    lo_upto(p + 1)
                    turn(s, 2, 3)
                elif steps[steps.index(s) + 1]["mixer"] == SWA:
                    for t in range(T):
                        post_tile(post, t)
                    for t in range(T):
                        pre_tile(s, t)
                    turn(s, 0, 1, 2, 3)
                else:
                    for t in range(T):
                        post_tile(post, t)
                        pre_tile(s, t)
                        turn(s, 2 * t, 2 * t + 1)
                    again = steps[steps.index(s) + 5]
                    if again["kind"] == "again":
                        dve.wait_ge(turned, 4 * (s["turn"] + 1))
                        for t in range(T):
                            pre_tile(again, t)
                lo_upto(p + RING - 1)

            def ffn(s):
                f, p = s["index"], s["piece"]

                def hidden_lo(src, odd):
                    nc.vector.tensor_tensor(ht_lo[odd][:, :, :], src, ht_hi[odd][:, :, :].bitcast(F32),
                                            ALU.subtract).then_inc(ht_lo_made, 1)

                r_wide = r_row[:, :].rearrange("p (k n) -> p k n", k=1).to_broadcast([P, 2, S])

                def chunk_(c, odd, more=0, pieces=True, banks=None):
                    wide = lambda bank: ps[:, bank, :].rearrange("p (k n) -> p k n", k=2)
                    used = p + 4 + more if pieces else p + 3 * NC - 2
                    dve.wait_ge(piece_used, used)
                    if banks:
                        nc.vector.tensor_tensor(sg[:, :, :], wide(banks[0]), r_wide, ALU.mult)\
                            .then_inc(gate_scaled, 1)
                        dve.wait_ge(ht_lo_made, NC * f + c)
                        nc.vector.tensor_tensor(hid[:, :, :], wide(banks[1]), r_wide, ALU.mult)\
                            .then_inc(up_scaled, 1)
                    else:
                        summed = 2 * (NC - 3) * f + 2 * (c - 2)
                        dve.wait_ge(gu_copied, (NC - 3) * f + c - 1)
                        for n, dst in enumerate((sg, hid)):
                            if n == 1:
                                dve.wait_ge(ht_lo_made, NC * f + c)
                            two = slice(GU_LOOP + 2 * n, GU_LOOP + 2 * n + 2)
                            nc.vector.tensor_tensor(dst[:, :, :], ps[:, two, 0:S], gu_part[:, 2 * n:2 * n + 2, :],
                                                    ALU.add).then_inc(gu_summed, 1)
                        for n, (dst, scaled) in enumerate(((sg, gate_scaled), (hid, up_scaled))):
                            dve.wait_ge(gu_summed, summed + n + 1)
                            nc.vector.tensor_tensor(dst[:, :, :], dst[:, :, :], r_wide, ALU.mult)\
                                .then_inc(scaled, 1)
                    if pieces:
                        lo(p + 6, more)
                    dve.wait_ge(silu_made, (NC + 1) * f + 2 + c)
                    dve.wait_ge(up_scaled, (NC - 1) * f + c)
                    nc.vector.tensor_tensor(hid[:, :, :], hid[:, :, :], sg[:, :, :], ALU.mult).then_inc(hid_made, 1)
                    if pieces:
                        lo(p + 7, more)
                    dve.wait_ge(ht_hi_made, NC * f + c + 1)
                    hidden_lo(hid[:, :, :], odd)
                    if pieces:
                        lo(p + 8, more)

                for t in range(T):
                    dve.wait_ge(silu_made, (NC + 1) * f + t + 1)
                    nc.vector.scalar_tensor_tensor(out=hid[:, t, :], in0=ps[:, GU_BANKS[0][t], FC:2 * FC],
                                                   scalar=rstd[:, t:t + 1], in1=sg[:, t, :],
                                                   op0=ALU.mult, op1=ALU.mult).then_inc(hid_made, 1)
                for t in range(T):
                    ins = nc.vector.tensor_scalar(r_diag[:, t, :], ident[:, :], rstd[:, t:t + 1], None, ALU.mult)
                ins.then_inc(r_diag_made, 1)
                lo(p + 3)
                lo(p + 4)
                dve.wait_ge(ht_hi_made, NC * f + 1)
                hidden_lo(ps[:, HT_BANK, :].rearrange("p (k n) -> p k n", k=2), 0)
                lo(p + 5)
                dve.wait_ge(r_row_made, f + 1)
                chunk_(1, 1, banks=GU_BANKS[1])
                with dve.Fori(2, NC - 1, 2) as c:
                    chunk_(c, 0, 3 * (c - 1))
                    chunk_(c + 1, 1, 3 * c)
                chunk_(NC - 1, 0, pieces=False, banks=GU_LAST)
                end = p + 3 * NC
                lo_skip(end)
                lo_upto(end)

            def taps(group, first, last):
                n0, b0 = 2 * TAPS * group, 2 * group
                for j in range(first, last):
                    for b in range(b0, b0 + 2):
                        if j == 0:
                            ins = nc.vector.tensor_scalar(acc[:, b, :], a_pad[:, b, 0:S], conv_cols[:, b, 0:1],
                                                          conv_cols[:, b, TAPS:TAPS + 1], ALU.mult, ALU.add)
                        else:
                            dve.wait_ge(conv_made, n0 + 2 * j + (b - b0) - 1)
                            ins = nc.vector.scalar_tensor_tensor(
                                out=acc[:, b, :], in0=a_pad[:, b, j:j + S], scalar=conv_cols[:, b, j:j + 1],
                                in1=acc[:, b, :], op0=ALU.mult, op1=ALU.add)
                        ins.then_inc(conv_made, 1)

            def proj(s):
                m, form, what = s["mixer"], s["form"], s["what"]
                last = s["piece"] + s["n"] - 1
                lo_upto(last + RING - (steps[steps.index(s) + 1]["kind"] != "proj"))
                if what[0] == "a":
                    group = int(what[1])
                    dve.wait_ge(proj_read, s["chunk"] + 1)
                    two = slice(2 * group, 2 * group + 2)
                    nc.vector.tensor_tensor(a_pad[:, two, TAPS - 1:], a_in[:, two, :], a_gate[:, two, :],
                                            ALU.mult).then_inc(a_made, 1)
                    dve.wait_ge(a_made, group + 1)
                    dve.wait_ge(conv_ready, 1)
                    if group == 0:
                        taps(0, 0, 14)
                    else:
                        taps(0, 14, TAPS)
                if what == "kv":
                    taps(1, 0, TAPS_AT[0])
                if form == "gates":
                    base = LF_STEPS * (m == MLSTM)
                    dve.wait_ge(proj_read, s["chunk"] + 1)
                    dve.wait_ge(zw_landed, 32 * (1 + (m == MLSTM)))
                    for t in range(T):
                        ins = nc.vector.tensor_tensor(z[:, t, :], z[:, t, :], z_bias[:, :], ALU.add)
                    ins.then_inc(lf_step, 1)
                    dve.wait_ge(lf_step, base + 1)
                    nc.vector.scalar_tensor_tensor(out=z_neg[:, :, :], in0=z[:, :, :], scalar=-1.0, in1=z[:, :, :],
                                                   op0=ALU.mult, op1=ALU.min).then_inc(lf_step, 1)
                    if m == MLSTM:
                        nc.vector.memset(lf[:, :, 0:32], 0.0).then_inc(lf_step, 1)
                        for group in range(3):
                            ins = nc.vector.tensor_copy(ig[:, :, 32 * group:32 * group + 8], z[:, :, 0:8])
                        ins.then_inc(lf_step, 1)
                    n_f, f0 = (16, 0) if m == FOX else (8, 8)
                    dve.wait_ge(act_step, n_z_ln[m == MLSTM])
                    if m == MLSTM:
                        dve.wait_ge(lf_step, base + 4)
                    nc.vector.scalar_tensor_tensor(out=lf[:, :, 16:16 + n_f], in0=z[:, :, f0:16], scalar=0.0,
                                                   in1=z_ln[:, :, f0:16], op0=ALU.min, op1=ALU.subtract)\
                        .then_inc(lf_step, 1)
                    dve.wait_ge(lf_step, base + 3 + 2 * (m == MLSTM))
                    nc.vector.tensor_scalar(lf[:, :, 0:n_f], lf[:, :, 16:16 + n_f], -1.0, None, ALU.mult)\
                        .then_inc(lf_step, 1)
                    dve.wait_ge(lf_step, base + 4 + 2 * (m == MLSTM))
                    nc.vector.tensor_copy(lf[:, :, 32:64], lf[:, :, 0:32])
                    nc.vector.tensor_copy(lf[:, :, 64:96], lf[:, :, 0:32]).then_inc(lf_made, 1)
                if form == "sums":
                    dve.wait_ge(proj_read, s["chunk"] + 1)
                    link(nc.vector.tensor_copy(c_parts[:, :], c_rows[:, :]))
                    linked()
                    link(nc.vector.tensor_tensor(c_rows[:, :], c_rows[:, :], c_parts[:, :], ALU.subtract))
                    linked()
                    link(nc.vector.tensor_copy(c_part[:, :], c_rows[:, :]))
                    linked()
                    link(nc.vector.tensor_tensor(c_rows[:, :], c_rows[:, :], c_part[:, :], ALU.subtract))
                    linked()
                    link(nc.vector.tensor_copy(c_parts[32:64, :], c_part[32:64, :]))
                    link(nc.vector.tensor_copy(c_parts[64:96, :], c_rows[64:96, :]))
                    linked()
                    link(nc.vector.tensor_scalar(aug_q[:, :], c_parts[:, :], row_b[:, 0:1], row_a[:, 0:1],
                                                 ALU.mult, ALU.add))
                    nc.vector.tensor_scalar(aug_k[:, :], c_parts[:, :], row_a[:, 0:1], row_b[:, 0:1],
                                            ALU.mult, ALU.add)
                    linked()
                    for i in range(2):
                        head_bias(m, i)
                if what in ("o0", "o1"):
                    dve.wait_ge(proj_read, s["chunk"] + 1)
                    at = 512 * int(what[1])
                    part = o_gate[:, :, at:at + 512]
                    dve.wait_ge(og_landed, 16)
                    for t in range(T):
                        link(nc.vector.tensor_tensor(part[:, t, :], part[:, t, :], og_gain[:, at:at + 512],
                                                     ALU.mult))

            def head_bias(m, i):
                nc.vector.tensor_scalar(aug_h[i % 2][:, :], aug_q[:, :], head_rows[:, i:i + 1], None,
                                        ALU.mult).then_inc(aug_made, 1)

            def mix(s):
                m = s["mixer"]
                H = HEADS[m]
                for i in range(H + 3):
                    n = HEAD0[m] + i
                    if i < H:
                        bank = i % (2 if m == MLSTM else 4)
                        dve.wait_ge(scores_made, n + 1)
                        nc.vector.reduce_max(top[:, n, 0:1], ps[:, bank, 0:P], AX_X)
                        link(nc.vector.reduce_max(top[:, n, 1:2], ps[:, bank, P:3 * P], AX_X))
                        linked()
                        if m == SWA:
                            ins = nc.vector.tensor_scalar(ntop[:, n, :], top[:, n, :], sinks[:, i:i + 1], -1.0,
                                                          ALU.max, ALU.mult)
                        else:
                            ins = nc.vector.tensor_scalar(ntop[:, n, :], top[:, n, :], -1.0, None, ALU.mult)
                        ins.then_inc(top_made, 1)
                        if m in (FOX, MLSTM) and i + 2 < H:
                            head_bias(m, i + 2)
                    if 0 <= i - 1 < H:
                        normalise(m, i - 1, n - 1)
                    if m == SWA:
                        taps(1, sum(TAPS_AT[:i + 1]), sum(TAPS_AT[:i + 2]))
                    if i == {SWA: H + 2, MLSTM: H + 1}.get(m, H):
                        lo_upto(s["piece"] + RING - 1)
                    if i == (H + 2 if m == MLSTM else H + 1) and m != SWA:
                        lo_upto(s["piece"] + RING)
                    j = i - 3
                    if m == MLSTM and j >= 0:
                        dve.wait_ge(o_made, n - 3 + 1)
                        for t in range(T):
                            nc.vector.scalar_tensor_tensor(
                                out=xn[:, t, j * P:(j + 1) * P], in0=ps[:, 6 + j % 2, t * P:(t + 1) * P],
                                scalar=rmass[:, n - 3, t:t + 1], in1=o_gate[:, t, j * P:(j + 1) * P],
                                op0=ALU.mult, op1=ALU.mult).then_inc(hs_made, 1)
                        if j == 4:
                            gated(0)
                        if i == H:
                            turn(s, 0, 1)
                    elif m != MLSTM and j > 0 and j % 2:
                        dve.wait_ge(o_hi_made, O_PAIR0[m] + j // 2 + 1)
                        kb = O_BLOCK[m] + j // 2
                        nc.vector.tensor_tensor(xt_lo[:, kb, :], ps[:, 6 + (j // 2) % 2, 0:S],
                                                xt_hi[:, kb, :].bitcast(F32), ALU.subtract).then_inc(o_lo_made, 1)
                if m == SWA:
                    conv_end()
                if m == MLSTM:
                    gated(1)
                    turn(s, 2, 3)

            def gated(half):
                dve.wait_ge(hs_made, T * 4 * (half + 1))
                dve.wait_ge(hs_rstd, half + 1)
                for t in range(T):
                    by_head = half_cols(xn, t, half).rearrange("p (h n) -> p h n", h=4)
                    r = hs_r[:, t, 4 * half:4 * half + 4].unsqueeze(2).to_broadcast([P, 4, P])
                    nc.vector.tensor_tensor(by_head, by_head, r, ALU.mult).then_inc(hs_gated, 1)

            def normalise(m, i, n):
                dve.wait_ge(prob_made, n + 1)
                pr = prob[i % 3]
                if m == MLSTM:
                    for q in range(T):
                        cols = slice(P * q, P * q + P * (q + 1))
                        ins = nc.vector.scalar_tensor_tensor(out=pr[:, cols], in0=ps[:, 2 + i % 2, cols],
                                                             scalar=1.0, in1=pr[:, cols], op0=ALU.mult,
                                                             op1=ALU.mult, accum_out=mass[:, n, q:q + 1])
                    ins.then_inc(prob_normed, 1)
                    dve.wait_ge(prob_normed, n + 1)
                    link(nc.vector.scalar_tensor_tensor(out=mass2[:, n, :], in0=mass[:, n, :], scalar=-1.0,
                                                        in1=mass[:, n, :], op0=ALU.mult, op1=ALU.max))
                    linked()
                    link(nc.vector.tensor_tensor(top[:, n, :], mass2[:, n, :], em[:, n, :], ALU.max))
                    linked()
                    link(nc.vector.reciprocal(rmass[:, n, :], top[:, n, :]))
                    return
                total = mass
                if m == SWA:
                    link(nc.vector.tensor_tensor(mass2[:, n, :], mass[:, n, :], em[:, n, :], ALU.add))
                    linked()
                    total = mass2
                ins = nc.vector.reciprocal(rmass[:, n, :], total[:, n, :])
                if m == SWA:
                    ins.then_inc(rmass_made, 1)
                    return
                link(ins)
                linked()
                for q in range(T):
                    cols = slice(P * q, P * q + P * (q + 1))
                    ins = nc.vector.tensor_scalar(pr[:, cols], pr[:, cols], rmass[:, n, q:q + 1], None, ALU.mult)
                ins.then_inc(prob_normed, 1)

            def conv_end():
                taps(1, sum(TAPS_AT), TAPS)
                dve.wait_ge(mean_made, 1)
                twos = [slice(2 * g, 2 * g + 2) for g in range(2)]
                for two in twos:
                    nc.vector.tensor_tensor(a_in[:, two, :], acc[:, two, :],
                                            ps[:, 4:5, 0:S].to_broadcast([P, 2, S]), ALU.subtract)\
                        .then_inc(centered, 1)
                dve.wait_ge(conv_rstd, 1)
                for g, two in enumerate(twos):
                    dve.wait_ge(centered, g + 1)
                    nc.vector.tensor_tensor(a_in[:, two, :], a_in[:, two, :],
                                            a_gate[:, 1:2, :].to_broadcast([P, 2, S]), ALU.mult)\
                        .then_inc(conv_normed, 1)
                for g, two in enumerate(twos):
                    dve.wait_ge(conv_hi, g + 1)
                    nc.vector.tensor_tensor(xt_lo[:, two, :], a_sq[:, two, :], xt_hi[:, two, :].bitcast(F32),
                                            ALU.subtract).then_inc(conv_lo, 1)

            for s in steps:
                k = s["kind"]
                if k in ("pre", "final"):
                    if k == "pre" and s["stat"] == 1:
                        dve.wait_ge(consts_made, N_CONST)
                    norms(s)
                elif k == "again":
                    turn(s, 0, 1, 2, 3)
                    lo_upto(s["piece"] + RING - 1)
                elif k == "ffn":
                    ffn(s)
                elif k == "proj":
                    proj(s)
                elif k == "mix":
                    mix(s)
                elif k == "out":
                    lo_upto(s["piece"] + 4)

        @block.tensor
        def _(pe):
            def three(o, xh, xl, wh, wl, start, stop, stands="x"):
                for n, (a, b) in enumerate(((xh, wh), (xl, wh), (xh, wl))):
                    if stands == "w":
                        a, b = b, a
                    ins = nc.tensor.matmul(o, a, b, start=start and n == 0, stop=stop and n == 2)
                return ins

            def split(p, more=0):
                made, count = lo_count(p)
                pe.wait_ge(made, count + more)

            def x_blocks(kb, t):
                place = (slice(None), kb, slice(t * P, (t + 1) * P))
                return xt_hi[place], xt_lo[place]

            def turn(s, *groups):
                for g in groups:
                    t, half, bank = group_place(s, g)
                    if s["kind"] == "mix":
                        pe.wait_ge(hs_gated, g + 1)
                    else:
                        pe.wait_ge(xn_made, 4 * s["at"] + g + 1)
                    for k in range(4):
                        c0 = (4 * half + k) * P
                        ins = nc.tensor.transpose(ps[:, bank, k * P:(k + 1) * P], xn[:, t, c0:c0 + P],
                                                  ident[:, :])
                    ins.then_inc(turned, 1)

            def half_product(o, p, half, t, ends=(0, KB - 1)):
                w = [v[p % RING] for v in (w_hi, w_lo)]
                for k in range(4):
                    kb = 4 * half + k
                    cols = slice(512 * k, 512 * (k + 1))
                    ins = three(o, *x_blocks(kb, t), w[0][:, cols], w[1][:, cols], kb == ends[0], kb == ends[1])
                return ins

            def first_product(s, banks, tile0):
                p, pre = s["piece"], steps[steps.index(s) - 1]
                turn_at = 4 * s["after_turn"]
                for g in range(4):
                    t, half = g // 2, g % 2
                    pe.wait_ge(xt_lo_made, turn_at + g + 1)
                    if t == 0:
                        split(p + half)
                    ins = half_product(ps[:, banks[t], :], p + half, half, t)
                    if t == 1:
                        ins.then_inc(piece_used, 1)
                    elif half == 1 and tile0:
                        ins.then_inc(gu_tile0, 1)
                    if t == 0:
                        turn(pre, 2 + half)

            def ffn(s):
                f, p = s["index"], s["piece"]

                def gate_up(q, more=0, banks=None, between=lambda: None):
                    for half in range(2):
                        slot = (q + half) % RING
                        split(q + half, more)
                        for k in range(4):
                            kb = 4 * half + k
                            for b in range(4):
                                cols = slice(512 * k + b * P, 512 * k + (b + 1) * P)
                                if banks:
                                    o = ps[:, banks[b // 2], (b % 2) * S:(b % 2 + 1) * S]
                                    ins = three(o, xt_hi[:, kb, :], xt_lo[:, kb, :], w_hi[slot][:, cols],
                                                w_lo[slot][:, cols], (kb, b % 2) == (0, 0),
                                                (kb, b % 2) == (KB - 1, 1), stands="w")
                                else:
                                    nc.tensor.matmul(ps[:, GU_LOOP + b, :], w_hi[slot][:, cols], xt[:, kb, :],
                                                     start=kb == 0, stop=False)
                                    ins = nc.tensor.matmul(ps[:, GU_LOOP + b, 0:S], w_lo[slot][:, cols],
                                                           xt_hi[:, kb, :], start=False, stop=kb == KB - 1)
                        ins.then_inc(piece_used, 1)
                        if half == 0:
                            between()

                def down_block(q, k, t, odd, start=False, stop=False):
                    for n in range(2):
                        cols = slice(k * D + n * 512, k * D + (n + 1) * 512)
                        h = (slice(None), k, slice(t * P, (t + 1) * P))
                        ins = three(ps[:, 2 * t + n, :], ht_hi[odd][h], ht_lo[odd][h], w_hi[q % RING][:, cols],
                                    w_lo[q % RING][:, cols], start and k == 0, stop and k == 1)
                    return ins

                def down(chunk, q, odd, more=0, start=False):
                    pe.wait_ge(ht_lo_made, f * NC + chunk + 1)
                    split(q, more)
                    for k in range(2):
                        for t in range(T):
                            ins = down_block(q, k, t, odd, start)
                    ins.then_inc(piece_used, 1)

                def step(c, q, odd, more=0):
                    pe.wait_ge(up_scaled, (NC - 1) * f + c - 1)
                    gate_up(q, more)
                    down(c - 1, q + 2, 1 - odd, more)

                def rows_between():
                    pe.wait_ge(hid_made, (NC + 1) * f + T)
                    for k in range(2):
                        for t in range(T):
                            ins = nc.tensor.transpose(ps[:, HT_BANK, k * S + t * P:k * S + (t + 1) * P],
                                                      hid[:, t, k * P:(k + 1) * P], ident[:, :])
                    ins.then_inc(ht_turned, 1)
                    pe.wait_ge(r_diag_made, f + 1)
                    for t in range(T):
                        ins = nc.tensor.matmul(ps[:, R_BANK, t * P:(t + 1) * P], ones[:, :], r_diag[:, t, :],
                                               start=True, stop=True)
                    ins.then_inc(r_row_turned, 1)

                if f == 0:
                    pe.wait_ge(consts_made, N_ONES)
                first_product(s, GU_BANKS[0], True)
                gate_up(p + 2, banks=GU_BANKS[1], between=rows_between)
                pe.wait_ge(r_row_made, f + 1)
                down(0, p + 4, 0, start=True)
                with pe.Fori(2, NC - 1, 2) as c:
                    step(c, p + 5, 0, 3 * (c - 2))
                    step(c + 1, p + 5, 1, 3 * (c - 1))

                q = p + 3 * NC - 2
                pe.wait_ge(up_scaled, (NC - 1) * f + NC - 2)
                gate_up(q - 2, banks=GU_LAST)
                pe.wait_ge(ht_lo_made, f * NC + NC - 1)
                split(q)
                down_block(q, 0, 0, 1)
                down_block(q, 1, 0, 1)
                down_block(q, 0, 1, 1)
                pe.wait_ge(ht_lo_made, f * NC + NC)
                split(q + 1)
                down_block(q + 1, 0, 0, 0)
                down_block(q + 1, 1, 0, 0, stop=True).then_inc(y_tile0, 1)
                down_block(q, 1, 1, 1).then_inc(piece_used, 1)
                down_block(q + 1, 0, 1, 0)
                down_block(q + 1, 1, 1, 0, stop=True).then_inc(piece_used, 1)

            def proj(s):
                m, form, what, b0, p = s["mixer"], s["form"], s["what"], half_of(s), s["piece"]
                if s["chunk"] >= 2:
                    pe.wait_ge(proj_read, s["chunk"] - 1)
                if what == "v0":
                    first_product(s, (b0, b0 + 1), False)
                    return
                pe.wait_ge(xt_lo_made, 4 * (s["after_turn"] + 1))
                if what == "a0":
                    pe.wait_ge(small_landed, 16 * 5)
                    for b in range(CB):
                        ins = nc.tensor.transpose(ps[:, 7, b * (TAPS + 3):(b + 1) * (TAPS + 3)],
                                                  conv_rows[:, b * P:(b + 1) * P], ident[0:TAPS + 3, 0:TAPS + 3])
                    ins.then_inc(conv_turned, 1)
                if what == "a1":
                    pe.wait_ge(conv_ready, 1)
                if form == "gates":
                    pe.wait_ge(zw_split, 2 * (1 + (m == MLSTM)))
                    for t in range(T):
                        for kb in range(KB):
                            ins = three(ps[:, b0 + t, 0:16], *x_blocks(kb, t), zw_hi[:, kb, :], zw_lo[:, kb, :],
                                        kb == 0, kb == KB - 1)
                    ins.then_inc(gates_made, 1)
                elif form == "sums":
                    pe.wait_ge(lf_made, 1 + (m == MLSTM))
                    last = m != MLSTM
                    for t in range(T):
                        o = ps[:, b0, t * P:(t + 1) * P]
                        nc.tensor.matmul(o, lf[:, t, :], upper[:, :], start=True, stop=last and t == 0)
                        if t == 1:
                            nc.tensor.matmul(o, lf[:, 0, :], ones[:, :], start=False, stop=last)
                        if m == MLSTM:
                            nc.tensor.matmul(o, ig[:, t, :], ident[:, :], start=False, stop=True)
                    nc.tensor.matmul(ps[:, b0 + 1, 0:P], lf[:, 0, :], ones[:, :], start=True, stop=True)\
                        .then_inc(gates_made, 1)
                elif form == "both":
                    split(p)
                    slot = p % RING
                    wh, wl = (w[slot][:, :].rearrange("p (k n) -> p k n", k=KB) for w in (w_hi, w_lo))
                    for kb in range(KB):
                        ends = (kb == 0, kb == KB - 1)
                        three(ps[:, b0, 0:S], xt_hi[:, kb, :], xt_lo[:, kb, :], wh[:, kb, 0:P], wl[:, kb, 0:P],
                              *ends, stands="w")
                        for t in range(T):
                            ins = three(ps[:, b0 + 2 + t, 0:P], *x_blocks(kb, t), wh[:, kb, P:2 * P],
                                        wl[:, kb, P:2 * P], *ends)
                    ins.then_inc(piece_used, 1)
                else:
                    for half in range(2):
                        slot = (p + half) % RING
                        split(p + half)
                        for k in range(4):
                            kb = 4 * half + k
                            ends = (kb == 0, kb == KB - 1)
                            cols = slice(512 * k, 512 * (k + 1))
                            wh, wl = w_hi[slot][:, cols], w_lo[slot][:, cols]
                            if form == "token":
                                for t in range(T):
                                    ins = three(ps[:, b0 + t, :], *x_blocks(kb, t), wh, wl, *ends)
                            else:
                                for b in range(4):
                                    bs = slice(b * P, (b + 1) * P)
                                    ins = three(ps[:, b0 + b, 0:S], xt_hi[:, kb, :], xt_lo[:, kb, :],
                                                wh[:, bs], wl[:, bs], *ends, stands="w")
                        ins.then_inc(piece_used, 1)

            def scores(m, i, n):
                H = HEADS[m]
                bank = i % (2 if m == MLSTM else 4)
                qk_bank = 2 + i % 2 if m == MLSTM else bank
                slot = i if m != SWA else 2 * (i % 4) + i // 4
                kb = {SWA: 0}.get(m, i // 2)
                if m == MLSTM and i >= 2:
                    pe.wait_ge(prob_normed, n - 1)
                elif i >= 4:
                    pe.wait_ge(prob_made, n - 3)
                if m in (FOX, MLSTM):
                    pe.wait_ge(aug_made, HEAD0_AUG[m] + i + 1)
                mm = nc.tensor.matmul
                for q in range(T):
                    qs = slice(q * P, (q + 1) * P)
                    o = ps[:, bank, P * q:P * q + P * (q + 1)]
                    diagonal = ps[:, bank, 2 * P * q:2 * P * q + P]
                    if m == MLSTM:
                        mm(ps[:, qk_bank, P * q:P * q + P * (q + 1)], qz[:, slot, qs], kt[:, kb, 0:P * (q + 1)],
                           start=True, stop=True)
                        mm(o, aug_h[i % 2][:, qs], aug_k[:, 0:P * (q + 1)], start=True, stop=False)
                        ins = mm(diagonal, ident_b[:, :], causal_b[:, :], start=False, stop=True)
                        continue
                    mm(o, qz[:, slot, qs], kt[:, kb, 0:P * (q + 1)], start=True, stop=False)
                    if m == SWA:
                        ins = mm(o, ident_b[:, :], alibi_b[:, i, P * (1 - q):S], start=False, stop=True)
                    elif m == FOX:
                        mm(o, aug_h[i % 2][:, qs], aug_k[:, 0:P * (q + 1)], start=False, stop=False)
                        ins = mm(diagonal, ident_b[:, :], causal_b[:, :], start=False, stop=True)
                    else:
                        mm(diagonal, mx[:, i, 0:P], flip[:, :], start=False, stop=False)
                        if q == 1:
                            mm(ps[:, bank, P:2 * P], mx[:, i, P:S], flip[:, :], start=False, stop=False)
                        ins = mm(diagonal, ident_b[:, :], chunk_b[:, :], start=False, stop=True)
                ins.then_inc(scores_made, 1)

            def mix(s):
                m = s["mixer"]
                H = HEADS[m]
                pe.wait_ge(proj_read, chunks_before(s) - (m != SWA))
                if m == REL:
                    pe.wait_ge(rel_landed, 16)
                for i in range(H + 3):
                    n = HEAD0[m] + i
                    if i < H:
                        scores(m, i, n)
                    j = i - 3
                    if j >= 0:
                        pe.wait_ge(prob_t_made, n - 3 + 1)
                        seg = lambda g: prob_t[j % 2][:, g * P:(g + 1) * P]
                        if m == MLSTM:
                            if j >= 2:
                                pe.wait_ge(hs_sq, j - 1)
                            v = lambda kt_: vt[:, kt_, j * P:(j + 1) * P]
                            bank = ps[:, 6 + j % 2, :]
                            nc.tensor.matmul(bank[:, 0:P], seg(0), v(0), start=True, stop=True)
                            nc.tensor.matmul(bank[:, P:S], seg(1), v(0), start=True, stop=False)
                            ins = nc.tensor.matmul(bank[:, P:S], seg(2), v(1), start=False, stop=True)
                        else:
                            if j >= 4 and j % 2 == 0:
                                pe.wait_ge(o_lo_made, O_PAIR0[m] + j // 2 - 1)
                            c0 = (j // 4 if m == SWA else j) * DH
                            r = slice(64 * (j % 2), 64 * (j % 2) + 64)
                            v = lambda kt_: vt[:, kt_, c0:c0 + DH]
                            bank = ps[r, 6 + (j // 2) % 2, :]
                            nc.tensor.matmul(bank[:, 0:P], v(0), seg(0), start=True, stop=True)
                            nc.tensor.matmul(bank[:, P:S], v(0), seg(1), start=True, stop=False)
                            ins = nc.tensor.matmul(bank[:, P:S], v(1), seg(2), start=False, stop=True)
                        ins.then_inc(o_made, 1)
                    if 0 <= i - 2 < H:
                        k = i - 2
                        if k == 0:
                            pe.wait_ge(proj_read, chunks_before(s))
                        pe.wait_ge(prob_normed, n - 2 + 1)
                        if k >= 2:
                            pe.wait_ge(prob_t_made, n - 2 - 1)
                        for g in range(3):
                            ins = nc.tensor.transpose(ps[:, 4 + k % 2, g * P:(g + 1) * P],
                                                      prob[k % 3][:, g * P:(g + 1) * P], ident[:, :])
                        ins.then_inc(prob_turned, 1)
                    if m == MLSTM and i == H:
                        pe.wait_ge(prob_made, HEAD0[m] + H)
                        turn(s, 0, 1)
                    if m == MLSTM and i > H:
                        pe.wait_ge(xt_lo_made, 4 * s["turn"] + 2)
                        out_piece(s["out"], i - H - 1)
                    if m in (FOX, REL) and i in (H, H + 1):
                        pe.wait_ge(prob_made, HEAD0[m] + i - 1)
                        pe.wait_ge(o_lo_made, O_PAIR0[m] + 4)
                        out_piece(s["out"], i - H)
                if m == SWA:
                    pe.wait_ge(o_lo_made, O_PAIR0[m] + HEADS[m] // 2)
                    out_piece(s["out"], 0)
                    for t, (made, bank, src) in enumerate(((mean_made, 4, acc), (var_made, 5, a_sq))):
                        for b in range(CB):
                            if t == 0:
                                pe.wait_ge(conv_made, 2 * TAPS * (b // 2 + 1))
                            else:
                                pe.wait_ge(squared, b // 2 + 1)
                            ins = nc.tensor.matmul(ps[:, bank, 0:S], mean_w[:, :], src[:, b, :], start=b == 0,
                                                   stop=b == CB - 1)
                        ins.then_inc(made, 1)
                        out_piece(s["out"], 1, [t])
                if m == MLSTM:
                    turn(s, 2, 3)

            def out_piece(s, n, tiles=range(T)):
                q, half = s["piece"] + n, out_half(s, n)
                split(q)
                for t in tiles:
                    ins = half_product(ps[:, 2 * t + n, :], q, half, t, (4 * half, None))
                if t == T - 1:
                    ins.then_inc(piece_used, 1)

            def out_(s):
                m = s["mixer"]
                if m == MLSTM:
                    pe.wait_ge(xt_lo_made, 4 * (s["after_turn"] + 1))
                elif m == SWA:
                    pe.wait_ge(conv_lo, 2)
                else:
                    pe.wait_ge(o_lo_made, O_PAIR0[m] + HEADS[m] // 2)
                q, half = s["piece"] + 2, out_half(s, 2)
                for t, n in ((0, 0), (0, 1), (1, 0), (1, 1)):
                    if t == 0:
                        split(q + n)
                    ins = half_product(ps[:, 2 * t + n, :], q + n, half, t, (None, 4 * half + 3))
                    if t == 1:
                        ins.then_inc(piece_used, 1)
                    elif n == 1:
                        ins.then_inc(y_tile0, 1)

            pe.wait_ge(consts_made, 2)
            for s in steps:
                k = s["kind"]
                if k == "pre":
                    turn(s, 0, 1)
                    if steps[steps.index(s) + 1].get("mixer") == SWA:
                        turn(s, 2, 3)
                elif k == "again":
                    pe.wait_ge(proj_read, chunks_before(s) - 1)
                    turn(s, 0, 1, 2, 3)
                elif k == "ffn":
                    ffn(s)
                elif k == "proj":
                    proj(s)
                elif k == "mix":
                    pe.wait_ge(consts_made, N_CONST)
                    mix(s)
                elif k == "out":
                    out_(s)


_INS = ["x", "norm_g", "ffn_w_gate", "ffn_w_up", "ffn_w_down", "ab_w_in", "conv_w", "conv_b",
        "conv_ln_g", "conv_ln_b", "swa_sinks", "ab_w_out", "fox_w_in", "fox_b_f", "fox_w_out",
        "a_w_in_2", "a_b_gate_2", "a_g_head_2", "a_w_out_2", "b_w_q_2", "b_rel_bias_2", "b_w_o_2",
        "kv_norm_g_2", "w_kv_2", "norm_mix_g_2", "norm_ffn_g_2", "ffn_w_gate_2", "ffn_w_up_2",
        "ffn_w_down_2", "final_norm_g_2"]


def kernel(**inputs):
    import numpy as _np
    import concourse.bacc as _bacc
    from concourse.bass_utils import run_bass_kernel_spmd as _run

    nc = _bacc.Bacc("TRN2", target_bir_lowering=False, num_devices=1)
    arrays, args = {}, {}
    for name in _INS:
        a = _np.ascontiguousarray(inputs[name])
        arrays[f"in_{name}_dram"] = a
        args[name] = nc.dram_tensor(f"in_{name}_dram", a.shape, mybir.dt.from_np(a.dtype),
                                    kind="ExternalInput").ap()
    out = nc.dram_tensor("out_0_dram", (1, S, D), F32, kind="ExternalOutput").ap()
    program(nc, args, out)
    r = _run(nc, [arrays], core_ids=[0])
    return r.results[0]["out_0_dram"]
```
